# Optimizing a Trainium2 kernel written in Bass

```python
import math
import jax
import jax.numpy as jnp
from jax import lax
import numpy as np

D_MODEL = 1024
BATCH = 1
SEQ = 2048
DEPTH = 2

EPS = 1e-6
S5_WIDTH = D_MODEL
S5_GROUP = 16
S5_GROUPS = S5_WIDTH // S5_GROUP
S5_STATE = 64
S5_CHUNK = 128
M_WIDTH = D_MODEL
M_HEADS = 4
M_HEAD_DIM = M_WIDTH // M_HEADS
M_CONV = 4
M_CHUNK = 128
A_HEAD_DIM = 64
A_HEADS = D_MODEL // A_HEAD_DIM
A_KV_HEADS = A_HEADS // 4
A_WINDOW = 128
ROPE_THETA = 500000.0
ROPE_DIM = A_HEAD_DIM // 4
EVEN_IN = 2 * S5_WIDTH + 2 * M_WIDTH
EVEN_OUT = S5_WIDTH + M_WIDTH
A_Q = A_HEADS * A_HEAD_DIM
A_KV = A_KV_HEADS * A_HEAD_DIM
ODD_IN = 2 * A_Q + 2 * A_KV
N_EVEN = (DEPTH + 1) // 2
N_ODD = DEPTH // 2

kernel_name = 'hybrid_s5_mlstm_swa_trunk'

F32 = jnp.float32

def rmsnorm(x, g):
    xf = x.astype(F32)
    return xf * lax.rsqrt(jnp.mean(xf * xf, axis=-1, keepdims=True) + EPS) * g.astype(F32)

def adaln(c, w, b):
    m = jax.nn.silu(c.astype(F32)) @ w.astype(F32) + b.astype(F32)
    shift, scale, gate = jnp.split(m[:, None, :], 3, axis=-1)
    return shift, scale, gate

def _lin_rec(e1, e2):
    a1, b1 = e1
    a2, b2 = e2
    return a1 * a2, a2 * b1 + b2

def s5_mixer(u, a_re, a_im, log_dt, b_re, b_im, c_re, c_im, d_skip, w_glu):
    bsz, seq, _ = u.shape
    n_chunks = seq // S5_CHUNK
    a = lax.complex(a_re.astype(F32), a_im.astype(F32))
    dt = jnp.exp(log_dt.astype(F32))[:, None]
    a_bar = jnp.exp(a * dt)
    b_bar = ((a_bar - 1.0) / a)[..., None] * lax.complex(b_re.astype(F32), b_im.astype(F32))
    c_mat = lax.complex(c_re.astype(F32), c_im.astype(F32))
    u_chunks = jnp.moveaxis(u.reshape(bsz, n_chunks, S5_CHUNK, S5_GROUPS, S5_GROUP), 1, 0)

    def chunk_step(state, u_c):
        bu = jnp.einsum('btgp,gnp->btgn', u_c.astype(jnp.complex64), b_bar)
        a_cum, xs = lax.associative_scan(_lin_rec, (jnp.broadcast_to(a_bar, bu.shape), bu), axis=1)
        xs = xs + a_cum * state[:, None]
        y = jnp.einsum('btgn,gpn->btgp', xs, c_mat).real
        return xs[:, -1], y

    state0 = jnp.zeros((bsz, S5_GROUPS, S5_STATE), jnp.complex64)
    _, y = lax.scan(chunk_step, state0, u_chunks)
    y = jnp.moveaxis(y, 0, 1).reshape(bsz, seq, S5_WIDTH)
    y = jax.nn.gelu(y + d_skip.astype(F32) * u)
    return y * jax.nn.sigmoid(y @ w_glu.astype(F32))

def causal_conv(x, w, b):
    seq = x.shape[1]
    k_taps = w.shape[0]
    xp = jnp.pad(x, ((0, 0), (k_taps - 1, 0), (0, 0)))
    out = xp[:, 0:seq] * w[0]
    for t in range(1, k_taps):
        out = out + xp[:, t:t + seq] * w[t]
    return out + b

def mlstm_cell(q, k, v, log_i, log_f):
    bsz, nh, seq, dh = q.shape
    n_chunks = seq // M_CHUNK
    chunk = lambda t: jnp.moveaxis(t.reshape(bsz, nh, n_chunks, M_CHUNK, *t.shape[3:]), 2, 0)
    tri = jnp.tril(jnp.ones((M_CHUNK, M_CHUNK), dtype=bool))

    def step(carry, inp):
        c_st, n_st, m_st = carry
        qc, kc, vc, li, lf = inp
        b = jnp.cumsum(lf, axis=-1)
        d_log = b[..., :, None] - b[..., None, :] + li[..., None, :]
        d_log = jnp.where(tri, d_log, -jnp.inf)
        inter = b + m_st[..., None]
        m_t = jnp.maximum(inter, jnp.max(d_log, axis=-1))
        s = jnp.einsum('bhtd,bhsd->bhts', qc, kc) * jnp.exp(d_log - m_t[..., None])
        g = jnp.exp(inter - m_t)
        num = jnp.einsum('bhts,bhsd->bhtd', s, vc) + g[..., None] * jnp.einsum('bhtd,bhde->bhte', qc, c_st)
        den = jnp.sum(s, axis=-1) + g * jnp.einsum('bhtd,bhd->bht', qc, n_st)
        h = num / jnp.maximum(jnp.abs(den), jnp.exp(-m_t))[..., None]
        b_last = b[..., -1]
        w_log = b_last[..., None] - b + li
        m_new = jnp.maximum(b_last + m_st, jnp.max(w_log, axis=-1))
        w_k = jnp.exp(w_log - m_new[..., None])
        decay = jnp.exp(b_last + m_st - m_new)
        c_new = decay[..., None, None] * c_st + jnp.einsum('bhs,bhsd,bhse->bhde', w_k, kc, vc)
        n_new = decay[..., None] * n_st + jnp.einsum('bhs,bhsd->bhd', w_k, kc)
        return (c_new, n_new, m_new), h

    carry0 = (jnp.zeros((bsz, nh, dh, dh), F32), jnp.zeros((bsz, nh, dh), F32), jnp.zeros((bsz, nh), F32))
    _, h = lax.scan(step, carry0, (chunk(q), chunk(k), chunk(v), chunk(log_i), chunk(log_f)))
    return jnp.moveaxis(h, 0, 2).reshape(bsz, nh, seq, dh)

def mlstm_mixer(m_in, conv_w, conv_b, wq, wk, wv, wo, w_if, b_if, norm_g, skip):
    bsz, seq, _ = m_in.shape
    xc = jax.nn.silu(causal_conv(m_in, conv_w.astype(F32), conv_b.astype(F32)))
    heads = lambda t: t.reshape(bsz, seq, M_HEADS, M_HEAD_DIM)
    q = jnp.einsum('blhd,hde->bhle', heads(xc), wq.astype(F32))
    k = jnp.einsum('blhd,hde->bhle', heads(xc), wk.astype(F32)) * (M_HEAD_DIM ** -0.5)
    v = jnp.einsum('blhd,hde->bhle', heads(m_in), wv.astype(F32))
    o = jax.nn.sigmoid(jnp.einsum('blhd,hde->blhe', heads(m_in), wo.astype(F32)))
    gates = jnp.concatenate([xc, m_in], axis=-1) @ w_if.astype(F32) + b_if.astype(F32)
    gates = jnp.moveaxis(gates, -1, 1)
    log_i = gates[:, :M_HEADS]
    log_f = jax.nn.log_sigmoid(gates[:, M_HEADS:])
    h = jnp.moveaxis(mlstm_cell(q, k, v, log_i, log_f), 1, 2)
    h = rmsnorm(o * h, norm_g) + skip.astype(F32).reshape(M_HEADS, M_HEAD_DIM) * heads(xc)
    return h.reshape(bsz, seq, M_WIDTH)

def s5_mlstm_layer(hn, w_in, a_re, a_im, log_dt, b_re, b_im, c_re, c_im, d_skip, w_glu,
                   conv_w, conv_b, wq, wk, wv, wo, w_if, b_if, m_norm_g, m_skip, w_out):
    proj = hn @ w_in.astype(F32)
    s5_u, s5_z, m_in, m_z = jnp.split(proj, [S5_WIDTH, 2 * S5_WIDTH, 2 * S5_WIDTH + M_WIDTH], axis=-1)
    y_s5 = s5_mixer(s5_u, a_re, a_im, log_dt, b_re, b_im, c_re, c_im, d_skip, w_glu) * jax.nn.silu(s5_z)
    y_m = mlstm_mixer(m_in, conv_w, conv_b, wq, wk, wv, wo, w_if, b_if, m_norm_g, m_skip) * jax.nn.silu(m_z)
    return jnp.concatenate([y_s5, y_m], axis=-1) @ w_out.astype(F32)

def rope_partial(x, positions):
    half = ROPE_DIM // 2
    inv_freq = jnp.exp(-math.log(ROPE_THETA) * jnp.arange(half, dtype=F32) / half)
    ang = positions.astype(F32)[..., None] * inv_freq
    cos = jnp.cos(ang)[:, :, None, :]
    sin = jnp.sin(ang)[:, :, None, :]
    x1 = x[..., :half]
    x2 = x[..., half:ROPE_DIM]
    return jnp.concatenate([x1 * cos - x2 * sin, x2 * cos + x1 * sin, x[..., ROPE_DIM:]], axis=-1)

def sliding_window_attention(q, k, v, sinks):
    bsz, seq, _, hd = q.shape
    grp = A_HEADS // A_KV_HEADS
    n_blocks = seq // A_WINDOW
    qb = q.reshape(bsz, n_blocks, A_WINDOW, A_KV_HEADS, grp, hd)
    kp = jnp.pad(k, ((0, 0), (A_WINDOW, 0), (0, 0), (0, 0)))
    vp = jnp.pad(v, ((0, 0), (A_WINDOW, 0), (0, 0), (0, 0)))
    qi = jnp.arange(A_WINDOW)[:, None] + A_WINDOW
    ki = jnp.arange(2 * A_WINDOW)[None, :]
    rel = qi - ki
    band = (rel >= 0) & (rel < A_WINDOW)
    sink_logits = sinks.astype(F32).reshape(A_KV_HEADS, grp)[None, :, :, None, None]
    scale = hd ** -0.5

    def block(j):
        qj = lax.dynamic_index_in_dim(qb, j, axis=1, keepdims=False)
        kj = lax.dynamic_slice_in_dim(kp, j * A_WINDOW, 2 * A_WINDOW, axis=1)
        vj = lax.dynamic_slice_in_dim(vp, j * A_WINDOW, 2 * A_WINDOW, axis=1)
        s = jnp.einsum('bqkgd,bskd->bkgqs', qj, kj) * scale
        valid = band & (ki + j * A_WINDOW - A_WINDOW >= 0)
        s = jnp.where(valid, s, -jnp.inf)
        sink = jnp.broadcast_to(sink_logits, s.shape[:-1] + (1,))
        p = jax.nn.softmax(jnp.concatenate([s, sink], axis=-1), axis=-1)[..., :-1]
        return jnp.einsum('bkgqs,bskd->bqkgd', p, vj)

    out = lax.map(block, jnp.arange(n_blocks))
    return jnp.moveaxis(out, 0, 1).reshape(bsz, seq, A_Q)

def swa_layer(hn, positions, w_in, q_g, k_g, sinks, w_out):
    bsz, seq, _ = hn.shape
    proj = hn @ w_in.astype(F32)
    q, k, v, z = jnp.split(proj, [A_Q, A_Q + A_KV, A_Q + 2 * A_KV], axis=-1)
    q = rope_partial(rmsnorm(q.reshape(bsz, seq, A_HEADS, A_HEAD_DIM), q_g), positions)
    k = rope_partial(rmsnorm(k.reshape(bsz, seq, A_KV_HEADS, A_HEAD_DIM), k_g), positions)
    v = v.reshape(bsz, seq, A_KV_HEADS, A_HEAD_DIM)
    a = sliding_window_attention(q, k, v, sinks)
    return (a * jax.nn.silu(z)) @ w_out.astype(F32)

def setup_inputs(seed: int = 0) -> dict:
    key = jax.random.key(seed)
    ks = iter(jax.random.split(key, 64))

    def nrm(shape, scale):
        return jax.random.normal(next(ks), shape, F32) * scale

    ne, no = N_EVEN, N_ODD
    g, n, p = S5_GROUPS, S5_STATE, S5_GROUP
    x = nrm((BATCH, SEQ, D_MODEL), 1.0)
    c = nrm((BATCH, D_MODEL), 1.0)
    positions = jnp.arange(SEQ, dtype=jnp.int32)[None, :] + jax.random.randint(next(ks), (BATCH, 1), 0, 1024, dtype=jnp.int32)
    ada_w = nrm((DEPTH, D_MODEL, 3 * D_MODEL), 0.5 * D_MODEL ** -0.5)
    ada_b = nrm((DEPTH, 3 * D_MODEL), 0.02)
    norm_g = 1.0 + nrm((DEPTH, D_MODEL), 0.02)
    ev_w_in = nrm((ne, D_MODEL, EVEN_IN), D_MODEL ** -0.5)
    s5_a_re = -0.5 * jnp.exp(nrm((ne, g, n), 0.05))
    s5_a_im = math.pi * jnp.arange(n, dtype=F32) + nrm((ne, g, n), 0.01)
    s5_log_dt = jax.random.uniform(next(ks), (ne, g), F32, math.log(1e-3), math.log(1e-1))
    s5_b_re = nrm((ne, g, n, p), (2 * p) ** -0.5)
    s5_b_im = nrm((ne, g, n, p), (2 * p) ** -0.5)
    s5_c_re = nrm((ne, g, p, n), (2 * n) ** -0.5)
    s5_c_im = nrm((ne, g, p, n), (2 * n) ** -0.5)
    s5_d = nrm((ne, S5_WIDTH), 1.0)
    s5_w_glu = nrm((ne, S5_WIDTH, S5_WIDTH), S5_WIDTH ** -0.5)
    m_conv_w = nrm((ne, M_CONV, M_WIDTH), M_CONV ** -0.5)
    m_conv_b = nrm((ne, M_WIDTH), 0.02)
    m_wq = nrm((ne, M_HEADS, M_HEAD_DIM, M_HEAD_DIM), M_HEAD_DIM ** -0.5)
    m_wk = nrm((ne, M_HEADS, M_HEAD_DIM, M_HEAD_DIM), M_HEAD_DIM ** -0.5)
    m_wv = nrm((ne, M_HEADS, M_HEAD_DIM, M_HEAD_DIM), M_HEAD_DIM ** -0.5)
    m_wo = nrm((ne, M_HEADS, M_HEAD_DIM, M_HEAD_DIM), M_HEAD_DIM ** -0.5)
    m_w_if = nrm((ne, 2 * M_WIDTH, 2 * M_HEADS), 0.1 * (2 * M_WIDTH) ** -0.5)
    m_b_if = jnp.concatenate([nrm((ne, M_HEADS), 0.1), jnp.linspace(3.0, 6.0, M_HEADS, dtype=F32) + nrm((ne, M_HEADS), 0.01)], axis=-1)
    m_norm_g = 1.0 + nrm((ne, M_HEADS, M_HEAD_DIM), 0.02)
    m_skip = 1.0 + nrm((ne, M_WIDTH), 0.02)
    ev_w_out = nrm((ne, EVEN_OUT, D_MODEL), EVEN_OUT ** -0.5)
    od_w_in = nrm((no, D_MODEL, ODD_IN), D_MODEL ** -0.5)
    od_q_norm_g = 1.0 + nrm((no, A_HEAD_DIM), 0.02)
    od_k_norm_g = 1.0 + nrm((no, A_HEAD_DIM), 0.02)
    od_sinks = nrm((no, A_HEADS), 1.0)
    od_w_out = nrm((no, A_Q, D_MODEL), A_Q ** -0.5)
    return {'x': x, 'c': c, 'positions': positions, 'ada_w': ada_w, 'ada_b': ada_b, 'norm_g': norm_g,
            'ev_w_in': ev_w_in, 's5_a_re': s5_a_re, 's5_a_im': s5_a_im, 's5_log_dt': s5_log_dt,
            's5_b_re': s5_b_re, 's5_b_im': s5_b_im, 's5_c_re': s5_c_re, 's5_c_im': s5_c_im,
            's5_d': s5_d, 's5_w_glu': s5_w_glu, 'm_conv_w': m_conv_w, 'm_conv_b': m_conv_b,
            'm_wq': m_wq, 'm_wk': m_wk, 'm_wv': m_wv, 'm_wo': m_wo, 'm_w_if': m_w_if, 'm_b_if': m_b_if,
            'm_norm_g': m_norm_g, 'm_skip': m_skip, 'ev_w_out': ev_w_out, 'od_w_in': od_w_in,
            'od_q_norm_g': od_q_norm_g, 'od_k_norm_g': od_k_norm_g, 'od_sinks': od_sinks, 'od_w_out': od_w_out}

def reference(x, c, positions, ada_w, ada_b, norm_g, ev_w_in, s5_a_re, s5_a_im, s5_log_dt,
              s5_b_re, s5_b_im, s5_c_re, s5_c_im, s5_d, s5_w_glu, m_conv_w, m_conv_b,
              m_wq, m_wk, m_wv, m_wo, m_w_if, m_b_if, m_norm_g, m_skip, ev_w_out, od_w_in,
              od_q_norm_g, od_k_norm_g, od_sinks, od_w_out):
    h = x.astype(F32)
    for layer in range(DEPTH):
        shift, scale, gate = adaln(c, ada_w[layer], ada_b[layer])
        hn = rmsnorm(h, norm_g[layer]) * (1.0 + scale) + shift
        if layer % 2 == 0:
            e = layer // 2
            y = s5_mlstm_layer(hn, ev_w_in[e], s5_a_re[e], s5_a_im[e], s5_log_dt[e], s5_b_re[e], s5_b_im[e],
                               s5_c_re[e], s5_c_im[e], s5_d[e], s5_w_glu[e], m_conv_w[e], m_conv_b[e],
                               m_wq[e], m_wk[e], m_wv[e], m_wo[e], m_w_if[e], m_b_if[e], m_norm_g[e],
                               m_skip[e], ev_w_out[e])
        else:
            o = layer // 2
            y = swa_layer(hn, positions, od_w_in[o], od_q_norm_g[o], od_k_norm_g[o], od_sinks[o], od_w_out[o])
        h = h + gate * y
    return h.astype(x.dtype)


_drawn_inputs = setup_inputs


def setup_inputs(seed=0):
    import zlib

    import numpy as np

    out = dict(_drawn_inputs(seed))
    spreads = {}
    factors = {'ada_b': 3.158,
     'norm_g': 7.201,
     's5_a_re': 64.0,
     's5_a_im': 64.0,
     's5_log_dt': 64.0,
     's5_b_re': 64.0,
     's5_b_im': 64.0,
     's5_c_re': 64.0,
     's5_c_im': 64.0,
     's5_w_glu': 3.139,
     'm_conv_b': 7.837,
     'm_w_if': 6.462,
     'm_norm_g': 45.876,
     'm_skip': 8.0,
     'od_q_norm_g': 23.453,
     'od_k_norm_g': 8.0,
     'od_sinks': 200.0}
    for name, (base, spread) in spreads.items():
        noise = np.random.default_rng([zlib.crc32(name.encode()), seed]).standard_normal(out[name].shape)
        drawn = base * np.exp(spread * noise) if base else spread * noise
        out[name] = jnp.asarray(drawn.astype(out[name].dtype))
    for name, factor in factors.items():
        out[name] = (out[name] * factor).astype(out[name].dtype)
    return out
```

```python
import math
from contextlib import ExitStack

import numpy as np
import concourse.bass as bass
from concourse import mybir

ALU = mybir.AluOpType
ACT = mybir.ActivationFunctionType
AX = mybir.AxisListType
F32 = mybir.dt.float32
F32R = mybir.dt.float32r
I32 = mybir.dt.int32

P = 128
D = 1024
KC = D // P
SEQ = 2048
TT = SEQ // P
NB = 4
BT = SEQ // NB
EPS = 1e-6

G = 64
GP = 16
NS = 64
CH = 8
NCH = SEQ // CH
KB = NCH // NB

MH = 4
HD = 256
MC = 128
NMC = SEQ // MC

AH = 16
AKV = 4
AD = 64
ROPE = AD // 4
THETA = 500000.0

NEG = -1.0e30
TWO_PI = 2.0 * math.pi
ROUND = 1.5 * 2.0 ** 23
PI_SAFE = 3.1415925
TWO_PI_PARTS = (6.28125, 1.9350051879882812e-3, TWO_PI - 6.28125 - 1.9350051879882812e-3)

ROWS = {}
_at = 0
for _name, _n in (("ada_b", 48), ("norm_g", 16), ("s5_d", 8), ("conv_w", 32), ("conv_b", 8),
                  ("m_norm_g", 8), ("m_skip", 8)):
    ROWS[_name] = _at
    _at += _n
assert _at == P

BIN, BIS, COC, COS, TOE = 0, 128, 256, 384, 512
EBC, EBS, EAC, EAS, RAD = 640, 656, 672, 688, 704
BW = 708


class Tally:

    def __init__(self, sem, step=1):
        self.sem, self.step = sem, step
        self.base, self.k, self.i, self.per, self.start = 0, 0, None, 0, 0

    def add(self, ins):
        ins.then_inc(self.sem, self.step)
        self.k += 1
        return self.mark()

    def mark(self):
        value = (self.base + self.k) * self.step
        return value if self.i is None else (self.i - self.start) * (self.per * self.step) + value

    def enter(self, i, per, start=0):
        self.base, self.k, self.i, self.per, self.start = self.base + self.k, 0, i, per, start

    def leave(self, rounds):
        assert self.k == self.per, (self.k, self.per)
        self.base, self.k, self.i = self.base + rounds * self.per, 0, None


def rope_frequencies():
    half = ROPE // 2
    return [float(x) for x in np.exp(np.float32(-math.log(THETA)) * np.arange(half, dtype=np.float32) / np.float32(half))]


def rsqrt_steps(nc, link, v, root, out, tmp):
    link(nc.vector.reciprocal(out, root))
    link(nc.vector.tensor_tensor(tmp, v, out, ALU.mult))
    link(nc.vector.scalar_tensor_tensor(out=tmp, in0=tmp, scalar=-0.5, in1=out, op0=ALU.mult, op1=ALU.mult))
    link(nc.vector.scalar_tensor_tensor(out=out, in0=tmp, scalar=1.5, in1=out, op0=ALU.add, op1=ALU.mult))


def exp_steps(nc, link, dst, x, n, r, whole):
    ts, stt = nc.vector.tensor_scalar, nc.vector.scalar_tensor_tensor
    link(ts(n, x, 1.0 / math.log(2.0), ROUND, ALU.mult, ALU.add))
    link(ts(n, n, ROUND, None, ALU.subtract))
    link(ts(n, n, -127.0, 128.0, ALU.max, ALU.min))
    link(stt(out=r, in0=n, scalar=-0.693359375, in1=x, op0=ALU.mult, op1=ALU.add))
    link(stt(out=r, in0=n, scalar=0.693359375 - math.log(2.0), in1=r, op0=ALU.mult, op1=ALU.add))
    link(ts(r, r, 0.35, -0.35, ALU.min, ALU.max))
    link(ts(n, n, 127.0, 2.0 ** 23, ALU.add, ALU.mult))
    link(nc.vector.tensor_copy(whole, n))
    link(ts(n, r, 1.0 / math.factorial(7), None, ALU.mult))
    for k in range(6, 0, -1):
        link(stt(out=n, in0=n, scalar=1.0 / math.factorial(k), in1=r, op0=ALU.add, op1=ALU.mult))
    link(stt(out=dst, in0=n, scalar=1.0, in1=whole.bitcast(F32), op0=ALU.add, op1=ALU.mult))


class Core:
    pass


def names(nc, ctx):
    m = Core()
    m.nc, m.ctx = nc, ctx

    m.sems = []

    def sem(name):
        m.sems.append(nc.alloc_semaphore(name=name))
        return m.sems[-1]

    def clear():
        nc.all_engine_barrier()
        nc.clear_and_free_semaphores(m.sems)
        nc.all_engine_barrier()
        m.sems = []

    def dram(name, shape):
        return nc.dram_tensor(name, shape, F32, kind="Internal").ap()

    m.sem, m.clear = sem, clear
    m.u_d = dram("u_d", [D, NB, CH, KB])
    m.y_d = dram("y_d", [D, NB, CH, KB])
    m.sz_d = dram("sz_d", [D, NB, CH, KB])
    m.m_d = dram("m_d", [D, SEQ])
    m.xc_d = dram("xc_d", [D, SEQ])
    m.smz_d = dram("smz_d", [D, SEQ])
    m.ys_d = dram("ys_d", [D, SEQ])
    m.h1_d = dram("h1_d", [SEQ, D])
    m.gate_d = dram("gate_d", [2, D])
    m.s5w_d = dram("s5w_d", [G, P, BW])
    m.kz_d = dram("kz_d", [G, GP, 240])
    m.gt_d = dram("gt_d", [2 * MH, SEQ])
    m.mx_d = dram("mx_d", [4, MH * NMC])
    m.gb_d = dram("gb_d", [MH * NMC, MC])
    m.ident = ctx.enter_context(nc.sbuf_tensor("ident", [P, P], F32))
    m.cols = ctx.enter_context(nc.sbuf_tensor("cols", [P, P], F32))
    m.ada = ctx.enter_context(nc.sbuf_tensor("ada", [P, 2, 24], F32))
    m.gacc = ctx.enter_context(nc.sbuf_tensor("gate_sums", [2 * MH, SEQ], F32))
    m.decay = ctx.enter_context(nc.sbuf_tensor("decay", [P, MH, NMC], F32))
    m.gcol = ctx.enter_context(nc.sbuf_tensor("gate_cols", [P, NMC, 4, MH], F32))
    m.moda = ctx.enter_context(nc.sbuf_tensor("moda", [P, 2, KC], F32))
    return m


def modulation(m, a):
    nc = m.nc
    with ExitStack() as ctx:
        sb = lambda n, s: ctx.enter_context(nc.sbuf_tensor(n, s, F32))
        rows = sb("vec_rows", [P, P])
        crow = sb("c_row", [KC, P])
        cs = sb("c_silu", [P, 2 * KC])
        wr = [sb(f"ada_w{j}", [P, 3 * D]) for j in range(2)]
        grow = sb("gate_rows", [KC, 2 * P])
        ps_v = ctx.enter_context(nc.psum_tensor("ps_vec", [P, 512], F32))
        ps_a = ctx.enter_context(nc.psum_tensor("ps_ada", [P, 512], F32))
        rows_in = m.sem("mod_rows_in")
        ident_ready = m.sem("mod_ident_ready")
        turned = m.sem("mod_turned")
        cols_ready = m.sem("mod_cols_ready")
        silu_ready = m.sem("mod_silu_ready")
        w_in = [m.sem(f"mod_w_in{j}") for j in range(2)]
        w_used = m.sem("mod_w_used")
        sum_read = m.sem("mod_sum_read")
        gate_turned = m.sem("mod_gate_turned")
        gate_out = m.sem("mod_gate_out")
        gate_copied = m.sem("mod_gate_copied")
        wflat = a["ada_w"].rearrange("l k n -> (l k) n").rearrange("(t p) n -> t p n", p=P)
        HALF = KC // 2
        with nc.Block() as block:
            @block.sync
            def _(sp):
                for name, pat in (("ada_b", "l (j p) -> (l j) p"), ("norm_g", "l (j p) -> (l j) p"),
                                  ("s5_d", "l (j p) -> (l j) p"), ("m_conv_w", "l t (j p) -> (l t j) p"),
                                  ("m_conv_b", "l (j p) -> (l j) p"), ("m_norm_g", "l h (j p) -> (l h j) p"),
                                  ("m_skip", "l (j p) -> (l j) p")):
                    src = a[name].rearrange(pat, p=P)
                    r = ROWS[name[2:] if name.startswith("m_conv") else name]
                    sp.dma_start(rows[r:r + src.shape[0], :], src).then_inc(rows_in, 16)
                sp.dma_start(crow[:], a["c"].rearrange("o (j p) -> (o j) p", p=P)).then_inc(rows_in, 16)
                for l in range(2):
                    with sp.Fori(0, HALF) as i:
                        for j in range(2):
                            sp.wait_ge(w_used, i * 2 + (2 * HALF * l + j + 1))
                            sp.dma_start(wr[j][:], wflat[i * 2 + (KC * l + j)]).then_inc(w_in[j], 16)
                sp.wait_ge(gate_copied, 1)
                sp.dma_start(m.gate_d.rearrange("l (j p) -> j l p", p=P),
                             grow[:].rearrange("j (l p) -> j l p", l=2)).then_inc(gate_out, 16)
                sp.wait_ge(gate_out, 16)

            @block.gpsimd
            def _(pool):
                nc.gpsimd.memset(m.ident[:], 0.0).then_inc(ident_ready, 1)
                pool.wait_ge(ident_ready, 1)
                nc.gpsimd.affine_select(out=m.ident[:], in_=m.ident[:], compare_op=ALU.not_equal, fill=1.0,
                                        base=0, pattern=[[-1, P]], channel_multiplier=1).then_inc(ident_ready, 1)

            @block.scalar
            def _(act):
                act.wait_ge(turned, 1)
                for l in range(2):
                    last = nc.scalar.activation(cs[:, KC * l:KC * l + KC], ps_v[:, P:P + KC], ACT.Silu)
                last.then_inc(silu_ready, 1)
                act.wait_ge(gate_turned, 1)
                nc.scalar.copy(grow[:], ps_v[0:KC, 0:2 * P]).then_inc(gate_copied, 1)

            @block.vector
            def _(v):
                v.wait_ge(turned, 1)
                v.wait_ge(silu_ready, 1)
                nc.vector.tensor_copy(m.cols[:], ps_v[:, 0:P]).then_inc(cols_ready, 1)
                v.wait_ge(cols_ready, 1)
                nc.vector.tensor_copy(m.ada[:], m.cols[:, 0:48].rearrange("p (l j) -> p l j", l=2)).then_inc(cols_ready, 1)
                v.wait_ge(cols_ready, 2)
                for l in range(2):
                    with v.Fori(0, HALF) as i:
                        v.wait_ge(w_used, i * 2 + (2 * HALF * l + 4))
                        v.wait_ge(sum_read, i + (HALF * l + 1))
                        nc.vector.tensor_tensor(m.ada[:, l, :], ps_a[:, 0:24], m.ada[:, l, :], ALU.add).then_inc(sum_read, 1)
                    v.wait_ge(sum_read, HALF * (l + 1) + 1)
                    last = nc.vector.scalar_tensor_tensor(
                        out=m.moda[:, l, :], in0=m.ada[:, l, KC:2 * KC], scalar=1.0,
                        in1=m.cols[:, ROWS["norm_g"] + KC * l:ROWS["norm_g"] + KC * l + KC],
                        op0=ALU.add, op1=ALU.mult)
                last.then_inc(cols_ready, 1)

            @block.tensor
            def _(pe):
                pe.wait_ge(rows_in, 16 * 8)
                pe.wait_ge(ident_ready, 2)
                nc.tensor.transpose(ps_v[:, 0:P], rows[:], m.ident[:])
                nc.tensor.transpose(ps_v[:, P:P + KC], crow[:], m.ident[0:KC, 0:KC]).then_inc(turned, 1)
                pe.wait_ge(silu_ready, 1)
                pe.sem_inc(w_used, 2)
                pe.sem_inc(sum_read, 1)
                for l in range(2):
                    with pe.Fori(0, HALF) as i:
                        pe.wait_ge(sum_read, i + (HALF * l + 1))
                        for j in range(2):
                            pe.wait_ge(w_in[j], i * 16 + (16 * HALF * l + 16))
                            for n in range(24):
                                mm = nc.tensor.matmul(ps_a[:, n:n + 1], wr[j][:, n * P:(n + 1) * P],
                                                      cs[:, bass.ds(i * 2 + j, 1)], start=(j == 0 and n == 0),
                                                      stop=(j == 1 and n == 23), skip_group_check=True)
                            mm.then_inc(w_used, 1)
                pe.wait_ge(cols_ready, 3)
                nc.tensor.transpose(ps_v[0:KC, 0:P], m.ada[:, 0, 2 * KC:3 * KC], m.ident[:])
                nc.tensor.transpose(ps_v[0:KC, P:2 * P], m.ada[:, 1, 2 * KC:3 * KC], m.ident[:]).then_inc(gate_turned, 1)


def s5_tables(m, a):
    nc = m.nc
    with ExitStack() as ctx:
        sb = lambda n, s, d=F32: ctx.enter_context(nc.sbuf_tensor(n, s, d))
        ab = sb("a_rows", [G, 2, P])
        are, aim = sb("a_re", [P, G]), sb("a_im", [P, G])
        dt = sb("dt", [P, G])
        bx, by = sb("b_x", [P, G, GP]), sb("b_y", [P, G, GP])
        cnat = sb("c_nat", [P, 2, KC, P])
        cx, cy = sb("c_x", [P, G, GP]), sb("c_y", [P, G, GP])
        btx, bty = sb("bt_x", [P, G, GP]), sb("bt_y", [P, G, GP])
        t = [sb(f"s5_t{j}", [P, G]) for j in range(6)]
        ti = sb("s5_ti", [P, G], I32)
        unit = [sb(f"unit_{j}", [P, G, CH + 1]) for j in range(2)]
        eb = [sb(f"eb_{j}", [P, G, 17]) for j in range(2)]
        ea = [sb(f"ea_{j}", [P, G, 17]) for j in range(2)]
        er = sb("er", [P, G, CH + 1])
        pw = [sb(f"pw_{j}", [P, G, CH + 1]) for j in range(2)]
        rv = [sb(f"rv_{j}", [P, G, CH]) for j in range(2)]
        qw = [sb(f"qw_{j}", [P, G, CH]) for j in range(3)]
        tw = [sb(f"s5_w{j}", [P, G, 8]) for j in range(4)]
        tmp = [sb(f"s5_m{j}", [P, 8, CH, GP]) for j in range(3)]
        tmq = [sb(f"s5_q{j}", [P, 8, CH, GP]) for j in range(2)]
        nx, ny, kx = (sb(n, [P, 8, CH, GP]) for n in ("n_x", "n_y", "k_x"))
        btx_s = sb("bt_x_slice", [P, 8, GP])
        pack = sb("s5_pack", [P, 8, 512])
        smal = sb("s5_small", [P, G, BW - EBC])
        kz = sb("kz", [GP, 8, 240])
        ps_t = [ctx.enter_context(nc.psum_tensor(f"ps_t{j}", [P, 4, P], F32)) for j in range(4)]
        ps_k = ctx.enter_context(nc.psum_tensor("ps_k", [P, 8, P], F32))
        a_in = m.sem("s5_a_in")
        bc_in = m.sem("s5_bc_in")
        a_turned = m.sem("s5_a_turned")
        c_turned = m.sem("s5_c_turned")
        angle_ready = m.sem("s5_angle_ready")
        unit_ready = m.sem("s5_unit_ready")
        c_ready = m.sem("s5_c_ready")
        b_ready = m.sem("s5_b_ready")
        dve = Tally(m.sem("s5_dve"))
        pool_done = Tally(m.sem("s5_pool"))
        base_ready = m.sem("s5_base_ready")
        nat_ready = m.sem("s5_nat_ready")
        nat_turned = m.sem("s5_nat_turned")
        kz_zeroed = m.sem("s5_kz_zeroed")
        ps_free = m.sem("s5_ps_free")
        nat_free = m.sem("s5_nat_free")
        out_mats_ready = m.sem("s5_out_mats_ready")
        stored = m.sem("s5_stored")
        small_stored = m.sem("s5_small_stored")
        toe_stored = m.sem("s5_toe_stored")

        with nc.Block() as block:
            @block.sync
            def _(sp):
                for j, n in enumerate(("s5_a_re", "s5_a_im")):
                    for h in range(2):
                        sp.dma_start(ab[:, j, h * NS:(h + 1) * NS], a[n][0]).then_inc(a_in, 16)
                sp.dma_start(dt[:], a["s5_log_dt"].broadcast_to([P, G])).then_inc(a_in, 16)
                cre = a["s5_c_re"].rearrange("o g p n -> (o g p) n").rearrange("(j r) n -> r j n", r=P)
                cim = a["s5_c_im"].rearrange("o g p n -> (o g p) n").rearrange("(j r) n -> r j n", r=P)
                for w, halves in enumerate(((cre, cim), (cim, cre))):
                    for h in range(2):
                        sp.dma_start(cnat[:, w, :, h * NS:(h + 1) * NS], halves[h]).then_inc(bc_in, 16)
                bre = a["s5_b_re"].rearrange("o g n p -> (o n) g p")
                bim = a["s5_b_im"].rearrange("o g n p -> (o n) g p")
                sp.dma_start(bx[0:NS], bre).then_inc(bc_in, 16)
                sp.dma_start(bx[NS:P], bim).then_inc(bc_in, 16)
                sp.dma_start(by[0:NS], bim).then_inc(bc_in, 16)
                sp.dma_start(by[NS:P], bre).then_inc(bc_in, 16)
                sp.wait_ge(base_ready, 1)
                sp.dma_start(m.s5w_d[:, :, EBC:BW].rearrange("g p w -> p g w"), smal[:]).then_inc(small_stored, 16)
                sp.sem_inc(stored, 32)
                with sp.Fori(0, KC) as i:
                    sp.wait_ge(out_mats_ready, i + 1)
                    sp.wait_ge(ps_free, i * 5 + 10)
                    sp.dma_start(m.s5w_d[bass.ds(i * 8, 8), :, 0:512].rearrange("g p w -> p g w"), pack[:]).then_inc(stored, 16)
                    sp.dma_start(m.kz_d[bass.ds(i * 8, 8)].rearrange("g p w -> p g w"), kz[:]).then_inc(stored, 16)
                sp.wait_ge(stored, 32 * (KC + 1))
                for i in range(CH):
                    sp.dma_start(m.s5w_d[:, i * GP:(i + 1) * GP, TOE:TOE + P],
                                 m.kz_d[:, :, 112 - 16 * i:240 - 16 * i]).then_inc(toe_stored, 16)
                sp.wait_ge(toe_stored, 16 * CH)
                sp.wait_ge(small_stored, 16)

            @block.scalar
            def _(act):
                act.wait_ge(angle_ready, 1)
                nc.scalar.activation(unit[1][:, :, 1], t[1][:], ACT.Sin)
                nc.scalar.activation(unit[0][:, :, 1], t[2][:], ACT.Sin).then_inc(unit_ready, 1)
                for w, dst in ((0, cx), (1, cy)):
                    for j in range(2):
                        act.wait_ge(c_turned, 2 * w + j + 1)
                        nc.scalar.copy(dst[:, 32 * j:32 * (j + 1), :].rearrange("p (a b) c -> p a (b c)", b=8),
                                       ps_t[2 * w + j][:]).then_inc(c_ready, 1)
                act.wait_ge(c_ready, 4)
                nc.scalar.mul(cx[NS:P], cx[NS:P], -1.0).then_inc(c_ready, 1)
                act.wait_ge(bc_in, 16 * 8)
                nc.scalar.mul(by[0:NS], by[0:NS], -1.0).then_inc(b_ready, 1)
                act.wait_ge(kz_zeroed, 1)
                with act.Fori(0, KC) as i:
                    act.wait_ge(stored, (i + 1) * 32)
                    for h in range(4):
                        act.wait_ge(nat_turned, i * 4 + (h + 1))
                        w, j = h // 2, h % 2
                        nc.scalar.copy(pack[:, 4 * j:4 * j + 4, w * P:(w + 1) * P], ps_t[h][:]).then_inc(ps_free, 1)
                    act.wait_ge(nat_free, i + 2)
                    nc.scalar.copy(kz[:, :, 112:240], ps_k[0:GP]).then_inc(ps_free, 1)

            @block.gpsimd
            def _(pool):
                nc.gpsimd.memset(kz[:], 0.0).then_inc(kz_zeroed, 1)
                pool.wait_ge(base_ready, 2)
                pool.wait_ge(c_ready, 5)
                qr, qi, nq = (q[:] for q in qw)
                with pool.Fori(0, KC) as i:
                    pool_done.enter(i, 6)
                    g8 = bass.ds(i * 8, 8)
                    x = lambda tab: tab[:, g8, :].unsqueeze(3).broadcast_to([P, 8, CH, GP])
                    c = lambda arr: arr[:, g8, :].unsqueeze(2).broadcast_to([P, 8, CH, GP])
                    v4 = lambda lo: pack[:, :, lo:lo + P].rearrange("p g (l q) -> p g l q", l=CH)
                    pool.wait_ge(stored, (i + 1) * 32)
                    for lo, e, A, B in ((COC, qr, cx, cy), (COS, nq, cy, cx)):
                        pool_done.add(nc.gpsimd.tensor_tensor(tmq[0][:], x(e), c(A), ALU.mult))
                        done = pool_done.add(nc.gpsimd.tensor_tensor(tmq[1][:], x(qi), c(B), ALU.mult))
                        pool.wait_ge(pool_done.sem, done)
                        done = pool_done.add(nc.gpsimd.tensor_tensor(v4(lo), tmq[0][:], tmq[1][:], ALU.subtract))
                        pool.wait_ge(pool_done.sem, done)
                    pool.sem_inc(out_mats_ready, 1)
                pool_done.leave(KC)

            @block.vector
            def _(v):
                def L(ins):
                    v.wait_ge(dve.sem, dve.add(ins))

                tt = nc.vector.tensor_tensor
                ts = nc.vector.tensor_scalar
                stt = nc.vector.scalar_tensor_tensor
                v.wait_ge(a_turned, 1)
                L(nc.vector.tensor_copy(are[:], ps_k[:, 0, 0:G]))
                L(nc.vector.tensor_copy(aim[:], ps_k[:, 1, 0:G]))

                def exp(dst, x):
                    exp_steps(nc, L, dst, x, t[4][:], t[5][:], ti[:])

                exp(dt[:], dt[:])
                L(tt(t[0][:], are[:], dt[:], ALU.mult))
                exp(er[:, :, 1], t[0][:])
                L(tt(t[3][:], aim[:], dt[:], ALU.mult))
                L(ts(t[4][:], t[3][:], 1.0 / TWO_PI, ROUND, ALU.mult, ALU.add))
                L(ts(t[4][:], t[4][:], ROUND, None, ALU.subtract))
                for c in TWO_PI_PARTS:
                    L(stt(out=t[3][:], in0=t[4][:], scalar=-c, in1=t[3][:], op0=ALU.mult, op1=ALU.add))
                L(ts(t[1][:], t[3][:], PI_SAFE, -PI_SAFE, ALU.min, ALU.max))
                L(ts(t[4][:], t[3][:], math.pi / 2, -TWO_PI, ALU.is_gt, ALU.mult))
                L(stt(out=t[2][:], in0=t[3][:], scalar=math.pi / 2, in1=t[4][:], op0=ALU.add, op1=ALU.add))
                L(ts(t[2][:], t[2][:], PI_SAFE, -PI_SAFE, ALU.min, ALU.max))
                v.sem_inc(angle_ready, 1)
                for tab in (unit, eb, ea):
                    L(nc.vector.memset(tab[0][:, :, 0:1], 1.0))
                    L(nc.vector.memset(tab[1][:, :, 0:1], 0.0))
                L(nc.vector.memset(er[:, :, 0:1], 1.0))
                L(nc.vector.memset(smal[:], 0.0))
                v.wait_ge(unit_ready, 1)

                def renorm(tab, lo, hi):
                    c, s = (q[:, :, lo:hi] for q in tab)
                    w0, w1 = (q[:, :, 0:hi - lo] for q in tw[2:4])
                    L(tt(w0, c, c, ALU.mult))
                    L(tt(w1, s, s, ALU.mult))
                    L(tt(w0, w0, w1, ALU.add))
                    L(ts(w0, w0, -0.5, 1.5, ALU.mult, ALU.add))
                    L(tt(c, c, w0, ALU.mult))
                    L(tt(s, s, w0, ALU.mult))

                def double(tab, top):
                    n = 1
                    while n < top:
                        lo, hi = n + 1, 2 * n + 1
                        c, s = (q[:, :, 1:n + 1] for q in tab)
                        c2_, s2_ = (q[:, :, n:n + 1].broadcast_to([P, G, n]) for q in tab)
                        oc, os_ = (q[:, :, lo:hi] for q in tab)
                        w = [q[:, :, 0:n] for q in tw]
                        L(tt(w[0], c, c2_, ALU.mult))
                        L(tt(w[1], s, s2_, ALU.mult))
                        L(tt(w[2], c, s2_, ALU.mult))
                        L(tt(w[3], s, c2_, ALU.mult))
                        L(tt(oc, w[0], w[1], ALU.subtract))
                        L(tt(os_, w[2], w[3], ALU.add))
                        renorm(tab, lo, hi)
                        n *= 2

                renorm(unit, 1, 2)
                double(unit, 8)
                for j in range(2):
                    L(nc.vector.tensor_copy(eb[j][:, :, 1:2], unit[j][:, :, 8:9]))
                double(eb, 16)
                for j in range(2):
                    L(nc.vector.tensor_copy(ea[j][:, :, 1:2], eb[j][:, :, 16:17]))
                double(ea, 16)
                for n in (1, 2, 4):
                    L(tt(er[:, :, n + 1:2 * n + 1], er[:, :, 1:n + 1], er[:, :, n:n + 1].broadcast_to([P, G, n]), ALU.mult))
                for j in range(2):
                    L(tt(pw[j][:], er[:], unit[j][:], ALU.mult))
                    L(nc.vector.tensor_copy(smal[:, :, 16 * j:16 * j + 16], eb[j][:, :, 0:16]))
                    L(nc.vector.tensor_copy(smal[:, :, 32 + 16 * j:48 + 16 * j], ea[j][:, :, 0:16]))
                nc.vector.tensor_copy(smal[:, :, 64:65], er[:, :, 8:9]).then_inc(base_ready, 1)
                for j in range(2):
                    for i in range(CH):
                        L(nc.vector.tensor_copy(rv[j][:, :, i:i + 1], pw[j][:, :, CH - 1 - i:CH - i]))
                c = eb[0][:, :, 1:2].broadcast_to([P, G, CH])
                s = eb[1][:, :, 1:2].broadcast_to([P, G, CH])
                pr, pi = pw[0][:, :, 1:CH + 1], pw[1][:, :, 1:CH + 1]
                L(tt(tw[0][:], pr, c, ALU.mult))
                L(tt(tw[1][:], pi, s, ALU.mult))
                L(tt(tw[2][:], pi, c, ALU.mult))
                L(tt(tw[3][:], pr, s, ALU.mult))
                L(tt(qw[0][:], tw[0][:], tw[1][:], ALU.add))
                L(tt(qw[1][:], tw[2][:], tw[3][:], ALU.subtract))
                ts(qw[2][:], qw[0][:], -1.0, None, ALU.mult).then_inc(base_ready, 1)
                L(ts(t[0][:], pw[0][:, :, 1], -1.0, None, ALU.add))
                L(tt(t[1][:], are[:], are[:], ALU.mult))
                L(tt(t[2][:], aim[:], aim[:], ALU.mult))
                L(tt(t[1][:], t[1][:], t[2][:], ALU.add))
                L(nc.vector.reciprocal(t[5][:], t[1][:]))
                p1 = pw[1][:, :, 1]
                L(tt(t[1][:], t[0][:], are[:], ALU.mult))
                L(tt(t[2][:], p1, aim[:], ALU.mult))
                L(tt(t[1][:], t[1][:], t[2][:], ALU.add))
                L(tt(t[1][:], t[1][:], t[5][:], ALU.mult))
                L(tt(t[2][:], p1, are[:], ALU.mult))
                L(tt(t[3][:], t[0][:], aim[:], ALU.mult))
                L(tt(t[2][:], t[2][:], t[3][:], ALU.subtract))
                L(tt(t[2][:], t[2][:], t[5][:], ALU.mult))
                v.wait_ge(b_ready, 1)
                wr, wi = (t[j][:].unsqueeze(2).broadcast_to([P, G, GP]) for j in (1, 2))
                s0 = nx[:].rearrange("p a b c -> p (a b) c")
                s1 = ny[:].rearrange("p a b c -> p (a b) c")
                L(tt(s0, wr, bx[:], ALU.mult))
                L(tt(s1, wi, by[:], ALU.mult))
                L(tt(btx[:], s0, s1, ALU.add))
                L(tt(s0, wr, by[:], ALU.mult))
                L(tt(s1, wi, bx[:], ALU.mult))
                L(tt(bty[:], s0, s1, ALU.subtract))
                v.wait_ge(c_ready, 5)
                with v.Fori(0, KC) as i:
                    dve.enter(i, 7)
                    g8 = bass.ds(i * 8, 8)
                    x = lambda tab, lo, hi: tab[:, g8, lo:hi].unsqueeze(3).broadcast_to([P, 8, CH, GP])
                    c = lambda arr: arr[:, g8, :].unsqueeze(2).broadcast_to([P, 8, CH, GP])
                    v.wait_ge(nat_free, i + 1)
                    for o, A, B, op in ((nx, btx, bty, ALU.add), (ny, bty, btx, None)):
                        dve.add(tt(tmp[0][:], x(rv[0], 0, CH), c(A), ALU.mult))
                        L(tt(tmp[1][:], x(rv[1], 0, CH), c(B), ALU.mult))
                        if op is None:
                            tt(o[:], tmp[1][:], tmp[0][:], ALU.subtract).then_inc(nat_ready, 1)
                        else:
                            tt(o[:], tmp[0][:], tmp[1][:], op).then_inc(nat_ready, 1)
                        v.wait_ge(nat_ready, i * 3 + (1 if op is ALU.add else 2))
                    dve.add(tt(tmp[0][:], x(pw[0], 0, CH), c(cx), ALU.mult))
                    dve.add(nc.vector.tensor_copy(btx_s[:], btx[:, g8, :]))
                    L(tt(tmp[1][:], x(pw[1], 0, CH), c(cy), ALU.mult))
                    tt(kx[:], tmp[0][:], tmp[1][:], ALU.subtract).then_inc(nat_ready, 1)
                    v.wait_ge(nat_ready, i * 3 + 3)
                dve.leave(KC)

            @block.tensor
            def _(pe):
                pe.wait_ge(a_in, 16 * 5)
                nc.tensor.transpose(ps_k[:, 0, 0:G], ab[:, 0, :], m.ident[0:G, 0:G])
                nc.tensor.transpose(ps_k[:, 1, 0:G], ab[:, 1, :], m.ident[0:G, 0:G]).then_inc(a_turned, 1)
                pe.wait_ge(bc_in, 16 * 8)
                for w in range(2):
                    for j in range(KC):
                        tr = nc.tensor.transpose(ps_t[2 * w + j // 4][:, j % 4, :], cnat[:, w, j, :], m.ident[:])
                        if j % 4 == 3:
                            tr.then_inc(c_turned, 1)
                pe.sem_inc(nat_free, 1)
                pe.wait_ge(c_ready, 4)
                pe.wait_ge(angle_ready, 1)
                pe.sem_inc(ps_free, 5)
                with pe.Fori(0, KC) as i:
                    for h in range(4):
                        w, j = h // 2, h % 2
                        pe.wait_ge(nat_ready, i * 3 + (w + 1))
                        pe.wait_ge(ps_free, i * 5 + (h + 1))
                        for g in range(4):
                            tr = nc.tensor.transpose(ps_t[h][:, g, :], (nx, ny)[w][:, 4 * j + g].rearrange("p a b -> p (a b)"), m.ident[:])
                        tr.then_inc(nat_turned, 1)
                    pe.wait_ge(nat_ready, i * 3 + 3)
                    pe.wait_ge(ps_free, i * 5 + 5)
                    for g in range(8):
                        mm = nc.tensor.matmul(ps_k[0:GP, g, :], btx_s[:, g, :], kx[:, g].rearrange("p a b -> p (a b)"),
                                              start=True, stop=True)
                    mm.then_inc(nat_free, 1)


def norm_transposed(m, a):
    nc = m.nc
    with ExitStack() as ctx:
        xt = [ctx.enter_context(nc.sbuf_tensor(f"n_x{j}", [P, D], F32)) for j in range(2)]
        junk = ctx.enter_context(nc.sbuf_tensor("n_junk", [P, D], F32))
        xf = [ctx.enter_context(nc.sbuf_tensor(f"n_f{j}", [P, KC, P], F32)) for j in range(2)]
        st = [ctx.enter_context(nc.sbuf_tensor(f"n_s{j}", [P, 8], F32)) for j in range(2)]
        ps = [ctx.enter_context(nc.psum_tensor(f"n_ps{j}", [P, KC, P], F32)) for j in range(2)]
        x_in = [m.sem(f"n_x_in{j}") for j in range(2)]
        squared = m.sem("n_squared")
        mean_ready = m.sem("n_mean_ready")
        root_ready = m.sem("n_root_ready")
        root = Tally(m.sem("n_root"))
        scaled = m.sem("n_scaled")
        turned = m.sem("n_turned")
        evacuated = m.sem("n_evacuated")
        split = m.sem("n_split")
        hi_done = m.sem("n_hi_done")
        xv = a["x"].rearrange("o (t p) d -> (o t) p d", p=P)
        with nc.Block() as block:
            @block.sync
            def _(sp):
                sp.sem_inc(turned, 2)
                with sp.Fori(0, TT // 2) as i:
                    t = i * 2
                    for j in range(2):
                        sp.wait_ge(turned, t + (j + 1))
                        sp.dma_start(xt[j][:], xv[t + j]).then_inc(x_in[j], 16)

            @block.scalar
            def _(act):
                with act.Fori(0, TT // 2) as i:
                    t = i * 2
                    for j in range(2):
                        act.wait_ge(x_in[j], t * 8 + 16)
                        nc.scalar.activation(junk[:], xt[j][:], ACT.Square, accum_out=st[j][:, 0:1]).then_inc(squared, 1)
                        act.wait_ge(mean_ready, t + (j + 1))
                        nc.scalar.activation(st[j][:, 2:3], st[j][:, 1:2], ACT.Sqrt).then_inc(root_ready, 1)
                        act.wait_ge(turned, t + (j + 3))
                        act.wait_ge(split, t + (j + 1))
                        for c in range(KC):
                            last = nc.scalar.activation(xf[j][:, c, :], ps[j][:, c, :], ACT.Identity,
                                                        scale=m.moda[:, 0, c:c + 1], bias=m.ada[:, 0, c:c + 1])
                        last.then_inc(evacuated, 1)

            @block.vector
            def _(v):
                def L(ins):
                    v.wait_ge(root.sem, root.add(ins))

                v.sem_inc(split, 2)
                with v.Fori(0, TT // 2) as i:
                    t = i * 2
                    root.enter(i, 8)
                    for j in range(2):
                        v.wait_ge(squared, t + (j + 1))
                        nc.vector.tensor_scalar(st[j][:, 1:2], st[j][:, 0:1], 1.0 / D, EPS, ALU.mult, ALU.add).then_inc(mean_ready, 1)
                        v.wait_ge(root_ready, t + (j + 1))
                        rsqrt_steps(nc, L, st[j][:, 1:2], st[j][:, 2:3], st[j][:, 3:4], st[j][:, 4:5])
                        nc.vector.tensor_scalar(xt[j][:], xt[j][:], st[j][:, 3:4], None, ALU.mult).then_inc(scaled, 1)
                        v.wait_ge(evacuated, t + (j + 1))
                        at = bass.ds((t + j) * P, P)
                        nc.vector.tensor_copy(m.hT[:, 0, :, at], xf[j][:]).then_inc(hi_done, 1)
                        v.wait_ge(hi_done, t + (j + 1))
                        nc.vector.tensor_tensor(m.hT[:, 1, :, at], xf[j][:], m.hT[:, 0, :, at].bitcast(F32), ALU.subtract).then_inc(split, 1)
                root.leave(TT // 2)

            @block.tensor
            def _(pe):
                with pe.Fori(0, TT // 2) as i:
                    t = i * 2
                    for j in range(2):
                        pe.wait_ge(scaled, t + (j + 1))
                        pe.wait_ge(split, t + (j + 1))
                        for c in range(KC):
                            tr = nc.tensor.transpose(ps[j][:, c, :], xt[j][:, c * P:(c + 1) * P], m.ident[:])
                        tr.then_inc(turned, 1)


def split_weights_hi(nc, act, raw, w):
    return nc.scalar.copy(w[:, 0], raw[:])


def split_weights_lo(nc, raw, w):
    return nc.vector.tensor_tensor(w[:, 1], raw[:], w[:, 0].bitcast(F32), ALU.subtract)


def split_product(nc, out, w, x, n=KC):
    for k in range(n):
        nc.tensor.matmul(out, w(0, k), x(0, k), start=(k == 0), stop=False)
        nc.tensor.matmul(out, w(0, k), x(1, k), start=False, stop=False)
        last = nc.tensor.matmul(out, w(1, k), x(0, k), start=False, stop=(k == n - 1))
    return last


def project(m, a):
    nc = m.nc
    with ExitStack() as ctx:
        sb = lambda n, s, d=F32: ctx.enter_context(nc.sbuf_tensor(n, s, d))
        raw = sb("w_raw", [P, KC, P])
        whl = [sb(f"w_hl{j}", [P, 2, KC, P], F32R) for j in range(3)]
        stage = [sb(f"stage{j}", [P, BT]) for j in range(2)]
        mb = [sb(f"m_blk{j}", [P, 3 + BT]) for j in range(2)]
        acc = sb("conv_acc", [P, BT])
        xst = [sb(f"xc_blk{j}", [P, BT]) for j in range(2)]
        wif = sb("w_if_tile", [P, 2, 2 * MH])
        cvec = sb("conv_vec", [P, 5])
        us = [sb(f"s5_u{j}", [P, NCH]) for j in range(2)]
        wt = [sb(f"s5_wt{j}", [P, BW]) for j in range(2)]
        cosk = [sb(f"s5_cos{j}", [P, NCH]) for j in range(2)]
        sink = [sb(f"s5_sin{j}", [P, NCH]) for j in range(2)]
        pt = [sb(f"s5_pt{j}", [P, NCH]) for j in range(2)]
        wa, wb = sb("s5_wa", [P, NCH]), sb("s5_wb", [P, NCH])
        zz = sb("s5_z", [P, NCH + 1])
        cz = [sb(f"s5_cz{j}", [P, 2, NCH]) for j in range(2)]
        yo = [sb(f"s5_yo{j}", [P, NCH]) for j in range(2)]
        pg = [ctx.enter_context(nc.psum_tensor(f"pg{j}", [P, BT], F32)) for j in range(3)]
        pv = [ctx.enter_context(nc.psum_tensor(f"pv{j}", [P, 2, NCH], F32)) for j in range(2)]
        py = [ctx.enter_context(nc.psum_tensor(f"py{j}", [P, 512], F32)) for j in range(2)]
        pgate = ctx.enter_context(nc.psum_tensor("pgate", [P, BT], F32))
        pg1 = [p[:] for p in pg] + [pv[0][:].rearrange("p a b -> p (a b)")]

        w1_in, w1_hi, w1_lo = m.sem("p1_w_in"), m.sem("p1_w_hi"), m.sem("p1_w_lo")
        u_done, u_read = m.sem("p1_done"), m.sem("p1_read")
        u_out = [m.sem(f"p1_out{j}") for j in range(2)]
        w_in, w_hi, w_lo = m.sem("p2_w_in"), m.sem("p2_w_hi"), m.sem("p2_w_lo")
        gemm_done = m.sem("p2_done")
        bank_free = [m.sem(f"p2_bank_free{j}") for j in range(3)]
        st_out = [m.sem(f"p2_stage_out{j}") for j in range(2)]
        st_ready = m.sem("p2_stage_ready")
        conv = m.sem("p2_conv")
        conv_free = m.sem("p2_conv_free")
        m_out = [m.sem(f"p2_m_out{j}") for j in range(2)]
        xc_out = [m.sem(f"p2_xc_out{j}") for j in range(2)]
        wif_in = m.sem("p2_wif_in")
        gate_done, gate_added = m.sem("p2_gate_done"), m.sem("p2_gate_added")
        s5_in = [m.sem(f"s5_in{j}") for j in range(2)]
        v_done, y_done = m.sem("s5_v_done"), m.sem("s5_y_done")
        table = Tally(m.sem("s5_table"))
        step = Tally(m.sem("p2_step"))
        z_turned = m.sem("s5_z_turned")
        v_read = m.sem("s5_v_read")
        y_read = m.sem("s5_y_read")
        y_out = [m.sem(f"s5_y_out{j}") for j in range(2)]

        w_cols = a["ev_w_in"][0].rearrange("(k p) n -> p k n", p=P)
        plan = []
        for n in range(12):
            groups = [s for s in range(8) if 3 * s // 2 == n]
            plan += [("in", s) for s in groups] + [("gemm", n)]
            if 5 <= n <= 8:
                plan.append(("gate", n - 5))
            plan += [("out", s) for s in groups]

        def u_rows(dram, i, s):
            return dram.rearrange("(g p) b j k -> g p b j k", p=GP)[i * 8 + s].rearrange("p b j k -> j p b k")

        def perm(ap):
            return ap.rearrange("p (k j) -> p j k", j=CH)

        with nc.Block() as block:
            @block.sync
            def _(sp):
                sp.sem_inc(w1_lo, 1)
                with sp.Fori(0, KC) as n:
                    sp.wait_ge(w1_lo, n + 1)
                    sp.dma_start(raw[:], w_cols[:, :, bass.ds(n * P, P)]).then_inc(w1_in, 16)
                sp.wait_ge(w1_lo, KC + 1)
                sp.dma_start(raw[:], w_cols[:, :, D:D + P]).then_inc(w_in, 16)
                for j in range(2):
                    sp.wait_ge(u_out[j], 16 * (2 * KC + 1))
                with sp.Fori(0, KC) as i:
                    sp.wait_ge(gate_done, i * 4 + 2)
                    w2 = a["m_w_if"][0].rearrange("(h k p) n -> k p h n", h=2, p=P)
                    sp.dma_start(wif[:], w2[i]).then_inc(wif_in, 16)
                    for what, n in plan:
                        if what == "in":
                            sp.wait_ge(y_done, i * 8 + (n + 1))
                            q = n % 2
                            sp.dma_start(us[q][:].rearrange("r (b k) -> r b k", b=NB), u_rows(m.u_d, i, n)).then_inc(s5_in[q], 16)
                            sp.dma_start(wt[q][:], m.s5w_d[i * 8 + n]).then_inc(s5_in[q], 16)
                        if what == "gemm" and n % 4 == 0:
                            sp.wait_ge(w_lo, i * 3 + (n // 4 + 1))
                            col = i * P + (2 * D, 3 * D, D + P)[n // 4]
                            sp.dma_start(raw[:], w_cols[:, :, bass.ds(col, P)]).then_inc(w_in, 16)
                sp.wait_ge(w_in, 16 * (3 * KC + 1))

            @block.scalar
            def _(act):
                for j in range(2):
                    act.sem_inc(u_out[j], 16)
                    act.sem_inc(st_out[j], 16)
                    act.sem_inc(m_out[j], 16)
                    act.sem_inc(xc_out[j], 16)
                    act.sem_inc(y_out[j], 16)
                with act.Fori(0, KC // 2) as i:
                    for j in range(2):
                        act.wait_ge(w1_in, i * 32 + 16 * (j + 1))
                        act.wait_ge(u_done, i * 8 + 4 * (j + 1))
                        split_weights_hi(nc, act, raw, whl[j]).then_inc(w1_hi, 1)
                        for b in range(NB):
                            act.wait_ge(u_done, i * 8 + (4 * j + b + 1 + 8))
                            act.wait_ge(u_out[b % 2], i * 64 + 16 * (2 * j + b // 2 + 1))
                            nc.scalar.copy(stage[b % 2][:].rearrange("p (j k) -> p j k", j=CH), perm(pg1[b])).then_inc(u_read, 1)
                            act.wait_ge(u_read, i * 8 + (4 * j + b + 1 + 4))
                            act.dma_start(m.u_d.rearrange("(t p) b j k -> t p b (j k)", p=P)[i * 2 + j, :, b],
                                          stage[b % 2][:]).then_inc(u_out[b % 2], 16)
                act.wait_ge(w_in, 16)
                act.wait_ge(u_done, 8 + 28)
                split_weights_hi(nc, act, raw, whl[0]).then_inc(w_hi, 1)
                for j in range(2):
                    act.wait_ge(u_out[j], 16 * (2 * KC + 1))
                act.wait_ge(u_done, 8 + 32)
                with act.Fori(0, KC) as i:
                    for what, n in plan:
                        if what == "gemm":
                            sec, b = n // 4, n % 4
                            if b == 0:
                                act.wait_ge(w_in, i * 48 + 16 * (sec + 2))
                                act.wait_ge(gemm_done, i * 12 + (8, 12, 16)[sec])
                                split_weights_hi(nc, act, raw, whl[(sec + 1) % 3]).then_inc(w_hi, 1)
                            if sec == 1:
                                act.wait_ge(conv, i * 4 + (b + 2))
                                act.wait_ge(xc_out[b % 2], i * 32 + 16 * (b // 2 + 1))
                                act.wait_ge(gate_done, i * 4 + (b + 1))
                                nc.scalar.activation(xst[b % 2][:], acc[:], ACT.Silu).then_inc(conv_free, 1)
                                act.dma_start(m.m_d.rearrange("(t p) (b n) -> t p b n", p=P, b=NB)[i, :, b],
                                              mb[b % 2][:, 3:3 + BT]).then_inc(m_out[b % 2], 16)
                                act.wait_ge(conv_free, i * 4 + (b + 2))
                                act.dma_start(m.xc_d.rearrange("(t p) (b n) -> t p b n", p=P, b=NB)[i, :, b],
                                              xst[b % 2][:]).then_inc(xc_out[b % 2], 16)
                            else:
                                act.wait_ge(gemm_done, i * 12 + (n + 1 + 12))
                                at = 0 if sec == 0 else 2
                                act.wait_ge(st_out[b % 2], i * 64 + 16 * (at + b // 2 + 1))
                                if sec == 0:
                                    ins = nc.scalar.activation(stage[b % 2][:].rearrange("p (j k) -> p j k", j=CH),
                                                               perm(pg[n % 3][:]), ACT.Silu)
                                    dst = m.sz_d.rearrange("(t p) b j k -> t p b (j k)", p=P)[i, :, b]
                                else:
                                    ins = nc.scalar.activation(stage[b % 2][:], pg[n % 3][:], ACT.Silu)
                                    dst = m.smz_d.rearrange("(t p) (b n) -> t p b n", p=P, b=NB)[i, :, b]
                                ins.then_inc(bank_free[n % 3], 1)
                                act.wait_ge(bank_free[n % 3], i * 4 + (n // 3 + 2))
                                act.dma_start(dst, stage[b % 2][:]).then_inc(st_out[b % 2], 16)
                        if what == "out":
                            q = n % 2
                            act.wait_ge(y_done, i * 8 + (n + 1 + 2))
                            act.wait_ge(y_out[q], i * 64 + 16 * (n // 2 + 1))
                            nc.scalar.copy(yo[q][:], py[q][:, 0:NCH]).then_inc(y_read, 1)
                            act.wait_ge(y_read, i * 8 + (n + 3))
                            act.dma_start(u_rows(m.y_d, i, n), yo[q][:].rearrange("r (b k) -> r b k", b=NB)).then_inc(y_out[q], 16)
                for j in range(2):
                    act.wait_ge(st_out[j], 16 * (4 * KC + 1))
                    act.wait_ge(m_out[j], 16 * (2 * KC + 1))
                    act.wait_ge(xc_out[j], 16 * (2 * KC + 1))
                    act.wait_ge(y_out[j], 16 * (4 * KC + 1))

            @block.gpsimd
            def _(pool):
                nc.gpsimd.memset(m.gacc[:], 0.0).then_inc(gate_added, 1)
                pool.sem_inc(z_turned, 2)
                with pool.Fori(0, KC) as i:
                    table.enter(i, 6 * 8)
                    for s in range(8):
                        q = s % 2
                        pool.wait_ge(s5_in[q], i * 128 + 32 * (s // 2 + 1))
                        pool.wait_ge(z_turned, i * 8 + (s + 1))
                        v3 = lambda ap: ap.rearrange("p (x y) -> p x y", y=16)
                        lo = lambda c: wt[q][:, c:c + 16].unsqueeze(1).broadcast_to([P, 16, 16])
                        hi = lambda c: wt[q][:, c:c + 16].unsqueeze(2).broadcast_to([P, 16, 16])
                        for dst, t0, t1, op in ((cosk[q], (EAC, EBC), (EAS, EBS), ALU.subtract),
                                                (sink[q], (EAS, EBC), (EAC, EBS), ALU.add)):
                            table.add(nc.gpsimd.tensor_tensor(v3(pt[0][:]), hi(t0[0]), lo(t0[1]), ALU.mult))
                            done = table.add(nc.gpsimd.tensor_tensor(v3(pt[1][:]), hi(t1[0]), lo(t1[1]), ALU.mult))
                            pool.wait_ge(table.sem, done)
                            done = table.add(nc.gpsimd.tensor_tensor(dst[:], pt[0][:], pt[1][:], op))
                            pool.wait_ge(table.sem, done)
                table.leave(KC)

            @block.vector
            def _(v):
                tt, stt, ts = nc.vector.tensor_tensor, nc.vector.scalar_tensor_tensor, nc.vector.tensor_scalar

                def L(ins):
                    v.wait_ge(step.sem, step.add(ins))

                L(nc.vector.memset(zz[:, 0:1], 0.0))
                v.sem_inc(conv_free, 1)
                v.sem_inc(conv, 1)
                v.sem_inc(y_read, 2)
                v.sem_inc(v_read, 2)
                for j in range(3):
                    v.sem_inc(bank_free[j], 1)
                with v.Fori(0, KC // 2) as i:
                    for j in range(2):
                        v.wait_ge(w1_hi, i * 2 + (j + 1))
                        split_weights_lo(nc, raw, whl[j]).then_inc(w1_lo, 1)
                v.wait_ge(w_hi, 1)
                split_weights_lo(nc, raw, whl[0]).then_inc(w_lo, 1)
                with v.Fori(0, KC) as i:
                    step.enter(i, 1 + 4 * 4 + 8 * 4)
                    v.wait_ge(conv, i * 4 + 1)
                    L(nc.vector.tensor_copy(cvec[:], m.cols[:, ROWS["conv_w"]:ROWS["conv_w"] + 40]
                                            .rearrange("p (t j) -> p j t", j=KC)[:, i]))
                    for what, n in plan:
                        if what == "gemm":
                            sec, b = n // 4, n % 4
                            if b == 0:
                                v.wait_ge(w_hi, i * 3 + (sec + 2))
                                split_weights_lo(nc, raw, whl[(sec + 1) % 3]).then_inc(w_lo, 1)
                            if sec == 1:
                                cur = mb[b % 2]
                                v.wait_ge(gemm_done, i * 12 + (n + 1 + 12))
                                v.wait_ge(m_out[b % 2], i * 32 + 16 * (b // 2 + 1))
                                v.wait_ge(gate_done, i * 4 + (b + 1))
                                if b == 0:
                                    step.add(nc.vector.memset(cur[:, 0:3], 0.0))
                                else:
                                    step.add(nc.vector.tensor_copy(cur[:, 0:3], mb[(b + 1) % 2][:, BT:BT + 3]))
                                nc.vector.tensor_copy(cur[:, 3:3 + BT], pg[n % 3][:]).then_inc(bank_free[n % 3], 1)
                                v.wait_ge(bank_free[n % 3], i * 4 + (n // 3 + 2))
                                v.wait_ge(step.sem, step.mark())
                                v.wait_ge(conv_free, i * 4 + (b + 1))
                                L(ts(acc[:], cur[:, 0:BT], cvec[:, 0:1], cvec[:, 4:5], ALU.mult, ALU.add))
                                L(stt(out=acc[:], in0=cur[:, 1:1 + BT], scalar=cvec[:, 1:2], in1=acc[:], op0=ALU.mult, op1=ALU.add))
                                L(stt(out=acc[:], in0=cur[:, 2:2 + BT], scalar=cvec[:, 2:3], in1=acc[:], op0=ALU.mult, op1=ALU.add))
                                stt(out=acc[:], in0=cur[:, 3:3 + BT], scalar=cvec[:, 3:4], in1=acc[:],
                                    op0=ALU.mult, op1=ALU.add).then_inc(conv, 1)
                        if what == "gate":
                            v.wait_ge(gate_done, i * 4 + (n + 1 + 2))
                            v.wait_ge(gate_added, i * 4 + (n + 1))
                            tt(m.gacc[:, n * BT:(n + 1) * BT], pgate[0:2 * MH, :], m.gacc[:, n * BT:(n + 1) * BT],
                               ALU.add).then_inc(gate_added, 1)
                        if what == "in":
                            q = n % 2
                            v.wait_ge(v_done, i * 8 + (n + 1))
                            v.wait_ge(table.sem, i * 48 + 6 * (n + 1))
                            step.add(tt(wa[:], pv[q][:, 0, :], cosk[q][:], ALU.mult))
                            tt(wb[:], pv[q][:, 1, :], sink[q][:], ALU.mult).then_inc(v_read, 1)
                            v.wait_ge(v_read, i * 8 + (n + 3))
                            L(tt(wa[:], wa[:], wb[:], ALU.add))
                            L(nc.vector.tensor_tensor_scan(zz[:, 1:1 + NCH], wt[q][:, RAD:RAD + 1].broadcast_to([P, NCH]), wa[:],
                                                           0.0, ALU.mult, ALU.add))
                            v.wait_ge(y_done, i * 8 + (n + 1))
                            step.add(tt(cz[q][:, 0, :], zz[:, 0:NCH], cosk[q][:], ALU.mult))
                            tt(cz[q][:, 1, :], zz[:, 0:NCH], sink[q][:], ALU.mult).then_inc(z_turned, 1)
                            v.wait_ge(z_turned, i * 8 + (n + 3))
                step.leave(KC)

            @block.tensor
            def _(pe):
                pe.sem_inc(u_done, 8)
                pe.sem_inc(u_read, 4)
                pe.sem_inc(gemm_done, 12)
                pe.sem_inc(gate_done, 2)
                pe.sem_inc(y_done, 2)
                xs = lambda b: (lambda part, k: m.hT[:, part, k, b * BT:(b + 1) * BT])
                ws = lambda w: (lambda part, k: w[:, part, k, :])
                with pe.Fori(0, KC // 2) as i:
                    for j in range(2):
                        pe.wait_ge(w1_lo, i * 2 + (j + 2))
                        for b in range(NB):
                            pe.wait_ge(u_read, i * 8 + (4 * j + b + 1))
                            split_product(nc, pg1[b], ws(whl[j]), xs(b)).then_inc(u_done, 1)
                pe.wait_ge(u_read, 4 * KC + 4)
                with pe.Fori(0, KC) as i:
                    for what, n in plan:
                        q = n % 2
                        if what == "gemm":
                            sec, b = n // 4, n % 4
                            if b == 0:
                                pe.wait_ge(w_lo, i * 3 + (sec + 1))
                            pe.wait_ge(bank_free[n % 3], i * 4 + (n // 3 + 1))
                            split_product(nc, pg[n % 3][:], ws(whl[sec]), xs(b)).then_inc(gemm_done, 1)
                        if what == "gate":
                            if n == 0:
                                pe.wait_ge(wif_in, i * 16 + 16)
                            pe.wait_ge(conv_free, i * 4 + (n + 2))
                            pe.wait_ge(gate_added, i * 4 + (n + 1))
                            nc.tensor.matmul(pgate[0:2 * MH, :], wif[:, 0, :], xst[q][:], start=True, stop=False)
                            nc.tensor.matmul(pgate[0:2 * MH, :], wif[:, 1, :], mb[q][:, 3:3 + BT], start=False,
                                             stop=True).then_inc(gate_done, 1)
                        if what == "in":
                            pe.wait_ge(s5_in[q], i * 128 + 32 * (n // 2 + 1))
                            pe.wait_ge(v_read, i * 8 + (n + 1))
                            nc.tensor.matmul(pv[q][:, 0, :], wt[q][:, BIN:BIN + P], us[q][:], start=True, stop=True)
                            nc.tensor.matmul(pv[q][:, 1, :], wt[q][:, BIS:BIS + P], us[q][:], start=True, stop=True).then_inc(v_done, 1)
                        if what == "out":
                            pe.wait_ge(y_read, i * 8 + (n + 1))
                            nc.tensor.matmul(py[q][:, 0:NCH], wt[q][:, TOE:TOE + P], us[q][:], start=True, stop=False)
                            pe.wait_ge(z_turned, i * 8 + (n + 3))
                            nc.tensor.matmul(py[q][:, 0:NCH], wt[q][:, COC:COC + P], cz[q][:, 0, :], start=False, stop=False)
                            nc.tensor.matmul(py[q][:, 0:NCH], wt[q][:, COS:COS + P], cz[q][:, 1, :], start=False,
                                             stop=True).then_inc(y_done, 1)


def glu(m, a):
    nc = m.nc
    with ExitStack() as ctx:
        sb = lambda n, s, d=F32: ctx.enter_context(nc.sbuf_tensor(n, s, d))
        raw = [sb(f"g_raw{j}", [P, KC, P]) for j in range(2)]
        wg = sb("g_w", [P, 2, KC, D], F32R)
        yt, ut, zt = sb("g_y", [P, KC, BT]), sb("g_u", [P, KC, BT]), sb("g_z", [P, KC, BT])
        gt = sb("g_g", [P, KC, BT])
        gh = sb("g_gh", [P, 2, KC, BT], F32R)
        sg = [sb(f"g_s{j}", [P, BT]) for j in range(2)]
        ot = [sb(f"g_o{j}", [P, BT]) for j in range(2)]
        ps = [ctx.enter_context(nc.psum_tensor(f"g_ps{j}", [P, BT], F32)) for j in range(4)]
        w_in = [m.sem(f"g_w_in{j}") for j in range(2)]
        w_hi, w_lo = m.sem("g_w_hi"), m.sem("g_w_lo")
        y_in, z_in = m.sem("g_y_in"), m.sem("g_z_in")
        pre, gel, hi, lo = m.sem("g_pre"), m.sem("g_gelu"), m.sem("g_hi"), m.sem("g_lo")
        done, sig, gated, stored = m.sem("g_done"), m.sem("g_sigmoid"), m.sem("g_gated"), m.sem("g_final")
        out = [m.sem(f"g_out{j}") for j in range(2)]
        wv = a["s5_w_glu"][0].rearrange("(k p) n -> p k n", p=P)
        tiled = lambda d_: d_.rearrange("(k p) b j c -> b p k (j c)", p=P)
        with nc.Block() as block:
            @block.sync
            def _(sp):
                sp.sem_inc(w_lo, 2)
                with sp.Fori(0, KC // 2) as i:
                    for j in range(2):
                        sp.wait_ge(w_lo, i * 2 + (j + 1))
                        sp.dma_start(raw[j][:], wv[:, :, bass.ds(i * (2 * P) + j * P, P)]).then_inc(w_in[j], 16)
                sp.sem_inc(gel, KC)
                sp.sem_inc(stored, KC)
                with sp.Fori(0, NB) as b:
                    sp.wait_ge(gel, b * KC + KC)
                    sp.dma_start(yt[:], tiled(m.y_d)[b]).then_inc(y_in, 16)
                    sp.dma_start(ut[:], tiled(m.u_d)[b]).then_inc(y_in, 16)
                    sp.wait_ge(stored, b * KC + KC)
                    sp.dma_start(zt[:], tiled(m.sz_d)[b]).then_inc(z_in, 16)

            @block.scalar
            def _(act):
                yd = m.ys_d.rearrange("(k p) (b t) -> k p b t", p=P, b=NB)

                def store(act, b, n):
                    act.wait_ge(stored, b * KC + (KC + n + 1))
                    act.dma_start(yd[n, :, b], ot[n % 2][:]).then_inc(out[n % 2], 16)

                with act.Fori(0, KC // 2) as i:
                    for j in range(2):
                        act.wait_ge(w_in[j], i * 16 + 16)
                        nc.scalar.copy(wg[:, 0, :, bass.ds(i * (2 * P) + j * P, P)], raw[j][:]).then_inc(w_hi, 1)
                with act.Fori(0, NB) as b:
                    act.wait_ge(stored, b * KC + KC)
                    for n in range(KC):
                        act.wait_ge(pre, b * KC + (n + 1))
                        nc.scalar.activation(gt[:, n], yt[:, n], ACT.Gelu_apprx_tanh).then_inc(gel, 1)
                    for n in range(KC):
                        act.wait_ge(done, b * KC + (n + 1 + 4))
                        act.wait_ge(gated, b * KC + (n + 1))
                        nc.scalar.activation(sg[n % 2][:], ps[n % 4][:], ACT.Sigmoid).then_inc(sig, 1)
                        if n > 0:
                            store(act, b, n - 1)
                    store(act, b, KC - 1)
                for j in range(2):
                    act.wait_ge(out[j], 16 * (KC // 2 * NB + 1))

            @block.vector
            def _(v):
                tt, stt = nc.vector.tensor_tensor, nc.vector.scalar_tensor_tensor
                v.sem_inc(gated, 2)
                for j in range(2):
                    v.sem_inc(out[j], 16)
                with v.Fori(0, KC // 2) as i:
                    for j in range(2):
                        v.wait_ge(w_hi, i * 2 + (j + 1))
                        at = bass.ds(i * (2 * P) + j * P, P)
                        tt(wg[:, 1, :, at], raw[j][:], wg[:, 0, :, at].bitcast(F32), ALU.subtract).then_inc(w_lo, 1)
                with v.Fori(0, NB) as b:
                    v.wait_ge(y_in, b * 32 + 32)
                    for n in range(KC):
                        stt(out=yt[:, n], in0=ut[:, n], scalar=m.cols[:, ROWS["s5_d"] + n:ROWS["s5_d"] + n + 1],
                            in1=yt[:, n], op0=ALU.mult, op1=ALU.add).then_inc(pre, 1)
                    v.wait_ge(done, b * KC + 4)
                    for n in range(KC):
                        v.wait_ge(gel, b * KC + (KC + n + 1))
                        nc.vector.tensor_copy(gh[:, 0, n], gt[:, n]).then_inc(hi, 1)
                        v.wait_ge(hi, b * KC + (n + 1))
                        tt(gh[:, 1, n], gt[:, n], gh[:, 0, n].bitcast(F32), ALU.subtract).then_inc(lo, 1)
                    v.wait_ge(z_in, b * 16 + 16)
                    for n in range(KC):
                        v.wait_ge(sig, b * KC + (n + 1 + 4))
                        tt(sg[n % 2][:], sg[n % 2][:], gt[:, n], ALU.mult).then_inc(gated, 1)
                        v.wait_ge(gated, b * KC + (n + 3))
                        v.wait_ge(out[n % 2], b * (16 * KC // 2) + 16 * (n // 2 + 1))
                        tt(ot[n % 2][:].rearrange("p (k j) -> p j k", j=CH), sg[n % 2][:].rearrange("p (j k) -> p j k", j=CH),
                           zt[:, n].rearrange("p (j k) -> p j k", j=CH), ALU.mult).then_inc(stored, 1)

            @block.tensor
            def _(pe):
                pe.sem_inc(done, 4)
                pe.sem_inc(sig, 4)
                pe.wait_ge(w_lo, KC + 2)
                with pe.Fori(0, NB) as b:
                    pe.wait_ge(lo, b * KC + KC)
                    for n in range(KC):
                        pe.wait_ge(sig, b * KC + (n + 1))
                        split_product(nc, ps[n % 4][:], lambda part, k: wg[:, part, k, n * P:(n + 1) * P],
                                      lambda part, k: gh[:, part, k, :]).then_inc(done, 1)


def gates(m, a):
    nc = m.nc
    R = MH * NMC
    with ExitStack() as ctx:
        sb = lambda n, s, d=F32: ctx.enter_context(nc.sbuf_tensor(n, s, d))
        bias = sb("t_bias", [2 * MH, 1])
        li, fr = sb("t_li", [R, MC]), sb("t_fr", [R, MC])
        w = [sb(f"t_w{j}", [R, MC]) for j in range(4)]
        whole = sb("t_whole", [R, MC], I32)
        ones = sb("t_ones", [R, MC])
        zeros = sb("t_zeros", [R, MC])
        run = sb("t_run", [R, MC])
        q = sb("t_q", [R, 4, MC])
        ends = sb("t_ends", [R, 2])
        er = sb("t_er", [MH, 2, NMC])
        mrow = sb("t_mrow", [MH, NMC + 1])
        mcol = sb("t_mcol", [R, 2])
        ps = ctx.enter_context(nc.psum_tensor("t_ps", [P, 4, R], F32))
        bias_in, logits = m.sem("t_bias_in"), m.sem("t_logits")
        moved = m.sem("t_moved")
        step = Tally(m.sem("t_step"))
        exp_in, exp_out = m.sem("t_exp_in"), m.sem("t_exp_out")
        ends_ready, m_ready, q_ready, turned = (m.sem(f"t_{n}") for n in ("ends", "m", "q", "turned"))
        with nc.Block() as block:
            @block.sync
            def _(sp):
                sp.dma_start(bias[:], a["m_b_if"].rearrange("o n -> n o"), allow_slow_non_contiguous=True).then_inc(bias_in, 16)
                sp.wait_ge(logits, 1)
                sp.dma_start(m.gt_d, m.gacc[:]).then_inc(moved, 16)
                sp.wait_ge(moved, 16)
                rows = m.gt_d.rearrange("n (c t) -> (n c) t", t=MC)
                sp.dma_start(li[:], rows[0:R]).then_inc(moved, 16)
                sp.dma_start(fr[:], rows[R:2 * R]).then_inc(moved, 16)
                sp.wait_ge(ends_ready, 1)
                sp.dma_start(m.mx_d[0:2].rearrange("k r -> r k"), ends[:], allow_slow_non_contiguous=True).then_inc(moved, 16)
                sp.wait_ge(moved, 64)
                sp.dma_start(er[:], m.mx_d[0:2].rearrange("k (h c) -> h k c", h=MH), allow_slow_non_contiguous=True).then_inc(moved, 16)
                sp.wait_ge(m_ready, 1)
                sp.dma_start(m.mx_d[2:3].rearrange("k (h c) -> (k h) c", h=MH), mrow[:, 0:NMC]).then_inc(moved, 16)
                sp.wait_ge(moved, 96)
                sp.dma_start(mcol[:, 0:1], m.mx_d[2:3].rearrange("k r -> r k"), allow_slow_non_contiguous=True).then_inc(moved, 16)
                sp.wait_ge(q_ready, 1)
                sp.dma_start(m.gb_d, run[:]).then_inc(moved, 16)
                sp.dma_start(m.mx_d[3:4].rearrange("k r -> r k"), mcol[:, 1:2], allow_slow_non_contiguous=True).then_inc(moved, 16)
                sp.wait_ge(moved, 144)
                sp.dma_start(m.decay[:].rearrange("p h c -> p (h c)"), m.mx_d[3:4].broadcast_to([P, R])).then_inc(moved, 16)
                sp.wait_ge(moved, 160)

            @block.vector
            def _(v):
                def L(ins):
                    v.wait_ge(step.sem, step.add(ins))

                tt, stt, ts = nc.vector.tensor_tensor, nc.vector.scalar_tensor_tensor, nc.vector.tensor_scalar
                v.wait_ge(bias_in, 16)
                ts(m.gacc[:], m.gacc[:], bias[:, 0:1], None, ALU.add).then_inc(logits, 1)
                L(nc.vector.memset(ones[:], 1.0))
                L(nc.vector.memset(zeros[:], 0.0))
                L(nc.vector.memset(mrow[:], 0.0))
                v.wait_ge(moved, 48)
                L(stt(out=w[0][:], in0=fr[:], scalar=-1.0, in1=fr[:], op0=ALU.mult, op1=ALU.min))
                exp_steps(nc, L, w[1][:], w[0][:], w[2][:], w[3][:], whole[:])
                L(ts(w[0][:], w[1][:], 2.0, None, ALU.add))
                L(nc.vector.reciprocal(w[2][:], w[0][:]))
                L(tt(w[0][:], w[1][:], w[2][:], ALU.mult))
                L(tt(w[1][:], w[0][:], w[0][:], ALU.mult))
                L(ts(w[2][:], w[1][:], 1.0 / 17, None, ALU.mult))
                for k in range(15, 1, -2):
                    L(stt(out=w[2][:], in0=w[2][:], scalar=1.0 / k, in1=w[1][:], op0=ALU.add, op1=ALU.mult))
                L(stt(out=w[2][:], in0=w[2][:], scalar=1.0, in1=w[0][:], op0=ALU.add, op1=ALU.mult))
                L(ts(w[0][:], fr[:], 0.0, None, ALU.min))
                L(stt(out=w[0][:], in0=w[2][:], scalar=-2.0, in1=w[0][:], op0=ALU.mult, op1=ALU.add))
                L(nc.vector.tensor_tensor_scan(w[1][:], ones[:], w[0][:], 0.0, ALU.mult, ALU.add))
                L(tt(q[:, 0, :], li[:], w[1][:], ALU.subtract))
                L(nc.vector.tensor_tensor_scan(run[:], q[:, 0, :], zeros[:], -3.0e38, ALU.max, ALU.add))
                L(nc.vector.tensor_copy(ends[:, 0:1], run[:, MC - 1:MC]))
                nc.vector.tensor_copy(ends[:, 1:2], w[1][:, MC - 1:MC]).then_inc(ends_ready, 1)
                v.wait_ge(moved, 80)
                nc.vector.tensor_tensor_scan(mrow[:, 1:NMC + 1], er[:, 0, :], er[:, 1, :], 0.0, ALU.max, ALU.add).then_inc(m_ready, 1)
                v.wait_ge(moved, 112)
                L(ts(run[:], run[:], mcol[:, 0:1], None, ALU.max))
                L(ts(q[:, 1, :], run[:], mcol[:, 0:1], -1.0, ALU.subtract, ALU.mult))
                L(ts(q[:, 2, :], q[:, 0, :], run[:, MC - 1:MC], None, ALU.subtract))
                L(tt(q[:, 3, :], run[:], w[1][:], ALU.add))
                ts(q[:, 3, :], q[:, 3, :], -1.0, None, ALU.mult).then_inc(exp_in, 1)
                v.wait_ge(turned, 1)
                nc.vector.tensor_copy(m.gcol[:], ps[:].rearrange("p q (h c) -> p c q h", h=MH)).then_inc(exp_in, 1)
                v.wait_ge(exp_in, 2)

            @block.scalar
            def _(act):
                act.wait_ge(exp_in, 1)
                nc.scalar.activation(q[:, 1:4, :], q[:, 1:4, :], ACT.Exp).then_inc(exp_out, 1)
                act.wait_ge(exp_out, 1)
                nc.scalar.copy(mcol[:, 1:2], q[:, 1, MC - 1:MC]).then_inc(q_ready, 1)

            @block.tensor
            def _(pe):
                pe.wait_ge(exp_out, 1)
                for j in range(4):
                    tr = nc.tensor.transpose(ps[:, j, :], q[:, j, :], m.ident[0:R, 0:R])
                tr.then_inc(turned, 1)


def mlstm(m, a):
    nc = m.nc
    HW = HD + 1
    with ExitStack() as ctx:
        sb = lambda n, s, d=F32: ctx.enter_context(nc.sbuf_tensor(n, s, d))
        wq, wk = sb("x_wq", [P, 2 * MH, HD]), sb("x_wk", [P, 2 * MH, HD])
        wvo = sb("x_wvo", [P, 2 * MH, 2, HD])
        wo = sb("x_wout", [P, 2 * KC, D])
        mt, xt, zt, yst = (sb(f"x_{n}", [P, KC, MC]) for n in ("m", "xc", "mz", "ys"))
        xr = sb("x_x", [P, D])
        gb = sb("x_gb", [P, MH, MC])
        gates0 = sb("x_gate", [P, D])
        mask = sb("x_mask", [P, MC])
        cc = sb("x_cols", [P, 4, MH])
        dec = sb("x_dec", [P, MH])
        qt = sb("x_qt", [P, 2, 2, MC])
        kt = sb("x_kt", [P, 2, 2, MC])
        kw = [sb(f"x_kw{j}", [P, HD]) for j in range(2)]
        ve = [sb(f"x_ve{j}", [P, HW]) for j in range(2)]
        og = sb("x_og", [P, MH, HD])
        pm = sb("x_pm", [P, MH, MC])
        st = [sb(f"x_st{j}", [P, MC]) for j in range(2)]
        cst = sb("x_c", [P, MH, 2, HW])
        bs = [sb(f"x_bs{j}", [P, HW]) for j in range(2)]
        ha = sb("x_ha", [P, MH, HW])
        hs = sb("x_hs", [P, MH, HD])
        sm = sb("x_small", [P, 6, MH])
        xs = sb("x_skip", [P, KC, MC])
        ym = sb("x_ym", [P, KC, MC])
        ho = sb("x_out", [P, D])
        pb = [ctx.enter_context(nc.psum_tensor(f"x_ps{j}", [P, 512], F32)) for j in range(8)]
        QK, KT, VO, SS, AA, BB, C0, C1 = pb
        w_in = m.sem("x_w_in")
        made = m.sem("x_made")
        in_mx, in_gb, in_zy, in_x = m.sem("x_in_mx"), m.sem("x_in_gb"), m.sem("x_in_zy"), m.sem("x_in_x")
        (qk_done, kt_done, vo_done, s_done, a_done, b_done, c_done, y_turned, o_done) = (
            m.sem(f"x_{n}") for n in ("qk_done", "kt_done", "vo_done", "s_done", "a_done", "b_done", "c_done",
                                      "y_turned", "o_done"))
        (qk_read, kw_ready, ve_ready, pm_ready, st_ready, bs_ready, ha_ready, c_ready, h_ready, y_read, y_ready,
         h1_ready, masked, skipped, cols_ready, o_ready, sq_ready, root_ready, var_ready) = (
            m.sem(f"x_{n}") for n in ("qk_read", "kw_ready", "ve_ready", "pm_ready", "st_ready", "bs_ready", "ha_ready",
                                      "c_ready", "h_ready", "y_read", "y_ready", "h1_ready", "masked", "skipped",
                                      "cols_ready", "o_ready", "sq_ready", "root_ready", "var_ready"))
        h1_out, ho_free, xs_made = m.sem("x_h1_out"), m.sem("x_ho_free"), m.sem("x_xs_made")
        step = Tally(m.sem("x_step"))
        fm = lambda d_: d_.rearrange("(k p) (c t) -> c p k t", p=P, t=MC)

        with nc.Block() as block:
            @block.sync
            def _(sp):
                head = lambda n: a[n][0].rearrange("h (k p) e -> p (h k) e", p=P)
                sp.dma_start(wq[:], head("m_wq")).then_inc(w_in, 16)
                sp.dma_start(wk[:], head("m_wk")).then_inc(w_in, 16)
                sp.dma_start(wvo[:, :, 0, :], head("m_wv")).then_inc(w_in, 16)
                sp.dma_start(wvo[:, :, 1, :], head("m_wo")).then_inc(w_in, 16)
                sp.dma_start(gates0[:], m.gate_d[0:1].broadcast_to([P, D])).then_inc(w_in, 16)
                sp.dma_start(wo[:], a["ev_w_out"][0].rearrange("(k p) n -> p k n", p=P)).then_inc(w_in, 16)
                with sp.Fori(0, NMC) as c:
                    sp.wait_ge(skipped, c + 1)
                    sp.wait_ge(vo_done, c * MH + 1)
                    sp.dma_start(mt[:], fm(m.m_d)[c]).then_inc(in_mx, 16)
                    sp.dma_start(xt[:], fm(m.xc_d)[c]).then_inc(in_mx, 16)
                    sp.wait_ge(masked, c + 1)
                    sp.dma_start(gb[:], m.gb_d.rearrange("(h c) t -> c h t", h=MH)[c].partition_broadcast(P)).then_inc(in_gb, 16)
                    sp.wait_ge(y_ready, c + 1)
                    sp.wait_ge(o_done, c + 1)
                    sp.dma_start(zt[:], fm(m.smz_d)[c]).then_inc(in_zy, 16)
                    sp.dma_start(yst[:], fm(m.ys_d)[c]).then_inc(in_zy, 16)
                    sp.wait_ge(h1_ready, c * 2 + 2)
                    sp.dma_start(xr[:], a["x"].rearrange("o (c t) d -> (o c) t d", t=MC)[c]).then_inc(in_x, 16)

            @block.gpsimd
            def _(pool):
                nc.gpsimd.memset(mask[:], 0.0).then_inc(made, 1)
                nc.gpsimd.memset(cst[:], 0.0).then_inc(made, 1)
                for j in range(2):
                    nc.gpsimd.memset(ve[j][:, HD:HW], 1.0).then_inc(made, 1)
                pool.wait_ge(made, 4)
                nc.gpsimd.affine_select(out=mask[:], in_=mask[:], compare_op=ALU.is_ge, fill=NEG, base=0,
                                        pattern=[[1, MC]], channel_multiplier=-1).then_inc(made, 1)
                pool.wait_ge(made, 5)
                pool.sem_inc(masked, 1)
                pool.sem_inc(skipped, 1)
                skip = m.cols[:, ROWS["m_skip"]:ROWS["m_skip"] + KC].unsqueeze(2).broadcast_to([P, KC, MC])
                with pool.Fori(0, NMC) as c:
                    pool.wait_ge(in_gb, c * 16 + 16)
                    pool.wait_ge(pm_ready, c * MH + MH)
                    pool.wait_ge(st_ready, c * MH + MH)
                    nc.gpsimd.tensor_tensor(pm[:], mask[:].unsqueeze(1).broadcast_to([P, MH, MC]), gb[:], ALU.subtract).then_inc(masked, 1)
                    pool.wait_ge(in_mx, c * 32 + 32)
                    pool.wait_ge(y_ready, c + 1)
                    nc.gpsimd.tensor_tensor(xs[:], xt[:], skip, ALU.mult).then_inc(xs_made, 1)
                    pool.wait_ge(xs_made, c + 1)
                    pool.wait_ge(kt_done, c * MH + (MH + 1))
                    pool.wait_ge(qk_done, c * MH + (MH + 1))
                    pool.sem_inc(skipped, 1)
                    pool.wait_ge(h1_ready, c * 2 + 4)
                    pool.dma_start(m.h1_d.rearrange("(c t) d -> c t d", t=MC)[c], ho[:]).then_inc(h1_out, 16)
                    pool.wait_ge(h1_out, c * 16 + 16)
                    pool.sem_inc(ho_free, 1)

            @block.scalar
            def _(act):
                act.sem_inc(pm_ready, MH)
                act.sem_inc(ve_ready, 2)
                act.sem_inc(bs_ready, 2)
                act.sem_inc(o_ready, 1)
                act.wait_ge(made, 5)
                with act.Fori(0, NMC) as c:
                    act.wait_ge(cols_ready, c + 1)
                    act.wait_ge(masked, c + 2)
                    for h in range(MH):
                        nc.scalar.activation(pm[:, h, :], pm[:, h, :], ACT.Exp, bias=cc[:, 0, h:h + 1]).then_inc(pm_ready, 1)
                    for h in range(MH):
                        r = h % 2
                        act.wait_ge(qk_done, c * MH + (h + 1 + 1))
                        act.wait_ge(c_done, c * MH + (h + 1))
                        nc.scalar.activation(qt[:, r], QK[:, 0:2 * MC].rearrange("p (a b) -> p a b", a=2), ACT.Copy, scale=HD ** -0.5)
                        nc.scalar.copy(kt[:, r], QK[:, 2 * MC:4 * MC].rearrange("p (a b) -> p a b", a=2)).then_inc(qk_read, 1)
                        act.wait_ge(vo_done, c * MH + (h + 1 + 1))
                        act.wait_ge(a_done, c * MH + (h + 1))
                        act.wait_ge(h_ready, c + 1)
                        nc.scalar.activation(og[:, h, :], VO[:, HD:2 * HD], ACT.Sigmoid)
                        nc.scalar.copy(ve[r][:, 0:HD], VO[:, 0:HD]).then_inc(ve_ready, 1)
                        act.wait_ge(b_done, c * MH + (h + 1))
                        act.wait_ge(ha_ready, c * MH + (h + 1))
                        nc.scalar.activation(bs[r][:], BB[:, 0:HW], ACT.Copy, scale=cc[:, 1, h:h + 1]).then_inc(bs_ready, 1)
                    act.wait_ge(var_ready, c * 2 + 1)
                    nc.scalar.activation(ha[:, :, 0:HD], hs[:], ACT.Square).then_inc(sq_ready, 1)
                    act.wait_ge(var_ready, c * 2 + 2)
                    nc.scalar.activation(sm[:, 3], sm[:, 2], ACT.Sqrt).then_inc(root_ready, 1)
                    for k in range(KC):
                        if k % 4 == 0:
                            act.wait_ge(y_turned, c * 2 + (k // 4 + 1))
                            if k == 0:
                                act.wait_ge(o_done, c + 1)
                        last = nc.scalar.activation(ym[:, k, :], (QK, VO)[k // 4][:, (k % 4) * MC:(k % 4 + 1) * MC], ACT.Copy,
                                                    scale=m.cols[:, ROWS["m_norm_g"] + k:ROWS["m_norm_g"] + k + 1])
                        if k % 4 == 3:
                            last.then_inc(y_read, 1)

            @block.vector
            def _(v):
                def L(ins):
                    v.wait_ge(step.sem, step.add(ins))

                tt, stt, ts = nc.vector.tensor_tensor, nc.vector.scalar_tensor_tensor, nc.vector.tensor_scalar
                v.sem_inc(kw_ready, 2)
                v.sem_inc(st_ready, MH)
                v.sem_inc(ha_ready, 2)
                v.sem_inc(h_ready, 1)
                v.sem_inc(y_ready, 1)
                v.sem_inc(h1_ready, 2)
                v.sem_inc(c_ready, 1)
                v.sem_inc(ho_free, 1)
                v.wait_ge(made, 5)
                with v.Fori(0, NMC) as c:
                    step.enter(c, 13)
                    v.wait_ge(ha_ready, c * MH + 2)
                    v.wait_ge(bs_ready, c * MH + 2)
                    v.wait_ge(pm_ready, c * MH + MH)
                    v.wait_ge(c_ready, c * MH + 1)
                    step.add(nc.vector.tensor_copy(dec[:], m.decay[:, :, c]))
                    nc.vector.tensor_copy(cc[:], m.gcol[:, c]).then_inc(cols_ready, 1)
                    v.wait_ge(cols_ready, c + 1)
                    v.wait_ge(step.sem, step.mark())
                    for h in range(MH):
                        r = h % 2
                        v.wait_ge(kt_done, c * MH + (h + 1 + 1))
                        v.wait_ge(c_done, c * MH + (h + 1))
                        ts(kw[r][:], KT[:, 0:HD], cc[:, 2, h:h + 1], None, ALU.mult).then_inc(kw_ready, 1)
                        v.wait_ge(s_done, c * MH + (h + 1))
                        v.wait_ge(pm_ready, c * MH + (h + 1 + MH))
                        v.wait_ge(a_done, c * MH + (h + 1))
                        tt(st[r][:], SS[:, 0:MC], pm[:, h, :], ALU.mult).then_inc(st_ready, 1)
                        v.wait_ge(c_done, c * MH + (h + 1 + 2))
                        v.wait_ge(c_ready, c * MH + (h + 1))
                        stt(out=cst[:, h, 0], in0=cst[:, h, 0], scalar=dec[:, h:h + 1], in1=C0[:, 0:HW], op0=ALU.mult, op1=ALU.add)
                        stt(out=cst[:, h, 1], in0=cst[:, h, 1], scalar=dec[:, h:h + 1], in1=C1[:, 0:HW],
                            op0=ALU.mult, op1=ALU.add).then_inc(c_ready, 1)
                        v.wait_ge(a_done, c * MH + (h + 1 + 2))
                        v.wait_ge(bs_ready, c * MH + (h + 1 + 2))
                        tt(ha[:, h, :], AA[:, 0:HW], bs[r][:], ALU.add).then_inc(ha_ready, 1)
                    v.wait_ge(ha_ready, c * MH + (MH + 2))
                    L(stt(out=sm[:, 0], in0=ha[:, :, HD], scalar=-1.0, in1=ha[:, :, HD], op0=ALU.mult, op1=ALU.max))
                    L(tt(sm[:, 0], sm[:, 0], cc[:, 3], ALU.max))
                    L(nc.vector.reciprocal(sm[:, 1], sm[:, 0]))
                    over = lambda s: s.unsqueeze(2).broadcast_to([P, MH, HD])
                    L(tt(hs[:], ha[:, :, 0:HD], over(sm[:, 1]), ALU.mult))
                    tt(hs[:], hs[:], og[:], ALU.mult).then_inc(var_ready, 1)
                    v.wait_ge(sq_ready, c + 1)
                    L(nc.vector.tensor_reduce(sm[:, 2], ha[:, :, 0:HD], AX.X, ALU.add))
                    ts(sm[:, 2], sm[:, 2], 1.0 / HD, EPS, ALU.mult, ALU.add).then_inc(var_ready, 1)
                    v.wait_ge(root_ready, c + 1)
                    rsqrt_steps(nc, L, sm[:, 2], sm[:, 3], sm[:, 4], sm[:, 5])
                    tt(hs[:], hs[:], over(sm[:, 4]), ALU.mult).then_inc(h_ready, 1)
                    v.wait_ge(y_read, c * 2 + 4)
                    v.wait_ge(xs_made, c + 1)
                    L(tt(ym[:], ym[:], xs[:], ALU.add))
                    v.wait_ge(in_zy, c * 32 + 32)
                    tt(ym[:], ym[:], zt[:], ALU.mult).then_inc(y_ready, 1)
                    v.wait_ge(in_x, c * 16 + 16)
                    v.wait_ge(ho_free, c + 1)
                    v.wait_ge(o_done, c + 2)
                    for n, bank in enumerate((AA, BB)):
                        at = slice(n * 512, (n + 1) * 512)
                        L(tt(ho[:, at], bank[:], gates0[:, at], ALU.mult))
                        tt(ho[:, at], ho[:, at], xr[:, at], ALU.add).then_inc(h1_ready, 1)
                step.leave(NMC)

            @block.tensor
            def _(pe):
                pe.sem_inc(vo_done, 1)
                pe.sem_inc(kt_done, 1)
                pe.sem_inc(qk_done, 1)
                pe.sem_inc(c_done, 2)
                pe.sem_inc(a_done, 2)
                pe.sem_inc(o_done, 1)
                pe.sem_inc(qk_read, 1)
                pe.sem_inc(y_read, 2)
                pe.wait_ge(w_in, 16 * 6)
                mm = nc.tensor.matmul

                def inputs(c, h):
                    pe.wait_ge(qk_read, c * MH + (h + 1))
                    if h == 0:
                        pe.wait_ge(y_read, c * 2 + 2)
                    for j, w in enumerate((wq, wk)):
                        for e in range(2):
                            at = (2 * j + e) * MC
                            for k in range(2):
                                last = mm(QK[:, at:at + MC], w[:, 2 * h + k, e * P:(e + 1) * P], xt[:, 2 * h + k, :],
                                          start=(k == 0), stop=(k == 1))
                    last.then_inc(qk_done, 1)
                    pe.wait_ge(kw_ready, c * MH + (h + 2))
                    for k in range(2):
                        last = mm(KT[:, 0:HD], xt[:, 2 * h + k, :], wk[:, 2 * h + k, :], start=(k == 0), stop=(k == 1))
                    last.then_inc(kt_done, 1)
                    pe.wait_ge(ve_ready, c * MH + (h + 2))
                    for k in range(2):
                        last = mm(VO[:], mt[:, 2 * h + k, :], wvo[:, 2 * h + k].rearrange("p a e -> p (a e)"), start=(k == 0), stop=(k == 1))
                    last.then_inc(vo_done, 1)

                def cell(c, h):
                    r = h % 2
                    pe.wait_ge(qk_read, c * MH + (h + 2))
                    pe.wait_ge(st_ready, c * MH + (h + MH))
                    for e in range(2):
                        last = mm(SS[:, 0:MC], kt[:, r, e], qt[:, r, e], start=(e == 0), stop=(e == 1))
                    last.then_inc(s_done, 1)
                    if h == 0:
                        pe.wait_ge(h1_ready, c * 2 + 2)
                    pe.wait_ge(bs_ready, c * MH + (h + 2))
                    pe.wait_ge(c_ready, c * MH + (h + 1))
                    for e in range(2):
                        last = mm(BB[:, 0:HW], qt[:, r, e], cst[:, h, e], start=(e == 0), stop=(e == 1))
                    last.then_inc(b_done, 1)
                    pe.wait_ge(kw_ready, c * MH + (h + 3))
                    pe.wait_ge(ve_ready, c * MH + (h + 3))
                    mm(C0[:, 0:HW], kw[r][:, 0:P], ve[r][:], start=True, stop=True)
                    mm(C1[:, 0:HW], kw[r][:, P:2 * P], ve[r][:], start=True, stop=True).then_inc(c_done, 1)
                    pe.wait_ge(ha_ready, c * MH + (h + 2))
                    pe.wait_ge(st_ready, c * MH + (h + 1 + MH))
                    mm(AA[:, 0:HW], st[r][:], ve[r][:], start=True, stop=True).then_inc(a_done, 1)

                with pe.Fori(0, NMC) as c:
                    pe.wait_ge(in_mx, c * 32 + 32)
                    for h in range(MH):
                        inputs(c, h)
                        cell(c, h)
                    pe.wait_ge(h_ready, c + 2)
                    hf = hs[:].rearrange("p h e -> p (h e)")
                    for k in range(KC):
                        tr = nc.tensor.transpose((QK, VO)[k // 4][:, (k % 4) * MC:(k % 4 + 1) * MC], hf[:, k * P:(k + 1) * P], m.ident[:])
                        if k % 4 == 3:
                            tr.then_inc(y_turned, 1)
                    pe.wait_ge(in_zy, c * 32 + 32)
                    pe.wait_ge(ha_ready, c * MH + (MH + 2))
                    for n, bank in enumerate((AA, BB)):
                        for k in range(KC):
                            mm(bank[:], yst[:, k, :], wo[:, k, n * 512:(n + 1) * 512], start=(k == 0), stop=False)
                    pe.wait_ge(y_ready, c + 2)
                    for n, bank in enumerate((AA, BB)):
                        for k in range(KC):
                            last = mm(bank[:], ym[:, k, :], wo[:, KC + k, n * 512:(n + 1) * 512], start=False, stop=(k == KC - 1))
                    last.then_inc(o_done, 1)


def attention(m, a, out):
    nc = m.nc
    NH = AH + AKV
    NW = NH * AD + AKV * AD + AH * AD
    QKW = NH * AD
    with ExitStack() as ctx:
        sb = lambda n, s, d=F32: ctx.enter_context(nc.sbuf_tensor(n, s, d))
        win = sb("a_win", [P, KC, NW])
        wout = sb("a_wout", [P, KC, D])
        pos_i, pos_f = sb("a_pos_i", [TT, P], I32), sb("a_pos_f", [TT, P])
        post = sb("a_pos", [P, TT])
        rc, rs_, rt = (sb(n, [P, TT, ROPE // 2]) for n in ("a_rope_c", "a_rope_s", "a_rope_t"))
        ra = sb("a_rope_a", [P, TT, ROPE // 2])
        gqk = sb("a_gqk", [P, NH, AD])
        gr = sb("a_g_rows", [P, 2, AD])
        sink = sb("a_sink", [P, AH])
        gate = sb("a_gate", [P, D])
        mk = [sb(f"a_mask{j}", [P, 2, P]) for j in range(2)]
        before = sb("a_mask_before", [P, P])
        ht = [sb(f"a_h{j}", [P, D]) for j in range(2)]
        xn = sb("a_xn", [P, D])
        xT = sb("a_xT", [P, KC, P])
        qk = sb("a_qk", [P, NH, AD])
        qr = sb("a_qr", [P, NH, AD])
        r4 = [sb(f"a_r{j}", [P, NH, ROPE // 2]) for j in range(4)]
        qT = sb("a_qT", [P, KC, P])
        kT = sb("a_kT", [P, 2, 2, P])
        vv = sb("a_v", [P, 2, AKV * AD])
        sz = sb("a_sz", [P, D])
        sc = [sb(f"a_sc{j}", [P, 4, 2 * P]) for j in range(2)]
        pT = [sb(f"a_pT{j}", [P, 8, P]) for j in range(2)]
        att = qk[:, 0:AH].rearrange("p h d -> p (h d)")
        aT = sb("a_aT", [P, KC, P])
        ot = [sb(f"a_o{j}", [P, D]) for j in range(2)]
        st = sb("a_stat", [P, 6])
        hstat = sb("a_hstat", [P, 5, NH])
        mx, nmx, rsum, den = (sb(n, [P, AH]) for n in ("a_mx", "a_nmx", "a_rsum", "a_den"))
        pq = ctx.enter_context(nc.psum_tensor("a_pq", [P, 2, 512], F32))
        t1 = ctx.enter_context(nc.psum_tensor("a_t1", [P, 4, P], F32))
        pz = ctx.enter_context(nc.psum_tensor("a_pz", [P, 2, 512], F32))
        t0 = ctx.enter_context(nc.psum_tensor("a_t0", [P, 4, P], F32))
        psc = ctx.enter_context(nc.psum_tensor("a_psc", [P, 4, 2 * P], F32))
        T = (t0, t1)

        w_in, c_in = m.sem("a_w_in"), m.sem("a_c_in")
        h_in = [m.sem(f"a_h_in{j}") for j in range(2)]
        step = Tally(m.sem("a_step"))
        pool_made, pos_ready, pos_turned, angles, tables = (m.sem(f"a_{n}") for n in ("made", "pos_ready", "pos_turned", "angles", "tables"))
        (sq_ready, var_ready, root_ready, xn_ready, xn_turned, xT_ready, q_done, kv_done, z_done, qk_squared, v_ready,
         z_ready, qk_var, qk_root, qk_ready, qk_turned, qT_ready, s_done, s_read, max_ready, exp_ready, p_turned,
         pT_ready, pT2_ready, pv_done, sink_ready, att_ready, att_turned, aT_ready, o_done, o_ready, mask_ready, q_read) = (
            m.sem(f"a_{n}") for n in
            ("sq_ready", "var_ready", "root_ready", "xn_ready", "xn_turned", "xT_ready", "q_done", "kv_done", "z_done",
             "qk_squared", "v_ready", "z_ready", "qk_var", "qk_root", "qk_ready", "qk_turned", "qT_ready", "s_done",
             "s_read", "max_ready", "exp_ready", "p_turned", "pT_ready", "pT2_ready", "pv_done", "sink_ready", "att_ready",
             "att_turned", "aT_ready", "o_done", "o_ready", "mask_ready", "q_read"))
        o_out = [m.sem(f"a_o_out{j}") for j in range(2)]

        with nc.Block() as block:
            @block.sync
            def _(sp):
                sp.dma_start(pos_i[:], a["positions"].rearrange("o (t p) -> (o t) p", p=P)).then_inc(c_in, 16)
                sp.dma_start(gr[:, 0, :], a["od_q_norm_g"].broadcast_to([P, AD])).then_inc(c_in, 16)
                sp.dma_start(gr[:, 1, :], a["od_k_norm_g"].broadcast_to([P, AD])).then_inc(c_in, 16)
                sp.dma_start(sink[:], a["od_sinks"].broadcast_to([P, AH])).then_inc(c_in, 16)
                sp.dma_start(gate[:], m.gate_d[1:2].broadcast_to([P, D])).then_inc(c_in, 16)
                wv = a["od_w_in"][0].rearrange("(k p) n -> p k n", p=P)
                hv = m.h1_d.rearrange("(t p) d -> t p d", p=P)
                sp.sem_inc(o_ready, 2)
                for j in range(2):
                    sp.sem_inc(o_out[j], 16)
                for k in range(KC):
                    sp.dma_start(win[:, k], wv[:, k]).then_inc(w_in, 16)
                sp.dma_start(wout[:], a["od_w_out"][0].rearrange("(k p) n -> p k n", p=P)).then_inc(w_in, 16)
                ov = out.rearrange("o (t p) d -> (o t) p d", p=P)
                with sp.Fori(0, TT // 2) as i:
                    t = i * 2
                    for j in range(2):
                        sp.wait_ge(o_ready, t + (j + 1))
                        sp.dma_start(ht[j][:], hv[t + j]).then_inc(h_in[j], 16)
                    for j in range(2):
                        sp.wait_ge(o_ready, t + (j + 3))
                        sp.dma_start(ov[t + j], ot[j][:]).then_inc(o_out[j], 16)
                for j in range(2):
                    sp.wait_ge(o_out[j], 16 * (TT // 2 + 1))

            @block.gpsimd
            def _(pool):
                made = 0
                for tile in (mk[0], mk[1], before, kT, vv):
                    nc.gpsimd.memset(tile[:], 0.0).then_inc(pool_made, 1)
                    made += 1
                pool.wait_ge(pool_made, made)
                now = dict(pattern=[[-1, P]], channel_multiplier=1, base=0)
                then = dict(pattern=[[1, P]], channel_multiplier=-1, base=-1)
                for tile, pat in ((mk[0][:, 0, :], now), (mk[1][:, 1, :], now), (mk[1][:, 0, :], then), (before[:], then)):
                    nc.gpsimd.affine_select(out=tile, in_=tile, compare_op=ALU.is_ge, fill=NEG, **pat).then_inc(pool_made, 1)
                nc.gpsimd.memset(mk[0][:, 1, :], NEG).then_inc(pool_made, 1)
                pool.wait_ge(pool_made, made + 5)
                pool.sem_inc(mask_ready, 1)

            @block.scalar
            def _(act):
                act.wait_ge(mask_ready, 1)
                act.wait_ge(angles, 1)
                nc.scalar.activation(rs_[:], rs_[:], ACT.Sin)
                nc.scalar.activation(rc[:], rc[:], ACT.Sin).then_inc(tables, 1)
                with act.Fori(0, TT // 2) as i:
                    for j in range(2):
                        t = i * 2 + j
                        act.wait_ge(h_in[j], i * 16 + 16)
                        act.wait_ge(xn_turned, t * 2 + 2)
                        nc.scalar.activation(xn[:], ht[j][:], ACT.Square, accum_out=st[:, 0:1]).then_inc(sq_ready, 1)
                        act.wait_ge(var_ready, t + 1)
                        nc.scalar.activation(st[:, 2:3], st[:, 1:2], ACT.Sqrt).then_inc(root_ready, 1)
                        for k in range(KC):
                            if k % 4 == 0:
                                act.wait_ge(xn_turned, t * 2 + (k // 4 + 3))
                            last = nc.scalar.activation(xT[:, k, :], T[k // 4][:, k % 4, :], ACT.Identity,
                                                        scale=m.moda[:, 1, k:k + 1], bias=m.ada[:, 1, k:k + 1])
                            if k % 4 == 3:
                                last.then_inc(xT_ready, 1)
                        act.wait_ge(q_done, t + 1)
                        act.wait_ge(qk_ready, t + 1)
                        act.wait_ge(qk_turned, t * 3 + 3)
                        nc.scalar.activation(qr[:, 0:AH, :], pq[:].rearrange("p a (h d) -> p (a h) d", d=AD), ACT.Square)
                        act.wait_ge(kv_done, t + 1)
                        nc.scalar.activation(qr[:, AH:NH, :], t1[:, 0:2, :].rearrange("p a (h d) -> p (a h) d", d=AD),
                                             ACT.Square).then_inc(qk_squared, 1)
                        act.wait_ge(pv_done, t * 4 + 4)
                        nc.scalar.copy(vv[:, j, :], t1[:, 2:4, :].rearrange("p a b -> p (a b)")).then_inc(v_ready, 1)
                        act.wait_ge(qk_var, t + 1)
                        nc.scalar.activation(hstat[:, 2], hstat[:, 1], ACT.Sqrt).then_inc(qk_root, 1)
                        act.wait_ge(att_ready, t + 1)
                        for n in range(2):
                            act.wait_ge(z_done, t * 2 + (n + 1))
                            nc.scalar.activation(sz[:, n * 512:(n + 1) * 512], pz[:, n, :], ACT.Silu).then_inc(z_ready, 1)
                        act.wait_ge(qk_turned, t * 3 + 4)
                        nc.scalar.copy(kT[:, :, j, :], t0[:, 0:2, :])
                        nc.scalar.copy(qT[:, 0:2, :], t0[:, 2:4, :]).then_inc(qT_ready, 1)
                        act.wait_ge(qk_turned, t * 3 + 5)
                        nc.scalar.copy(qT[:, 2:6, :], t1[:]).then_inc(qT_ready, 1)
                        act.wait_ge(qk_turned, t * 3 + 6)
                        nc.scalar.copy(qT[:, 6:8, :], t0[:, 0:2, :]).then_inc(qT_ready, 1)
                        for g in range(AKV):
                            act.wait_ge(max_ready, t * 4 + (g + 1))
                            for r in range(4):
                                h = 4 * g + r
                                last = nc.scalar.activation(sc[g % 2][:, r, :], sc[g % 2][:, r, :], ACT.Exp,
                                                            bias=nmx[:, h:h + 1], accum_out=rsum[:, h:h + 1])
                            last.then_inc(exp_ready, 1)
                            act.wait_ge(p_turned, t * 8 + (2 * g + 5))
                            act.wait_ge(pv_done, t * 4 + (g + 3))
                            nc.scalar.copy(pT[g % 2][:, 0:4, :], t0[:]).then_inc(pT_ready, 1)
                        act.wait_ge(max_ready, t * 4 + 4)
                        nc.scalar.activation(den[:], den[:], ACT.Exp).then_inc(sink_ready, 1)
                        for k in range(2):
                            act.wait_ge(att_turned, t * 2 + (k + 1))
                            nc.scalar.copy(aT[:, 4 * k:4 * k + 4, :], T[k][:]).then_inc(aT_ready, 1)

            @block.vector
            def _(v):
                def L(ins):
                    v.wait_ge(step.sem, step.add(ins))

                tt, stt, ts = nc.vector.tensor_tensor, nc.vector.scalar_tensor_tensor, nc.vector.tensor_scalar
                v.wait_ge(c_in, 80)
                nc.vector.tensor_copy(pos_f[:], pos_i[:]).then_inc(pos_ready, 1)
                L(ts(gqk[:, 0:AH, :], gr[:, 0:1, :].broadcast_to([P, AH, AD]), AD ** -0.5, None, ALU.mult))
                L(nc.vector.tensor_copy(gqk[:, AH:NH, :], gr[:, 1:2, :].broadcast_to([P, AKV, AD])))
                v.wait_ge(pos_turned, 1)
                L(nc.vector.tensor_copy(post[:], t0[:, 0, 0:TT]))
                freq = rope_frequencies()
                for f in range(ROPE // 2):
                    L(ts(ra[:, :, f], post[:], freq[f], None, ALU.mult))
                L(ts(rt[:], ra[:], 1.0 / TWO_PI, ROUND, ALU.mult, ALU.add))
                L(ts(rt[:], rt[:], ROUND, None, ALU.subtract))
                for c in TWO_PI_PARTS:
                    L(stt(out=ra[:], in0=rt[:], scalar=-c, in1=ra[:], op0=ALU.mult, op1=ALU.add))
                L(ts(rs_[:], ra[:], PI_SAFE, -PI_SAFE, ALU.min, ALU.max))
                L(ts(rt[:], ra[:], math.pi / 2, -TWO_PI, ALU.is_gt, ALU.mult))
                L(stt(out=rc[:], in0=ra[:], scalar=math.pi / 2, in1=rt[:], op0=ALU.add, op1=ALU.add))
                L(ts(rc[:], rc[:], PI_SAFE, -PI_SAFE, ALU.min, ALU.max))
                v.sem_inc(angles, 1)
                v.sem_inc(qk_ready, 1)
                v.sem_inc(att_ready, 1)
                v.sem_inc(s_read, 1)
                v.wait_ge(tables, 1)
                with v.Fori(0, TT // 2) as i:
                    step.enter(i, 2 * 35 + 1)
                    for j in range(2):
                        t = i * 2 + j
                        v.wait_ge(sq_ready, t + 1)
                        ts(st[:, 1:2], st[:, 0:1], 1.0 / D, EPS, ALU.mult, ALU.add).then_inc(var_ready, 1)
                        v.wait_ge(root_ready, t + 1)
                        v.wait_ge(var_ready, t + 1)
                        rsqrt_steps(nc, L, st[:, 1:2], st[:, 2:3], st[:, 3:4], st[:, 4:5])
                        ts(xn[:], ht[j][:], st[:, 3:4], None, ALU.mult).then_inc(xn_ready, 1)
                        v.wait_ge(qk_squared, t + 1)
                        L(nc.vector.tensor_reduce(hstat[:, 0], qr[:], AX.X, ALU.add))
                        ts(hstat[:, 1], hstat[:, 0], 1.0 / AD, EPS, ALU.mult, ALU.add).then_inc(qk_var, 1)
                        v.wait_ge(qk_root, t + 1)
                        rsqrt_steps(nc, L, hstat[:, 1], hstat[:, 2], hstat[:, 3], hstat[:, 4])
                        over = lambda lo, hi: hstat[:, 3, lo:hi].unsqueeze(2).broadcast_to([P, hi - lo, AD])
                        step.add(tt(qk[:, 0:AH], pq[:].rearrange("p a (h d) -> p (a h) d", d=AD), over(0, AH), ALU.mult))
                        L(tt(qk[:, AH:NH], t1[:, 0:2, :].rearrange("p a (h d) -> p (a h) d", d=AD), over(AH, NH), ALU.mult))
                        v.sem_inc(q_read, 1)
                        for b in range(2):
                            q8 = slice(8 * b, 8 * b + 8)
                            step.add(tt(qr[:, q8].rearrange("p (r b) d -> p b r d", b=2), qk[:, q8].rearrange("p (b r) d -> p b r d", b=2),
                                        gqk[:, q8].rearrange("p (b r) d -> p b r d", b=2), ALU.mult))
                        L(tt(qr[:, AH:NH], qk[:, AH:NH], gqk[:, AH:NH], ALU.mult))
                        H8 = ROPE // 2
                        c8, s8 = (x[:, t, :].unsqueeze(1).broadcast_to([P, NH, H8]) for x in (rc, rs_))
                        x1, x2 = qr[:, :, 0:H8], qr[:, :, H8:ROPE]
                        step.add(tt(r4[0][:], x1, c8, ALU.mult))
                        step.add(tt(r4[1][:], x2, s8, ALU.mult))
                        step.add(tt(r4[2][:], x2, c8, ALU.mult))
                        L(tt(r4[3][:], x1, s8, ALU.mult))
                        L(tt(x1, r4[0][:], r4[1][:], ALU.subtract))
                        tt(x2, r4[2][:], r4[3][:], ALU.add).then_inc(qk_ready, 1)
                        for g in range(AKV):
                            hs = slice(4 * g, 4 * g + 4)
                            v.wait_ge(s_done, t * 4 + (g + 1))
                            v.wait_ge(mask_ready, 1)
                            v.wait_ge(p_turned, t * 8 + (2 * g + 2))
                            tt(sc[g % 2][:], psc[:], mk[j][:].rearrange("p a b -> p (a b)").unsqueeze(1).broadcast_to([P, 4, 2 * P]),
                               ALU.add).then_inc(s_read, 1)
                            v.wait_ge(s_read, t * 4 + (g + 2))
                            L(nc.vector.tensor_reduce(mx[:, hs], sc[g % 2][:], AX.X, ALU.max))
                            L(tt(mx[:, hs], mx[:, hs], sink[:, hs], ALU.max))
                            L(tt(den[:, hs], sink[:, hs], mx[:, hs], ALU.subtract))
                            ts(nmx[:, hs], mx[:, hs], -1.0, None, ALU.mult).then_inc(max_ready, 1)
                            v.wait_ge(p_turned, t * 8 + (2 * g + 6))
                            nc.vector.tensor_copy(pT[g % 2][:, 4:8, :], t1[:]).then_inc(pT2_ready, 1)
                        if j == 0:
                            L(nc.vector.tensor_copy(mk[0][:, 1, :], before[:]))
                        v.wait_ge(sink_ready, t + 1)
                        L(tt(den[:], den[:], rsum[:], ALU.add))
                        L(nc.vector.reciprocal(mx[:], den[:]))
                        v.wait_ge(pv_done, t * 4 + 8)
                        L(tt(qk[:, 0:AH], pq[:].rearrange("p a (h d) -> p (a h) d", d=AD),
                             mx[:].unsqueeze(2).broadcast_to([P, AH, AD]), ALU.mult))
                        v.wait_ge(z_ready, t * 2 + 2)
                        tt(att, att, sz[:], ALU.mult).then_inc(att_ready, 1)
                        v.wait_ge(o_out[j], i * 16 + 16)
                        v.wait_ge(o_done, t + 1)
                        L(tt(ot[j][:], pz[:].rearrange("p a b -> p (a b)"), gate[:], ALU.mult))
                        tt(ot[j][:], ot[j][:], ht[j][:], ALU.add).then_inc(o_ready, 1)
                step.leave(TT // 2)

            @block.tensor
            def _(pe):
                mm = nc.tensor.matmul
                pe.sem_inc(xn_turned, 2)
                pe.sem_inc(qk_turned, 3)
                pe.sem_inc(pv_done, 4)
                pe.sem_inc(p_turned, 4)
                pe.wait_ge(pos_ready, 1)
                nc.tensor.transpose(t0[:, 0, 0:TT], pos_f[:], m.ident[0:TT, 0:TT]).then_inc(pos_turned, 1)
                pe.wait_ge(w_in, 16 * (KC + 1))
                pe.wait_ge(angles, 1)
                with pe.Fori(0, TT // 2) as i:
                    for j in range(2):
                        t = i * 2 + j
                        pe.wait_ge(xn_ready, t + 1)
                        for k in range(KC):
                            tr = nc.tensor.transpose(T[k // 4][:, k % 4, :], xn[:, k * P:(k + 1) * P], m.ident[:])
                            if k % 4 == 3:
                                tr.then_inc(xn_turned, 1)
                        pe.wait_ge(xT_ready, t * 2 + 2)
                        proj = lambda dst, lo: [mm(dst, xT[:, k, :], win[:, k, lo:lo + 512], start=(k == 0), stop=(k == KC - 1))
                                                for k in range(KC)][-1]
                        proj(pq[:, 0, :], 0)
                        proj(pq[:, 1, :], 512).then_inc(q_done, 1)
                        proj(t1[:].rearrange("p a b -> p (a b)"), AH * AD).then_inc(kv_done, 1)
                        pe.wait_ge(o_ready, t + 2)
                        for n in range(2):
                            proj(pz[:, n, :], QKW + AKV * AD + n * 512).then_inc(z_done, 1)
                        pe.wait_ge(qk_ready, t + 2)
                        pe.wait_ge(v_ready, t + 1)
                        for k in range(2):
                            nc.tensor.transpose(t0[:, k, :], qr[:, AH + 2 * k:AH + 2 * k + 2, :].rearrange("p h d -> p (h d)"), m.ident[:])
                        for n in range(8):
                            if n == 6:
                                pe.wait_ge(qT_ready, t * 3 + 1)
                            dst = t0[:, 2 + n, :] if n < 2 else t1[:, n - 2, :] if n < 6 else t0[:, n - 6, :]
                            tr = nc.tensor.transpose(dst, qr[:, 2 * n:2 * n + 2, :].rearrange("p h d -> p (h d)"), m.ident[:])
                            if n in (1, 5, 7):
                                tr.then_inc(qk_turned, 1)
                        pe.wait_ge(qT_ready, t * 3 + 3)

                        def scores(g):
                            lo = AD * (g % 2)
                            pe.wait_ge(s_read, t * 4 + (g + 1))
                            for r in range(4):
                                last = mm(psc[:, r, :], qT[lo:lo + AD, 4 * (g // 2) + r, :],
                                          kT[lo:lo + AD, g // 2].rearrange("p a b -> p (a b)"), start=True, stop=True)
                            last.then_inc(s_done, 1)

                        scores(0)
                        for g in range(AKV):
                            if g + 1 < AKV:
                                scores(g + 1)
                            pe.wait_ge(exp_ready, t * 4 + (g + 1))
                            for x in range(8):
                                tr = nc.tensor.transpose(T[x // 4][:, x % 4, :], sc[g % 2][:, x // 2, (x % 2) * P:(x % 2 + 1) * P], m.ident[:])
                                if x % 4 == 3:
                                    tr.then_inc(p_turned, 1)
                            pe.wait_ge(pT_ready, t * 4 + (g + 1))
                            pe.wait_ge(pT2_ready, t * 4 + (g + 1))
                            for r in range(4):
                                h = 4 * g + r
                                dst = pq[:].rearrange("p a b -> p (a b)")[:, h * AD:(h + 1) * AD]
                                for s in range(2):
                                    last = mm(dst, pT[g % 2][:, 2 * r + s, :], vv[:, s, g * AD:(g + 1) * AD], start=(s == 0), stop=(s == 1))
                            last.then_inc(pv_done, 1)
                        pe.wait_ge(att_ready, t + 2)
                        for k in range(KC):
                            tr = nc.tensor.transpose(T[k // 4][:, k % 4, :], att[:, k * P:(k + 1) * P], m.ident[:])
                            if k % 4 == 3:
                                tr.then_inc(att_turned, 1)
                        pe.wait_ge(aT_ready, t * 2 + 2)
                        for n in range(2):
                            for k in range(KC):
                                last = mm(pz[:, n, :], aT[:, k, :], wout[:, k, n * 512:(n + 1) * 512], start=(k == 0), stop=(k == KC - 1))
                        last.then_inc(o_done, 1)


_INS = ['x', 'c', 'positions', 'ada_w', 'ada_b', 'norm_g', 'ev_w_in', 's5_a_re', 's5_a_im', 's5_log_dt',
        's5_b_re', 's5_b_im', 's5_c_re', 's5_c_im', 's5_d', 's5_w_glu', 'm_conv_w', 'm_conv_b',
        'm_wq', 'm_wk', 'm_wv', 'm_wo', 'm_w_if', 'm_b_if', 'm_norm_g', 'm_skip', 'ev_w_out', 'od_w_in',
        'od_q_norm_g', 'od_k_norm_g', 'od_sinks', 'od_w_out']


def trunk(nc, a, out):
    with ExitStack() as ctx:
        m = names(nc, ctx)
        modulation(m, a)
        s5_tables(m, a)
        with ExitStack() as own:
            m.hT = own.enter_context(nc.sbuf_tensor("hT", [P, 2, KC, SEQ], F32R))
            norm_transposed(m, a)
            project(m, a)
        m.clear()
        glu(m, a)
        gates(m, a)
        mlstm(m, a)
        attention(m, a, out)


def kernel(**inputs):
    import concourse.bacc as bacc
    from concourse.bass_utils import run_bass_kernel_spmd

    nc = bacc.Bacc("TRN2", target_bir_lowering=False, num_devices=1)
    arrays, a = {}, {}
    for name in _INS:
        arrays[f"in_{name}"] = np.ascontiguousarray(inputs[name])
        a[name] = nc.dram_tensor(f"in_{name}", arrays[f"in_{name}"].shape, mybir.dt.from_np(arrays[f"in_{name}"].dtype),
                                 kind="ExternalInput").ap()
    out = nc.dram_tensor("out", [1, SEQ, D], F32, kind="ExternalOutput").ap()
    trunk(nc, a, out)
    r = run_bass_kernel_spmd(nc, [arrays], core_ids=[0])
    return r.results[0]["out"]
```

```python
import math
from contextlib import ExitStack

import numpy as np
import concourse.bass as bass
from concourse import mybir

ALU = mybir.AluOpType
ACT = mybir.ActivationFunctionType
AX = mybir.AxisListType
F32 = mybir.dt.float32
F32R = mybir.dt.float32r
I32 = mybir.dt.int32

P = 128
D = 1024
KC = D // P
SEQ = 2048
TT = SEQ // P
NB = 4
BT = SEQ // NB
EPS = 1e-6

G = 64
GP = 16
NS = 64
CH = 8
NCH = SEQ // CH
KB = NCH // NB

MH = 4
HD = 256
MC = 128
NMC = SEQ // MC

AH = 16
AKV = 4
AD = 64
ROPE = AD // 4
THETA = 500000.0

NEG = -1.0e30
TWO_PI = 2.0 * math.pi
ROUND = 1.5 * 2.0 ** 23
PI_SAFE = 3.1415925
TWO_PI_PARTS = (6.28125, 1.9350051879882812e-3, TWO_PI - 6.28125 - 1.9350051879882812e-3)

ROWS = {}
_at = 0
for _name, _n in (("ada_b", 48), ("norm_g", 16), ("s5_d", 8), ("conv_w", 32), ("conv_b", 8),
                  ("m_norm_g", 8), ("m_skip", 8)):
    ROWS[_name] = _at
    _at += _n
assert _at == P

BIN, BIS, COC, COS, TOE = 0, 128, 256, 384, 512
EBC, EBS, EAC, EAS, RAD = 640, 656, 672, 688, 704
BW = 708


class Tally:

    def __init__(self, sem, step=1):
        self.sem, self.step = sem, step
        self.base, self.k, self.i, self.per, self.start = 0, 0, None, 0, 0

    def add(self, ins):
        ins.then_inc(self.sem, self.step)
        self.k += 1
        return self.mark()

    def mark(self):
        value = (self.base + self.k) * self.step
        return value if self.i is None else (self.i - self.start) * (self.per * self.step) + value

    def enter(self, i, per, start=0):
        self.base, self.k, self.i, self.per, self.start = self.base + self.k, 0, i, per, start

    def leave(self, rounds):
        assert self.k == self.per, (self.k, self.per)
        self.base, self.k, self.i = self.base + rounds * self.per, 0, None


def rope_frequencies():
    half = ROPE // 2
    return [float(x) for x in np.exp(np.float32(-math.log(THETA)) * np.arange(half, dtype=np.float32) / np.float32(half))]


def rsqrt_steps(nc, link, v, root, out, tmp):
    link(nc.vector.reciprocal(out, root))
    link(nc.vector.tensor_tensor(tmp, v, out, ALU.mult))
    link(nc.vector.scalar_tensor_tensor(out=tmp, in0=tmp, scalar=-0.5, in1=out, op0=ALU.mult, op1=ALU.mult))
    link(nc.vector.scalar_tensor_tensor(out=out, in0=tmp, scalar=1.5, in1=out, op0=ALU.add, op1=ALU.mult))


def exp_steps(nc, link, dst, x, n, r, whole):
    ts, stt = nc.vector.tensor_scalar, nc.vector.scalar_tensor_tensor
    link(ts(n, x, 1.0 / math.log(2.0), ROUND, ALU.mult, ALU.add))
    link(ts(n, n, ROUND, None, ALU.subtract))
    link(ts(n, n, -127.0, 128.0, ALU.max, ALU.min))
    link(stt(out=r, in0=n, scalar=-0.693359375, in1=x, op0=ALU.mult, op1=ALU.add))
    link(stt(out=r, in0=n, scalar=0.693359375 - math.log(2.0), in1=r, op0=ALU.mult, op1=ALU.add))
    link(ts(r, r, 0.35, -0.35, ALU.min, ALU.max))
    link(ts(n, n, 127.0, 2.0 ** 23, ALU.add, ALU.mult))
    link(nc.vector.tensor_copy(whole, n))
    link(ts(n, r, 1.0 / math.factorial(7), None, ALU.mult))
    for k in range(6, 0, -1):
        link(stt(out=n, in0=n, scalar=1.0 / math.factorial(k), in1=r, op0=ALU.add, op1=ALU.mult))
    link(stt(out=dst, in0=n, scalar=1.0, in1=whole.bitcast(F32), op0=ALU.add, op1=ALU.mult))


class Core:
    pass


def names(nc, ctx):
    m = Core()
    m.nc, m.ctx = nc, ctx

    m.sems = []

    def sem(name):
        m.sems.append(nc.alloc_semaphore(name=name))
        return m.sems[-1]

    def clear():
        nc.all_engine_barrier()
        nc.clear_and_free_semaphores(m.sems)
        nc.all_engine_barrier()
        m.sems = []

    def dram(name, shape):
        return nc.dram_tensor(name, shape, F32, kind="Internal").ap()

    m.sem, m.clear = sem, clear
    m.u_d = dram("u_d", [D, NB, CH, KB])
    m.y_d = dram("y_d", [D, NB, CH, KB])
    m.sz_d = dram("sz_d", [D, NB, CH, KB])
    m.m_d = dram("m_d", [D, SEQ])
    m.xc_d = dram("xc_d", [D, SEQ])
    m.smz_d = dram("smz_d", [D, SEQ])
    m.ys_d = dram("ys_d", [D, SEQ])
    m.h1_d = dram("h1_d", [SEQ, D])
    m.gate_d = dram("gate_d", [2, D])
    m.s5w_d = dram("s5w_d", [G, P, BW])
    m.kz_d = dram("kz_d", [G, GP, 240])
    m.gt_d = dram("gt_d", [2 * MH, SEQ])
    m.mx_d = dram("mx_d", [4, MH * NMC])
    m.gb_d = dram("gb_d", [MH * NMC, MC])
    m.ident = ctx.enter_context(nc.sbuf_tensor("ident", [P, P], F32))
    m.cols = ctx.enter_context(nc.sbuf_tensor("cols", [P, P], F32))
    m.ada = ctx.enter_context(nc.sbuf_tensor("ada", [P, 2, 24], F32))
    m.spare = ctx.enter_context(nc.sbuf_tensor("gate_sums", [P, SEQ], F32))
    m.gacc = m.spare[0:2 * MH]
    m.decay = ctx.enter_context(nc.sbuf_tensor("decay", [P, MH, NMC], F32))
    m.gcol = ctx.enter_context(nc.sbuf_tensor("gate_cols", [P, NMC, 4, MH], F32))
    m.moda = ctx.enter_context(nc.sbuf_tensor("moda", [P, 2, KC], F32))
    return m


class Modulation:

    def __init__(self, m, a, ctx):
        nc, self.m, self.a = m.nc, m, a
        sb = lambda n, s: ctx.enter_context(nc.sbuf_tensor(n, s, F32))
        self.rows = sb("vec_rows", [P, P])
        self.crow = sb("c_row", [KC, P])
        self.cs = sb("c_silu", [P, KC])
        self.wr = [sb(f"ada_w{j}", [P, 3 * D]) for j in range(2)]
        self.grow = sb("gate_rows", [KC, 2 * P])
        self.ps_v = ctx.enter_context(nc.psum_tensor("ps_vec", [P, 512], F32))
        self.ps_a = ctx.enter_context(nc.psum_tensor("ps_ada", [P, 512], F32))
        self.rows_in, self.ident_ready, self.turned = m.sem("mod_rows_in"), m.sem("mod_ident_ready"), m.sem("mod_turned")
        self.cols_ready, self.silu_ready = m.sem("mod_cols_ready"), m.sem("mod_silu_ready")
        self.w_in = [m.sem(f"mod_w_in{j}") for j in range(2)]
        self.w1_in, self.w1_used = [m.sem(f"mod_w1_in{j}") for j in range(2)], m.sem("mod_w1_used")
        self.w_used, self.sums_done = m.sem("mod_w_used"), m.sem("mod_sums_done")
        self.gate_turned, self.gate_out = m.sem("mod_gate_turned"), m.sem("mod_gate_out")
        self.gate_copied = m.sem("mod_gate_copied")
        self.wflat = a["ada_w"].rearrange("l k n -> (l k) n").rearrange("(t p) n -> t p n", p=P)

    def vectors(self, block):
        m, a, nc, ps_v = self.m, self.a, self.m.nc, self.ps_v

        @block.sync
        def _(sp):
            for name, pat in (("ada_b", "l (j p) -> (l j) p"), ("norm_g", "l (j p) -> (l j) p"),
                              ("s5_d", "l (j p) -> (l j) p"), ("m_conv_w", "l t (j p) -> (l t j) p"),
                              ("m_conv_b", "l (j p) -> (l j) p"), ("m_norm_g", "l h (j p) -> (l h j) p"),
                              ("m_skip", "l (j p) -> (l j) p")):
                src = a[name].rearrange(pat, p=P)
                r = ROWS[name[2:] if name.startswith("m_conv") else name]
                sp.dma_start(self.rows[r:r + src.shape[0], :], src).then_inc(self.rows_in, 16)
            sp.dma_start(self.crow[:], a["c"].rearrange("o (j p) -> (o j) p", p=P)).then_inc(self.rows_in, 16)

        @block.gpsimd
        def _(pool):
            nc.gpsimd.memset(m.ident[:], 0.0).then_inc(self.ident_ready, 1)
            pool.wait_ge(self.ident_ready, 1)
            nc.gpsimd.affine_select(out=m.ident[:], in_=m.ident[:], compare_op=ALU.not_equal, fill=1.0,
                                    base=0, pattern=[[-1, P]], channel_multiplier=1).then_inc(self.ident_ready, 1)

        @block.tensor
        def _(pe):
            pe.wait_ge(self.rows_in, 16 * 8)
            pe.wait_ge(self.ident_ready, 2)
            nc.tensor.transpose(ps_v[:, 0:P], self.rows[:], m.ident[:])
            nc.tensor.transpose(ps_v[:, P:P + KC], self.crow[:], m.ident[0:KC, 0:KC]).then_inc(self.turned, 1)

        @block.scalar
        def _(act):
            act.wait_ge(self.turned, 1)
            nc.scalar.copy(m.cols[:], ps_v[:, 0:P]).then_inc(self.cols_ready, 1)
            nc.scalar.activation(self.cs[:], ps_v[:, P:P + KC], ACT.Silu).then_inc(self.silu_ready, 1)

    def tile(self, w, l, k):
        for n in range(24):
            mm = self.m.nc.tensor.matmul(self.ps_a[:, 24 * l + n:24 * l + n + 1], w[:, n * P:(n + 1) * P], self.cs[:, k],
                                         start=False, stop=True, skip_group_check=True)
        return mm

    def layer0(self, block):
        m, nc = self.m, self.m.nc

        @block.sync
        def _(sp):
            sp.sem_inc(self.w_used, 2)
            with sp.Fori(0, KC // 2) as i:
                for j in range(2):
                    sp.wait_ge(self.w_used, i * 2 + (j + 1))
                    sp.dma_start(self.wr[j][:], self.wflat[i * 2 + j]).then_inc(self.w_in[j], 16)

        @block.tensor
        def _(pe):
            pe.wait_ge(self.cols_ready, 1)
            pe.wait_ge(self.silu_ready, 1)
            nc.tensor.matmul(self.ps_a[:, 0:48], m.ident[:], m.cols[:, 0:48], start=True, stop=True, skip_group_check=True)
            with pe.Fori(0, KC // 2) as i:
                for j in range(2):
                    pe.wait_ge(self.w_in[j], i * 16 + 16)
                    self.tile(self.wr[j], 0, bass.ds(i * 2 + j, 1)).then_inc(self.w_used, 1)

    def load_layer1(self, sp, i, j):
        sp.wait_ge(self.w1_used, i * 2 + (j + 1))
        sp.dma_start(self.wr[j][:], self.wflat[i * 2 + (j + KC)]).then_inc(self.w1_in[j], 16)

    def layer1(self, pe, i, j):
        pe.wait_ge(self.w1_in[j], i * 16 + 16)
        self.tile(self.wr[j], 1, bass.ds(i * 2 + j, 1)).then_inc(self.w1_used, 1)

    def finish(self, block):
        m, nc, ps_v = self.m, self.m.nc, self.ps_v

        @block.vector
        def _(v):
            v.wait_ge(self.w1_used, KC + 2)
            nc.vector.tensor_copy(m.ada[:], self.ps_a[:, 0:48].rearrange("p (l j) -> p l j", l=2)).then_inc(self.cols_ready, 1)
            v.wait_ge(self.cols_ready, 2)
            nc.vector.scalar_tensor_tensor(out=m.moda[:], in0=m.ada[:, :, KC:2 * KC], scalar=1.0,
                                           in1=m.cols[:, ROWS["norm_g"]:ROWS["norm_g"] + 2 * KC].rearrange("p (l j) -> p l j", l=2),
                                           op0=ALU.add, op1=ALU.mult).then_inc(self.cols_ready, 1)

        @block.tensor
        def _(pe):
            pe.wait_ge(self.cols_ready, 2)
            nc.tensor.transpose(ps_v[0:KC, 0:P], m.ada[:, 0, 2 * KC:3 * KC], m.ident[:])
            nc.tensor.transpose(ps_v[0:KC, P:2 * P], m.ada[:, 1, 2 * KC:3 * KC], m.ident[:]).then_inc(self.gate_turned, 1)

        @block.scalar
        def _(act):
            act.wait_ge(self.gate_turned, 1)
            nc.scalar.copy(self.grow[:], ps_v[0:KC, 0:2 * P]).then_inc(self.gate_copied, 1)

        @block.sync
        def _(sp):
            sp.wait_ge(self.gate_copied, 1)
            sp.dma_start(m.gate_d.rearrange("l (j p) -> j l p", p=P),
                         self.grow[:].rearrange("j (l p) -> j l p", l=2)).then_inc(self.gate_out, 16)
            sp.wait_ge(self.gate_out, 16)


def s5_tables(m, a):
    nc = m.nc
    with ExitStack() as ctx:
        mod = Modulation(m, a, ctx)
        sb = lambda n, s, d=F32: ctx.enter_context(nc.sbuf_tensor(n, s, d))
        ab = sb("a_rows", [G, 2, P])
        are, aim = sb("a_re", [P, G]), sb("a_im", [P, G])
        dt = sb("dt", [P, G])
        bx, by = sb("b_x", [P, G, GP]), sb("b_y", [P, G, GP])
        cnat = sb("c_nat", [P, 2, KC, P])
        cx, cy = sb("c_x", [P, G, GP]), sb("c_y", [P, G, GP])
        btx, bty = sb("bt_x", [P, G, GP]), sb("bt_y", [P, G, GP])
        t = [sb(f"s5_t{j}", [P, G]) for j in range(6)]
        ti = sb("s5_ti", [P, G], I32)
        unit = [sb(f"unit_{j}", [P, G, CH + 1]) for j in range(2)]
        eb = [sb(f"eb_{j}", [P, G, 17]) for j in range(2)]
        ea = [sb(f"ea_{j}", [P, G, 17]) for j in range(2)]
        er = sb("er", [P, G, CH + 1])
        pw = [sb(f"pw_{j}", [P, G, CH + 1]) for j in range(2)]
        rv = [sb(f"rv_{j}", [P, G, CH]) for j in range(2)]
        qw = [sb(f"qw_{j}", [P, G, CH]) for j in range(3)]
        tw = [sb(f"s5_w{j}", [P, G, 8]) for j in range(4)]
        tmp = [sb(f"s5_m{j}", [P, 8, CH, GP]) for j in range(3)]
        tmq = [sb(f"s5_q{j}", [P, 8, CH, GP]) for j in range(2)]
        nx, ny, kx = (sb(n, [P, 8, CH, GP]) for n in ("n_x", "n_y", "k_x"))
        btx_s = sb("bt_x_slice", [P, 8, GP])
        pack = sb("s5_pack", [P, 8, 512])
        smal = sb("s5_small", [P, G, BW - EBC])
        kz = sb("kz", [GP, 8, 240])
        ps_t = [ctx.enter_context(nc.psum_tensor(f"ps_t{j}", [P, 4, P], F32)) for j in range(4)]
        ps_k = ctx.enter_context(nc.psum_tensor("ps_k", [P, 8, P], F32))
        a_in = m.sem("s5_a_in")
        bc_in = m.sem("s5_bc_in")
        a_turned = m.sem("s5_a_turned")
        c_turned = m.sem("s5_c_turned")
        angle_ready = m.sem("s5_angle_ready")
        unit_ready = m.sem("s5_unit_ready")
        c_ready = m.sem("s5_c_ready")
        b_ready = m.sem("s5_b_ready")
        dve = Tally(m.sem("s5_dve"))
        pool_done = Tally(m.sem("s5_pool"))
        base_ready = m.sem("s5_base_ready")
        nat_ready = m.sem("s5_nat_ready")
        nat_turned = m.sem("s5_nat_turned")
        kz_zeroed = m.sem("s5_kz_zeroed")
        ps_free = m.sem("s5_ps_free")
        nat_free = m.sem("s5_nat_free")
        out_mats_ready = m.sem("s5_out_mats_ready")
        stored = m.sem("s5_stored")
        out_stored = [m.sem(f"s5_out_stored{n}") for n in range(2)]
        small_stored = m.sem("s5_small_stored")

        with nc.Block() as block:
            mod.vectors(block)

            @block.sync
            def _(sp):
                for j, n in enumerate(("s5_a_re", "s5_a_im")):
                    for h in range(2):
                        sp.dma_start(ab[:, j, h * NS:(h + 1) * NS], a[n][0]).then_inc(a_in, 16)
                sp.dma_start(dt[:], a["s5_log_dt"].broadcast_to([P, G])).then_inc(a_in, 16)
                cre = a["s5_c_re"].rearrange("o g p n -> (o g p) n").rearrange("(j r) n -> r j n", r=P)
                cim = a["s5_c_im"].rearrange("o g p n -> (o g p) n").rearrange("(j r) n -> r j n", r=P)
                for w, halves in enumerate(((cre, cim), (cim, cre))):
                    for h in range(2):
                        sp.dma_start(cnat[:, w, :, h * NS:(h + 1) * NS], halves[h]).then_inc(bc_in, 16)
                bre = a["s5_b_re"].rearrange("o g n p -> (o n) g p")
                bim = a["s5_b_im"].rearrange("o g n p -> (o n) g p")
                sp.dma_start(bx[0:NS], bre).then_inc(bc_in, 16)
                sp.dma_start(bx[NS:P], bim).then_inc(bc_in, 16)
                sp.dma_start(by[0:NS], bim).then_inc(bc_in, 16)
                sp.dma_start(by[NS:P], bre).then_inc(bc_in, 16)

            @block.tensor
            def _(pe):
                pe.wait_ge(a_in, 16 * 5)
                nc.tensor.transpose(ps_k[:, 0, 0:G], ab[:, 0, :], m.ident[0:G, 0:G])
                nc.tensor.transpose(ps_k[:, 1, 0:G], ab[:, 1, :], m.ident[0:G, 0:G]).then_inc(a_turned, 1)
                pe.wait_ge(bc_in, 16 * 8)
                for w in range(2):
                    for j in range(KC):
                        tr = nc.tensor.transpose(ps_t[2 * w + j // 4][:, j % 4, :], cnat[:, w, j, :], m.ident[:])
                        if j % 4 == 3:
                            tr.then_inc(c_turned, 1)

            mod.layer0(block)

            @block.sync
            def _(sp):
                sp.wait_ge(base_ready, 1)
                sp.dma_start(m.s5w_d[:, :, EBC:BW].rearrange("g p w -> p g w"), smal[:]).then_inc(small_stored, 16)
                sp.sem_inc(stored, 32)
                for n in range(2):
                    sp.sem_inc(out_stored[n], 16)
                sp.wait_ge(mod.w_used, KC + 2)
                sp.sem_inc(mod.w1_used, 2)

                def store(i):
                    part = lambda lo, hi: (m.s5w_d[bass.ds(i * 8, 8), :, lo:hi].rearrange("g p w -> p g w"), pack[:, :, lo:hi])
                    for n, lo in enumerate((COC, COS)):
                        sp.wait_ge(out_mats_ready, i * 2 + (n + 1))
                        sp.dma_start(*part(lo, lo + P)).then_inc(out_stored[n], 16)
                    sp.wait_ge(ps_free, i * 5 + 10)
                    sp.dma_start(m.kz_d[bass.ds(i * 8, 8)].rearrange("g p w -> p g w"), kz[:]).then_inc(stored, 16)
                    sp.dma_start(*part(BIN, COC)).then_inc(stored, 16)

                mod.load_layer1(sp, 0, 0)
                with sp.Fori(0, KC // 2 - 1) as i:
                    for j in range(2):
                        mod.load_layer1(sp, i + j, 1 - j)
                        store(i * 2 + j)
                mod.load_layer1(sp, KC // 2 - 1, 1)
                store(KC - 2)
                store(KC - 1)
                sp.wait_ge(stored, 32 * (KC + 1))
                for n in range(2):
                    sp.wait_ge(out_stored[n], 16 * (KC + 1))
                sp.wait_ge(small_stored, 16)

            @block.scalar
            def _(act):
                act.wait_ge(angle_ready, 1)
                nc.scalar.activation(unit[1][:, :, 1], t[1][:], ACT.Sin)
                nc.scalar.activation(unit[0][:, :, 1], t[2][:], ACT.Sin).then_inc(unit_ready, 1)
                for w, dst in ((0, cx), (1, cy)):
                    for j in range(2):
                        act.wait_ge(c_turned, 2 * w + j + 1)
                        nc.scalar.copy(dst[:, 32 * j:32 * (j + 1), :].rearrange("p (a b) c -> p a (b c)", b=8),
                                       ps_t[2 * w + j][:]).then_inc(c_ready, 1)
                act.wait_ge(c_ready, 4)
                nc.scalar.mul(cx[NS:P], cx[NS:P], -1.0).then_inc(c_ready, 1)
                act.wait_ge(bc_in, 16 * 8)
                nc.scalar.mul(by[0:NS], by[0:NS], -1.0).then_inc(b_ready, 1)
                act.wait_ge(kz_zeroed, 1)
                with act.Fori(0, KC) as i:
                    act.wait_ge(stored, (i + 1) * 32)
                    for h in range(4):
                        act.wait_ge(nat_turned, i * 4 + (h + 1))
                        w, j = h // 2, h % 2
                        nc.scalar.copy(pack[:, 4 * j:4 * j + 4, w * P:(w + 1) * P], ps_t[h][:]).then_inc(ps_free, 1)
                    act.wait_ge(nat_free, i + 2)
                    nc.scalar.copy(kz[:, :, 112:240], ps_k[0:GP]).then_inc(ps_free, 1)

            @block.gpsimd
            def _(pool):
                nc.gpsimd.memset(kz[:], 0.0).then_inc(kz_zeroed, 1)
                pool.wait_ge(base_ready, 2)
                pool.wait_ge(c_ready, 5)
                qr, qi, nq = (q[:] for q in qw)
                with pool.Fori(0, KC) as i:
                    pool_done.enter(i, 6)
                    g8 = bass.ds(i * 8, 8)
                    x = lambda tab: tab[:, g8, :].unsqueeze(3).broadcast_to([P, 8, CH, GP])
                    c = lambda arr: arr[:, g8, :].unsqueeze(2).broadcast_to([P, 8, CH, GP])
                    v4 = lambda lo: pack[:, :, lo:lo + P].rearrange("p g (l q) -> p g l q", l=CH)
                    for n, (lo, e, A, B) in enumerate(((COC, qr, cx, cy), (COS, nq, cy, cx))):
                        pool_done.add(nc.gpsimd.tensor_tensor(tmq[0][:], x(e), c(A), ALU.mult))
                        done = pool_done.add(nc.gpsimd.tensor_tensor(tmq[1][:], x(qi), c(B), ALU.mult))
                        pool.wait_ge(out_stored[n], i * 16 + 16)
                        pool.wait_ge(pool_done.sem, done)
                        done = pool_done.add(nc.gpsimd.tensor_tensor(v4(lo), tmq[0][:], tmq[1][:], ALU.subtract))
                        pool.wait_ge(pool_done.sem, done)
                        pool.sem_inc(out_mats_ready, 1)
                pool_done.leave(KC)

            @block.vector
            def _(v):
                def L(ins):
                    v.wait_ge(dve.sem, dve.add(ins))

                tt = nc.vector.tensor_tensor
                ts = nc.vector.tensor_scalar
                stt = nc.vector.scalar_tensor_tensor
                v.wait_ge(a_turned, 1)
                L(nc.vector.tensor_copy(are[:], ps_k[:, 0, 0:G]))
                L(nc.vector.tensor_copy(aim[:], ps_k[:, 1, 0:G]))

                def exp(dst, x):
                    exp_steps(nc, L, dst, x, t[4][:], t[5][:], ti[:])

                exp(dt[:], dt[:])
                L(tt(t[0][:], are[:], dt[:], ALU.mult))
                exp(er[:, :, 1], t[0][:])
                L(tt(t[3][:], aim[:], dt[:], ALU.mult))
                L(ts(t[4][:], t[3][:], 1.0 / TWO_PI, ROUND, ALU.mult, ALU.add))
                L(ts(t[4][:], t[4][:], ROUND, None, ALU.subtract))
                for c in TWO_PI_PARTS:
                    L(stt(out=t[3][:], in0=t[4][:], scalar=-c, in1=t[3][:], op0=ALU.mult, op1=ALU.add))
                L(ts(t[1][:], t[3][:], PI_SAFE, -PI_SAFE, ALU.min, ALU.max))
                L(ts(t[4][:], t[3][:], math.pi / 2, -TWO_PI, ALU.is_gt, ALU.mult))
                L(stt(out=t[2][:], in0=t[3][:], scalar=math.pi / 2, in1=t[4][:], op0=ALU.add, op1=ALU.add))
                L(ts(t[2][:], t[2][:], PI_SAFE, -PI_SAFE, ALU.min, ALU.max))
                v.sem_inc(angle_ready, 1)
                for tab in (unit, eb, ea):
                    L(nc.vector.memset(tab[0][:, :, 0:1], 1.0))
                    L(nc.vector.memset(tab[1][:, :, 0:1], 0.0))
                L(nc.vector.memset(er[:, :, 0:1], 1.0))
                L(nc.vector.memset(smal[:], 0.0))
                v.wait_ge(unit_ready, 1)

                def renorm(tab, lo, hi):
                    c, s = (q[:, :, lo:hi] for q in tab)
                    w0, w1 = (q[:, :, 0:hi - lo] for q in tw[2:4])
                    L(tt(w0, c, c, ALU.mult))
                    L(tt(w1, s, s, ALU.mult))
                    L(tt(w0, w0, w1, ALU.add))
                    L(ts(w0, w0, -0.5, 1.5, ALU.mult, ALU.add))
                    L(tt(c, c, w0, ALU.mult))
                    L(tt(s, s, w0, ALU.mult))

                def double(tab, top):
                    n = 1
                    while n < top:
                        lo, hi = n + 1, 2 * n + 1
                        c, s = (q[:, :, 1:n + 1] for q in tab)
                        c2_, s2_ = (q[:, :, n:n + 1].broadcast_to([P, G, n]) for q in tab)
                        oc, os_ = (q[:, :, lo:hi] for q in tab)
                        w = [q[:, :, 0:n] for q in tw]
                        L(tt(w[0], c, c2_, ALU.mult))
                        L(tt(w[1], s, s2_, ALU.mult))
                        L(tt(w[2], c, s2_, ALU.mult))
                        L(tt(w[3], s, c2_, ALU.mult))
                        L(tt(oc, w[0], w[1], ALU.subtract))
                        L(tt(os_, w[2], w[3], ALU.add))
                        renorm(tab, lo, hi)
                        n *= 2

                renorm(unit, 1, 2)
                double(unit, 8)
                for j in range(2):
                    L(nc.vector.tensor_copy(eb[j][:, :, 1:2], unit[j][:, :, 8:9]))
                double(eb, 16)
                for j in range(2):
                    L(nc.vector.tensor_copy(ea[j][:, :, 1:2], eb[j][:, :, 16:17]))
                double(ea, 16)
                for n in (1, 2, 4):
                    L(tt(er[:, :, n + 1:2 * n + 1], er[:, :, 1:n + 1], er[:, :, n:n + 1].broadcast_to([P, G, n]), ALU.mult))
                for j in range(2):
                    L(tt(pw[j][:], er[:], unit[j][:], ALU.mult))
                    L(nc.vector.tensor_copy(smal[:, :, 16 * j:16 * j + 16], eb[j][:, :, 0:16]))
                    L(nc.vector.tensor_copy(smal[:, :, 32 + 16 * j:48 + 16 * j], ea[j][:, :, 0:16]))
                nc.vector.tensor_copy(smal[:, :, 64:65], er[:, :, 8:9]).then_inc(base_ready, 1)
                for j in range(2):
                    for i in range(CH):
                        L(nc.vector.tensor_copy(rv[j][:, :, i:i + 1], pw[j][:, :, CH - 1 - i:CH - i]))
                c = eb[0][:, :, 1:2].broadcast_to([P, G, CH])
                s = eb[1][:, :, 1:2].broadcast_to([P, G, CH])
                pr, pi = pw[0][:, :, 1:CH + 1], pw[1][:, :, 1:CH + 1]
                L(tt(tw[0][:], pr, c, ALU.mult))
                L(tt(tw[1][:], pi, s, ALU.mult))
                L(tt(tw[2][:], pi, c, ALU.mult))
                L(tt(tw[3][:], pr, s, ALU.mult))
                L(tt(qw[0][:], tw[0][:], tw[1][:], ALU.add))
                L(tt(qw[1][:], tw[2][:], tw[3][:], ALU.subtract))
                ts(qw[2][:], qw[0][:], -1.0, None, ALU.mult).then_inc(base_ready, 1)
                L(ts(t[0][:], pw[0][:, :, 1], -1.0, None, ALU.add))
                L(tt(t[1][:], are[:], are[:], ALU.mult))
                L(tt(t[2][:], aim[:], aim[:], ALU.mult))
                L(tt(t[1][:], t[1][:], t[2][:], ALU.add))
                L(nc.vector.reciprocal(t[5][:], t[1][:]))
                p1 = pw[1][:, :, 1]
                L(tt(t[1][:], t[0][:], are[:], ALU.mult))
                L(tt(t[2][:], p1, aim[:], ALU.mult))
                L(tt(t[1][:], t[1][:], t[2][:], ALU.add))
                L(tt(t[1][:], t[1][:], t[5][:], ALU.mult))
                L(tt(t[2][:], p1, are[:], ALU.mult))
                L(tt(t[3][:], t[0][:], aim[:], ALU.mult))
                L(tt(t[2][:], t[2][:], t[3][:], ALU.subtract))
                L(tt(t[2][:], t[2][:], t[5][:], ALU.mult))
                v.wait_ge(b_ready, 1)
                wr, wi = (t[j][:].unsqueeze(2).broadcast_to([P, G, GP]) for j in (1, 2))
                s0 = nx[:].rearrange("p a b c -> p (a b) c")
                s1 = ny[:].rearrange("p a b c -> p (a b) c")
                L(tt(s0, wr, bx[:], ALU.mult))
                L(tt(s1, wi, by[:], ALU.mult))
                L(tt(btx[:], s0, s1, ALU.add))
                L(tt(s0, wr, by[:], ALU.mult))
                L(tt(s1, wi, bx[:], ALU.mult))
                L(tt(bty[:], s0, s1, ALU.subtract))
                v.wait_ge(c_ready, 5)
                with v.Fori(0, KC) as i:
                    dve.enter(i, 7)
                    g8 = bass.ds(i * 8, 8)
                    x = lambda tab, lo, hi: tab[:, g8, lo:hi].unsqueeze(3).broadcast_to([P, 8, CH, GP])
                    c = lambda arr: arr[:, g8, :].unsqueeze(2).broadcast_to([P, 8, CH, GP])
                    v.wait_ge(nat_free, i + 1)
                    for o, A, B, op in ((nx, btx, bty, ALU.add), (ny, bty, btx, None)):
                        dve.add(tt(tmp[0][:], x(rv[0], 0, CH), c(A), ALU.mult))
                        L(tt(tmp[1][:], x(rv[1], 0, CH), c(B), ALU.mult))
                        if op is None:
                            tt(o[:], tmp[1][:], tmp[0][:], ALU.subtract).then_inc(nat_ready, 1)
                        else:
                            tt(o[:], tmp[0][:], tmp[1][:], op).then_inc(nat_ready, 1)
                        v.wait_ge(nat_ready, i * 3 + (1 if op is ALU.add else 2))
                    dve.add(tt(tmp[0][:], x(pw[0], 0, CH), c(cx), ALU.mult))
                    dve.add(nc.vector.tensor_copy(btx_s[:], btx[:, g8, :]))
                    L(tt(tmp[1][:], x(pw[1], 0, CH), c(cy), ALU.mult))
                    tt(kx[:], tmp[0][:], tmp[1][:], ALU.subtract).then_inc(nat_ready, 1)
                    v.wait_ge(nat_ready, i * 3 + 3)
                dve.leave(KC)

            @block.tensor
            def _(pe):
                pe.sem_inc(nat_free, 1)
                pe.wait_ge(c_ready, 4)
                pe.wait_ge(angle_ready, 1)
                pe.sem_inc(ps_free, 5)
                with pe.Fori(0, KC // 2) as i2:
                    for half in range(2):
                        i = i2 * 2 + half
                        for h in range(4):
                            w, j = h // 2, h % 2
                            pe.wait_ge(nat_ready, i * 3 + (w + 1))
                            pe.wait_ge(ps_free, i * 5 + (h + 1))
                            for g in range(4):
                                tr = nc.tensor.transpose(ps_t[h][:, g, :], (nx, ny)[w][:, 4 * j + g].rearrange("p a b -> p (a b)"), m.ident[:])
                            tr.then_inc(nat_turned, 1)
                        pe.wait_ge(nat_ready, i * 3 + 3)
                        pe.wait_ge(ps_free, i * 5 + 5)
                        for g in range(8):
                            mm = nc.tensor.matmul(ps_k[0:GP, g, :], btx_s[:, g, :], kx[:, g].rearrange("p a b -> p (a b)"),
                                                  start=True, stop=True)
                        mm.then_inc(nat_free, 1)
                        mod.layer1(pe, i2, half)

            mod.finish(block)


def norm_transposed(m, a):
    nc = m.nc
    with ExitStack() as ctx:
        sb = lambda n, s: ctx.enter_context(nc.sbuf_tensor(n, s, F32))
        xt = [sb(f"n_x{j}", [P, D]) for j in range(2)]
        xs = [sb(f"n_scaled{j}", [P, D]) for j in range(2)]
        junk = [sb(f"n_junk{j}", [P, D]) for j in range(2)]
        xf = [sb(f"n_f{j}", [P, KC, P]) for j in range(2)]
        st = sb("n_stat", [P, 5, 2])
        ps = [ctx.enter_context(nc.psum_tensor(f"n_ps{j}", [P, KC, P], F32)) for j in range(2)]
        x_in = [m.sem(f"n_x_in{j}") for j in range(2)]
        root = Tally(m.sem("n_root"))
        squared, mean_ready, root_ready, scaled, turned, evacuated, evacuated2, split, hi_done = (
            m.sem(f"n_{n}") for n in "squared mean_ready root_ready scaled turned evacuated evacuated2 split hi_done".split())
        xv = a["x"].rearrange("o (t p) d -> (o t) p d", p=P)
        HALF = KC // 2
        toe_stored = m.sem("s5_toe_stored")
        assert TT // 2 == CH
        with nc.Block() as block:
            @block.sync
            def _(sp):
                sp.sem_inc(scaled, 2)
                with sp.Fori(0, TT // 2) as i:
                    t = i * 2
                    for j in range(2):
                        sp.wait_ge(scaled, t + (j + 1))
                        sp.dma_start(xt[j][:], xv[t + j]).then_inc(x_in[j], 16)
                    sp.dma_start(m.s5w_d.rearrange("g (r p) w -> r g p w", p=GP)[i, :, :, TOE:TOE + P],
                                 m.kz_d[:, :, bass.ds(i * (-GP) + 112, P)]).then_inc(toe_stored, 16)
                sp.wait_ge(toe_stored, 16 * CH)

            @block.scalar
            def _(act):
                def squares(i):
                    for j in range(2):
                        act.wait_ge(x_in[j], i * 16 + 16)
                        nc.scalar.activation(junk[j][:], xt[j][:], ACT.Square, accum_out=st[:, 0, j:j + 1]).then_inc(squared, 1)

                def roots(i):
                    act.wait_ge(mean_ready, i + 1)
                    nc.scalar.activation(st[:, 2, :], st[:, 1, :], ACT.Sqrt).then_inc(root_ready, 1)

                def evacuate(i):
                    for j in range(2):
                        act.wait_ge(turned, i * 2 + (j + 1))
                        act.wait_ge(split, i * 2 + (j + 1))
                        for c in range(HALF):
                            last = nc.scalar.activation(xf[j][:, c, :], ps[j][:, c, :], ACT.Identity,
                                                        scale=m.moda[:, 0, c:c + 1], bias=m.ada[:, 0, c:c + 1])
                        last.then_inc(evacuated, 1)

                squares(0)
                roots(0)
                with act.Fori(0, TT // 2 - 1) as i:
                    evacuate(i)
                    squares(i + 1)
                    roots(i + 1)
                evacuate(TT // 2 - 1)

            @block.vector
            def _(v):
                def L(ins):
                    v.wait_ge(root.sem, root.add(ins))

                ts = nc.vector.tensor_scalar

                def means(i):
                    v.wait_ge(squared, i * 2 + 2)
                    ts(st[:, 1, :], st[:, 0, :], 1.0 / D, EPS, ALU.mult, ALU.add).then_inc(mean_ready, 1)

                def scales(i):
                    v.wait_ge(root_ready, i + 1)
                    v.wait_ge(mean_ready, i + 1)
                    rsqrt_steps(nc, L, st[:, 1, :], st[:, 2, :], st[:, 3, :], st[:, 4, :])
                    for j in range(2):
                        ts(xs[j][:], xt[j][:], st[:, 3, j:j + 1], None, ALU.mult).then_inc(scaled, 1)

                def split_pair(i):
                    for j in range(2):
                        v.wait_ge(turned, i * 2 + (j + 1))
                        for c in range(HALF, KC):
                            last = ts(xf[j][:, c, :], ps[j][:, c, :], m.moda[:, 0, c:c + 1], m.ada[:, 0, c:c + 1], ALU.mult, ALU.add)
                        last.then_inc(evacuated2, 1)
                        v.wait_ge(evacuated, i * 2 + (j + 1))
                        v.wait_ge(evacuated2, i * 2 + (j + 1))
                        at = bass.ds((i * 2 + j) * P, P)
                        nc.vector.tensor_copy(m.hT[:, 0, :, at], xf[j][:]).then_inc(hi_done, 1)
                        v.wait_ge(hi_done, i * 2 + (j + 1))
                        nc.vector.tensor_tensor(m.hT[:, 1, :, at], xf[j][:], m.hT[:, 0, :, at].bitcast(F32), ALU.subtract).then_inc(split, 1)

                v.sem_inc(split, 2)
                means(0)
                scales(0)
                with v.Fori(0, TT // 2 - 1) as i:
                    root.enter(i, 4)
                    split_pair(i)
                    means(i + 1)
                    scales(i + 1)
                root.leave(TT // 2 - 1)
                split_pair(TT // 2 - 1)

            @block.tensor
            def _(pe):
                with pe.Fori(0, TT // 2) as i:
                    t = i * 2
                    for j in range(2):
                        pe.wait_ge(scaled, t + (j + 3))
                        pe.wait_ge(split, t + (j + 1))
                        for c in range(KC):
                            tr = nc.tensor.transpose(ps[j][:, c, :], xs[j][:, c * P:(c + 1) * P], m.ident[:])
                        tr.then_inc(turned, 1)


def split_weights_hi(nc, act, raw, w):
    return nc.scalar.copy(w[:, 0], raw[:])


def split_weights_lo(nc, raw, w):
    return nc.vector.tensor_tensor(w[:, 1], raw[:], w[:, 0].bitcast(F32), ALU.subtract)


def split_product(nc, out, w, x, n=KC):
    for k in range(n):
        nc.tensor.matmul(out, w(0, k), x(0, k), start=(k == 0), stop=False)
        nc.tensor.matmul(out, w(0, k), x(1, k), start=False, stop=False)
        last = nc.tensor.matmul(out, w(1, k), x(0, k), start=False, stop=(k == n - 1))
    return last


def project(m, a):
    nc = m.nc
    with ExitStack() as ctx:
        sb = lambda n, s, d=F32: ctx.enter_context(nc.sbuf_tensor(n, s, d))
        raw = sb("w_raw", [P, KC, P])
        whl = [sb(f"w_hl{j}", [P, 2, KC, P], F32R) for j in range(3)]
        stage = [sb(f"stage{j}", [P, BT]) for j in range(2)]
        mb = [sb(f"m_blk{j}", [P, 3 + BT]) for j in range(2)]
        acc = sb("conv_acc", [P, BT])
        xst = [sb(f"xc_blk{j}", [P, BT]) for j in range(2)]
        wif = sb("w_if_tile", [P, 2, 2 * MH])
        cvec = sb("conv_vec", [P, 5])
        us = [sb(f"s5_u{j}", [P, NCH]) for j in range(2)]
        wt = [sb(f"s5_wt{j}", [P, BW]) for j in range(2)]
        cosk = [sb(f"s5_cos{j}", [P, NCH]) for j in range(2)]
        sink = [sb(f"s5_sin{j}", [P, NCH]) for j in range(2)]
        pt = [sb(f"s5_pt{j}", [P, NCH]) for j in range(2)]
        wa, wb = sb("s5_wa", [P, NCH]), sb("s5_wb", [P, NCH])
        zz = sb("s5_z", [P, NCH + 1])
        cz = [sb(f"s5_cz{j}", [P, 2, NCH]) for j in range(2)]
        yo = [sb(f"s5_yo{j}", [P, NCH]) for j in range(2)]
        pg = [ctx.enter_context(nc.psum_tensor(f"pg{j}", [P, BT], F32)) for j in range(3)]
        pv = [ctx.enter_context(nc.psum_tensor(f"pv{j}", [P, 2, NCH], F32)) for j in range(2)]
        py = [ctx.enter_context(nc.psum_tensor(f"py{j}", [P, 512], F32)) for j in range(2)]
        pgate = ctx.enter_context(nc.psum_tensor("pgate", [P, BT], F32))
        pg1 = [p[:] for p in pg] + [pv[0][:].rearrange("p a b -> p (a b)")]

        w1_in, w1_hi, w1_lo = m.sem("p1_w_in"), m.sem("p1_w_hi"), m.sem("p1_w_lo")
        u_done, u_read = m.sem("p1_done"), m.sem("p1_read")
        u_out = [m.sem(f"p1_out{j}") for j in range(2)]
        w_in, w_hi, w_lo = m.sem("p2_w_in"), m.sem("p2_w_hi"), m.sem("p2_w_lo")
        gemm_done = m.sem("p2_done")
        bank_free = [m.sem(f"p2_bank_free{j}") for j in range(3)]
        st_out = [m.sem(f"p2_stage_out{j}") for j in range(2)]
        st_ready = m.sem("p2_stage_ready")
        conv = m.sem("p2_conv")
        conv_free = m.sem("p2_conv_free")
        m_out = [m.sem(f"p2_m_out{j}") for j in range(2)]
        xc_out = [m.sem(f"p2_xc_out{j}") for j in range(2)]
        wif_in = m.sem("p2_wif_in")
        gate_done, gate_added = m.sem("p2_gate_done"), m.sem("p2_gate_added")
        s5_in = [m.sem(f"s5_in{j}") for j in range(2)]
        v_done, y_done = m.sem("s5_v_done"), m.sem("s5_y_done")
        table = Tally(m.sem("s5_table"))
        step = Tally(m.sem("p2_step"))
        z_turned = m.sem("s5_z_turned")
        v_read = m.sem("s5_v_read")
        y_read = m.sem("s5_y_read")
        y_out = [m.sem(f"s5_y_out{j}") for j in range(2)]

        w_cols = a["ev_w_in"][0].rearrange("(k p) n -> p k n", p=P)
        plan = []
        for n in range(12):
            groups = [s for s in range(8) if 3 * s // 2 == n]
            plan += [("in", s) for s in groups] + [("gemm", n)]
            if 5 <= n <= 8:
                plan.append(("gate", n - 5))
            plan += [("out", s) for s in groups]

        def u_rows(dram, i, s):
            return dram.rearrange("(g p) b j k -> g p b j k", p=GP)[i * 8 + s].rearrange("p b j k -> j p b k")

        def perm(ap):
            return ap.rearrange("p (k j) -> p j k", j=CH)

        with nc.Block() as block:
            @block.sync
            def _(sp):
                sp.sem_inc(w1_lo, 1)
                with sp.Fori(0, KC) as n:
                    sp.wait_ge(w1_lo, n + 1)
                    sp.dma_start(raw[:], w_cols[:, :, bass.ds(n * P, P)]).then_inc(w1_in, 16)
                sp.wait_ge(w1_lo, KC + 1)
                sp.dma_start(raw[:], w_cols[:, :, D:D + P]).then_inc(w1_in, 16)
                sp.sem_inc(w_in, 16)
                for j in range(2):
                    sp.wait_ge(u_out[j], 16 * (2 * KC + 1))
                with sp.Fori(0, KC) as i:
                    sp.wait_ge(gate_done, i * 4 + 2)
                    w2 = a["m_w_if"][0].rearrange("(h k p) n -> k p h n", h=2, p=P)
                    sp.dma_start(wif[:], w2[i]).then_inc(wif_in, 16)
                    for what, n in plan:
                        if what == "in":
                            sp.wait_ge(y_done, i * 8 + (n + 1))
                            q = n % 2
                            sp.dma_start(us[q][:].rearrange("r (b k) -> r b k", b=NB), u_rows(m.u_d, i, n)).then_inc(s5_in[q], 16)
                            sp.dma_start(wt[q][:], m.s5w_d[i * 8 + n]).then_inc(s5_in[q], 16)
                        if what == "gemm" and n % 4 == 0:
                            sp.wait_ge(w_lo, i * 3 + (n // 4 + 1))
                            col = i * P + (2 * D, 3 * D, D + P)[n // 4]
                            sp.dma_start(raw[:], w_cols[:, :, bass.ds(col, P)]).then_inc(w_in, 16)
                sp.wait_ge(w_in, 16 * (3 * KC + 1))

            @block.scalar
            def _(act):
                for j in range(2):
                    act.sem_inc(u_out[j], 16)
                    act.sem_inc(st_out[j], 16)
                    act.sem_inc(m_out[j], 16)
                    act.sem_inc(xc_out[j], 16)
                    act.sem_inc(y_out[j], 16)
                act.wait_ge(w1_in, 16)
                split_weights_hi(nc, act, raw, whl[0]).then_inc(w1_hi, 1)
                with act.Fori(0, KC // 2) as i:
                    for j in range(2):
                        for b in range(NB):
                            if b == 1:
                                act.wait_ge(w1_in, i * 32 + 16 * (j + 2))
                                act.wait_ge(u_done, i * 8 + 4 * (j + 2))
                                split_weights_hi(nc, act, raw, whl[1 - j]).then_inc(w1_hi, 1)
                            act.wait_ge(u_done, i * 8 + (4 * j + b + 1 + 8))
                            act.wait_ge(u_out[b % 2], i * 64 + 16 * (2 * j + b // 2 + 1))
                            nc.scalar.copy(stage[b % 2][:].rearrange("p (j k) -> p j k", j=CH), perm(pg1[b])).then_inc(u_read, 1)
                            act.wait_ge(u_read, i * 8 + (4 * j + b + 1 + 4))
                            act.dma_start(m.u_d.rearrange("(t p) b j k -> t p b (j k)", p=P)[i * 2 + j, :, b],
                                          stage[b % 2][:]).then_inc(u_out[b % 2], 16)
                for j in range(2):
                    act.wait_ge(u_out[j], 16 * (2 * KC + 1))
                act.wait_ge(u_done, 8 + 32)
                with act.Fori(0, KC) as i:
                    for what, n in plan:
                        if what == "gemm":
                            sec, b = n // 4, n % 4
                            if b == 0:
                                act.wait_ge(w_in, i * 48 + 16 * (sec + 2))
                                act.wait_ge(gemm_done, i * 12 + (8, 12, 16)[sec])
                                split_weights_hi(nc, act, raw, whl[(sec + 1) % 3]).then_inc(w_hi, 1)
                            if sec == 1:
                                act.wait_ge(conv, i * 4 + (b + 2))
                                act.wait_ge(xc_out[b % 2], i * 32 + 16 * (b // 2 + 1))
                                act.wait_ge(gate_done, i * 4 + (b + 1))
                                nc.scalar.activation(xst[b % 2][:], acc[:], ACT.Silu).then_inc(conv_free, 1)
                                act.dma_start(m.m_d.rearrange("(t p) (b n) -> t p b n", p=P, b=NB)[i, :, b],
                                              mb[b % 2][:, 3:3 + BT]).then_inc(m_out[b % 2], 16)
                                act.wait_ge(conv_free, i * 4 + (b + 2))
                                act.dma_start(m.xc_d.rearrange("(t p) (b n) -> t p b n", p=P, b=NB)[i, :, b],
                                              xst[b % 2][:]).then_inc(xc_out[b % 2], 16)
                            else:
                                act.wait_ge(gemm_done, i * 12 + (n + 1 + 12))
                                at = 0 if sec == 0 else 2
                                act.wait_ge(st_out[b % 2], i * 64 + 16 * (at + b // 2 + 1))
                                if sec == 0:
                                    ins = nc.scalar.activation(stage[b % 2][:].rearrange("p (j k) -> p j k", j=CH),
                                                               perm(pg[n % 3][:]), ACT.Silu)
                                    dst = m.sz_d.rearrange("(t p) b j k -> t p b (j k)", p=P)[i, :, b]
                                else:
                                    ins = nc.scalar.activation(stage[b % 2][:], pg[n % 3][:], ACT.Silu)
                                    dst = m.smz_d.rearrange("(t p) (b n) -> t p b n", p=P, b=NB)[i, :, b]
                                ins.then_inc(bank_free[n % 3], 1)
                                act.wait_ge(bank_free[n % 3], i * 4 + (n // 3 + 2))
                                act.dma_start(dst, stage[b % 2][:]).then_inc(st_out[b % 2], 16)
                        if what == "out":
                            q = n % 2
                            act.wait_ge(y_done, i * 8 + (n + 1 + 2))
                            act.wait_ge(y_out[q], i * 64 + 16 * (n // 2 + 1))
                            nc.scalar.copy(yo[q][:], py[q][:, 0:NCH]).then_inc(y_read, 1)
                            act.wait_ge(y_read, i * 8 + (n + 3))
                            act.dma_start(u_rows(m.y_d, i, n), yo[q][:].rearrange("r (b k) -> r b k", b=NB)).then_inc(y_out[q], 16)
                for j in range(2):
                    act.wait_ge(st_out[j], 16 * (4 * KC + 1))
                    act.wait_ge(m_out[j], 16 * (2 * KC + 1))
                    act.wait_ge(xc_out[j], 16 * (2 * KC + 1))
                    act.wait_ge(y_out[j], 16 * (4 * KC + 1))

            @block.gpsimd
            def _(pool):
                nc.gpsimd.memset(m.gacc[:], 0.0).then_inc(gate_added, 1)
                pool.sem_inc(z_turned, 2)
                with pool.Fori(0, KC) as i:
                    table.enter(i, 6 * 8)
                    for s in range(8):
                        q = s % 2
                        pool.wait_ge(s5_in[q], i * 128 + 32 * (s // 2 + 1))
                        pool.wait_ge(z_turned, i * 8 + (s + 1))
                        v3 = lambda ap: ap.rearrange("p (x y) -> p x y", y=16)
                        lo = lambda c: wt[q][:, c:c + 16].unsqueeze(1).broadcast_to([P, 16, 16])
                        hi = lambda c: wt[q][:, c:c + 16].unsqueeze(2).broadcast_to([P, 16, 16])
                        for dst, t0, t1, op in ((cosk[q], (EAC, EBC), (EAS, EBS), ALU.subtract),
                                                (sink[q], (EAS, EBC), (EAC, EBS), ALU.add)):
                            table.add(nc.gpsimd.tensor_tensor(v3(pt[0][:]), hi(t0[0]), lo(t0[1]), ALU.mult))
                            done = table.add(nc.gpsimd.tensor_tensor(v3(pt[1][:]), hi(t1[0]), lo(t1[1]), ALU.mult))
                            pool.wait_ge(table.sem, done)
                            done = table.add(nc.gpsimd.tensor_tensor(dst[:], pt[0][:], pt[1][:], op))
                            pool.wait_ge(table.sem, done)
                table.leave(KC)

            @block.vector
            def _(v):
                tt, stt, ts = nc.vector.tensor_tensor, nc.vector.scalar_tensor_tensor, nc.vector.tensor_scalar

                def L(ins):
                    v.wait_ge(step.sem, step.add(ins))

                L(nc.vector.memset(zz[:, 0:1], 0.0))
                v.sem_inc(conv_free, 1)
                v.sem_inc(conv, 1)
                v.sem_inc(y_read, 2)
                v.sem_inc(v_read, 2)
                for j in range(3):
                    v.sem_inc(bank_free[j], 1)
                with v.Fori(0, KC // 2) as i:
                    for j in range(2):
                        v.wait_ge(w1_hi, i * 2 + (j + 1))
                        split_weights_lo(nc, raw, whl[j]).then_inc(w1_lo, 1)
                v.wait_ge(w1_hi, KC + 1)
                split_weights_lo(nc, raw, whl[0]).then_inc(w1_lo, 1)
                v.wait_ge(w1_lo, KC + 2)
                v.sem_inc(w_hi, 1)
                v.sem_inc(w_lo, 1)
                with v.Fori(0, KC) as i:
                    step.enter(i, 1 + 4 * 4 + 8 * 4)
                    v.wait_ge(conv, i * 4 + 1)
                    L(nc.vector.tensor_copy(cvec[:], m.cols[:, ROWS["conv_w"]:ROWS["conv_w"] + 40]
                                            .rearrange("p (t j) -> p j t", j=KC)[:, i]))
                    for what, n in plan:
                        if what == "gemm":
                            sec, b = n // 4, n % 4
                            if b == 0:
                                v.wait_ge(w_hi, i * 3 + (sec + 2))
                                split_weights_lo(nc, raw, whl[(sec + 1) % 3]).then_inc(w_lo, 1)
                            if sec == 1:
                                cur = mb[b % 2]
                                v.wait_ge(gemm_done, i * 12 + (n + 1 + 12))
                                v.wait_ge(m_out[b % 2], i * 32 + 16 * (b // 2 + 1))
                                v.wait_ge(gate_done, i * 4 + (b + 1))
                                if b == 0:
                                    step.add(nc.vector.memset(cur[:, 0:3], 0.0))
                                else:
                                    step.add(nc.vector.tensor_copy(cur[:, 0:3], mb[(b + 1) % 2][:, BT:BT + 3]))
                                nc.vector.tensor_copy(cur[:, 3:3 + BT], pg[n % 3][:]).then_inc(bank_free[n % 3], 1)
                                v.wait_ge(bank_free[n % 3], i * 4 + (n // 3 + 2))
                                v.wait_ge(step.sem, step.mark())
                                v.wait_ge(conv_free, i * 4 + (b + 1))
                                L(ts(acc[:], cur[:, 0:BT], cvec[:, 0:1], cvec[:, 4:5], ALU.mult, ALU.add))
                                L(stt(out=acc[:], in0=cur[:, 1:1 + BT], scalar=cvec[:, 1:2], in1=acc[:], op0=ALU.mult, op1=ALU.add))
                                L(stt(out=acc[:], in0=cur[:, 2:2 + BT], scalar=cvec[:, 2:3], in1=acc[:], op0=ALU.mult, op1=ALU.add))
                                stt(out=acc[:], in0=cur[:, 3:3 + BT], scalar=cvec[:, 3:4], in1=acc[:],
                                    op0=ALU.mult, op1=ALU.add).then_inc(conv, 1)
                        if what == "gate":
                            v.wait_ge(gate_done, i * 4 + (n + 1 + 2))
                            v.wait_ge(gate_added, i * 4 + (n + 1))
                            tt(m.gacc[:, n * BT:(n + 1) * BT], pgate[0:2 * MH, :], m.gacc[:, n * BT:(n + 1) * BT],
                               ALU.add).then_inc(gate_added, 1)
                        if what == "in":
                            q = n % 2
                            v.wait_ge(v_done, i * 8 + (n + 1))
                            v.wait_ge(table.sem, i * 48 + 6 * (n + 1))
                            step.add(tt(wa[:], pv[q][:, 0, :], cosk[q][:], ALU.mult))
                            tt(wb[:], pv[q][:, 1, :], sink[q][:], ALU.mult).then_inc(v_read, 1)
                            v.wait_ge(v_read, i * 8 + (n + 3))
                            L(tt(wa[:], wa[:], wb[:], ALU.add))
                            L(nc.vector.tensor_tensor_scan(zz[:, 1:1 + NCH], wt[q][:, RAD:RAD + 1].broadcast_to([P, NCH]), wa[:],
                                                           0.0, ALU.mult, ALU.add))
                            v.wait_ge(y_done, i * 8 + (n + 1))
                            step.add(tt(cz[q][:, 0, :], zz[:, 0:NCH], cosk[q][:], ALU.mult))
                            tt(cz[q][:, 1, :], zz[:, 0:NCH], sink[q][:], ALU.mult).then_inc(z_turned, 1)
                            v.wait_ge(z_turned, i * 8 + (n + 3))
                step.leave(KC)

            @block.tensor
            def _(pe):
                pe.sem_inc(u_done, 8)
                pe.sem_inc(u_read, 4)
                pe.sem_inc(gemm_done, 12)
                pe.sem_inc(gate_done, 2)
                pe.sem_inc(y_done, 2)
                xs = lambda b: (lambda part, k: m.hT[:, part, k, b * BT:(b + 1) * BT])
                ws = lambda w: (lambda part, k: w[:, part, k, :])
                with pe.Fori(0, KC // 2) as i:
                    for j in range(2):
                        pe.wait_ge(w1_lo, i * 2 + (j + 2))
                        for b in range(NB):
                            pe.wait_ge(u_read, i * 8 + (4 * j + b + 1))
                            split_product(nc, pg1[b], ws(whl[j]), xs(b)).then_inc(u_done, 1)
                pe.wait_ge(u_read, 4 * KC + 4)
                with pe.Fori(0, KC) as i:
                    for what, n in plan:
                        q = n % 2
                        if what == "gemm":
                            sec, b = n // 4, n % 4
                            if b == 0:
                                pe.wait_ge(w_lo, i * 3 + (sec + 1))
                            pe.wait_ge(bank_free[n % 3], i * 4 + (n // 3 + 1))
                            split_product(nc, pg[n % 3][:], ws(whl[sec]), xs(b)).then_inc(gemm_done, 1)
                        if what == "gate":
                            if n == 0:
                                pe.wait_ge(wif_in, i * 16 + 16)
                            pe.wait_ge(conv_free, i * 4 + (n + 2))
                            pe.wait_ge(gate_added, i * 4 + (n + 1))
                            nc.tensor.matmul(pgate[0:2 * MH, :], wif[:, 0, :], xst[q][:], start=True, stop=False)
                            nc.tensor.matmul(pgate[0:2 * MH, :], wif[:, 1, :], mb[q][:, 3:3 + BT], start=False,
                                             stop=True).then_inc(gate_done, 1)
                        if what == "in":
                            pe.wait_ge(s5_in[q], i * 128 + 32 * (n // 2 + 1))
                            pe.wait_ge(v_read, i * 8 + (n + 1))
                            nc.tensor.matmul(pv[q][:, 0, :], wt[q][:, BIN:BIN + P], us[q][:], start=True, stop=True)
                            nc.tensor.matmul(pv[q][:, 1, :], wt[q][:, BIS:BIS + P], us[q][:], start=True, stop=True).then_inc(v_done, 1)
                        if what == "out":
                            pe.wait_ge(y_read, i * 8 + (n + 1))
                            nc.tensor.matmul(py[q][:, 0:NCH], wt[q][:, TOE:TOE + P], us[q][:], start=True, stop=False)
                            pe.wait_ge(z_turned, i * 8 + (n + 3))
                            nc.tensor.matmul(py[q][:, 0:NCH], wt[q][:, COC:COC + P], cz[q][:, 0, :], start=False, stop=False)
                            nc.tensor.matmul(py[q][:, 0:NCH], wt[q][:, COS:COS + P], cz[q][:, 1, :], start=False,
                                             stop=True).then_inc(y_done, 1)


def gates(m, a, ctx, block, bank, bank_read):
    nc = m.nc
    R = MH * NMC
    sb = lambda n, s, d=F32: ctx.enter_context(nc.sbuf_tensor(n, s, d))
    bias = sb("t_bias", [2 * MH, 1])
    li, fr = sb("t_li", [R, MC]), sb("t_fr", [R, MC])
    w = [sb(f"t_w{j}", [R, MC]) for j in range(4)]
    whole = sb("t_whole", [R, MC], I32)
    ones = sb("t_ones", [R, MC])
    zeros = sb("t_zeros", [R, MC])
    run = sb("t_run", [R, MC])
    q = sb("t_q", [R, 4, MC])
    ends = sb("t_ends", [R, 2])
    er = sb("t_er", [MH, 2, NMC])
    mrow = sb("t_mrow", [MH, NMC + 1])
    mcol = sb("t_mcol", [R, 2])
    ps = bank[:, 0:4 * R].rearrange("p (q r) -> p q r", q=4)
    bias_in, logits = m.sem("t_bias_in"), m.sem("t_logits")
    moved = m.sem("t_moved")
    step = Tally(m.sem("t_step"))
    exp_in, exp_out = m.sem("t_exp_in"), m.sem("t_exp_out")
    ends_ready, m_ready, q_ready, turned = (m.sem(f"t_{n}") for n in ("ends", "m", "q", "turned"))

    @block.sync
    def _(sp):
        sp.dma_start(bias[:], a["m_b_if"].rearrange("o n -> n o"), allow_slow_non_contiguous=True).then_inc(bias_in, 16)
        sp.wait_ge(logits, 1)
        sp.dma_start(m.gt_d, m.gacc[:]).then_inc(moved, 16)
        sp.wait_ge(moved, 16)
        rows = m.gt_d.rearrange("n (c t) -> (n c) t", t=MC)
        sp.dma_start(li[:], rows[0:R]).then_inc(moved, 16)
        sp.dma_start(fr[:], rows[R:2 * R]).then_inc(moved, 16)
        sp.wait_ge(ends_ready, 1)
        sp.dma_start(m.mx_d[0:2].rearrange("k r -> r k"), ends[:], allow_slow_non_contiguous=True).then_inc(moved, 16)
        sp.wait_ge(moved, 64)
        sp.dma_start(er[:], m.mx_d[0:2].rearrange("k (h c) -> h k c", h=MH), allow_slow_non_contiguous=True).then_inc(moved, 16)
        sp.wait_ge(m_ready, 1)
        sp.dma_start(m.mx_d[2:3].rearrange("k (h c) -> (k h) c", h=MH), mrow[:, 0:NMC]).then_inc(moved, 16)
        sp.wait_ge(moved, 96)
        sp.dma_start(mcol[:, 0:1], m.mx_d[2:3].rearrange("k r -> r k"), allow_slow_non_contiguous=True).then_inc(moved, 16)
        sp.wait_ge(q_ready, 1)
        sp.dma_start(m.gb_d, run[:]).then_inc(moved, 16)
        sp.dma_start(m.mx_d[3:4].rearrange("k r -> r k"), mcol[:, 1:2], allow_slow_non_contiguous=True).then_inc(moved, 16)
        sp.wait_ge(moved, 144)
        sp.dma_start(m.decay[:].rearrange("p h c -> p (h c)"), m.mx_d[3:4].broadcast_to([P, R])).then_inc(moved, 16)
        sp.wait_ge(moved, 160)

    @block.vector
    def _(v):
        def L(ins):
            v.wait_ge(step.sem, step.add(ins))

        tt, stt, ts = nc.vector.tensor_tensor, nc.vector.scalar_tensor_tensor, nc.vector.tensor_scalar
        v.wait_ge(bias_in, 16)
        ts(m.gacc[:], m.gacc[:], bias[:, 0:1], None, ALU.add).then_inc(logits, 1)
        L(nc.vector.memset(ones[:], 1.0))
        L(nc.vector.memset(zeros[:], 0.0))
        L(nc.vector.memset(mrow[:], 0.0))
        v.wait_ge(moved, 48)
        L(stt(out=w[0][:], in0=fr[:], scalar=-1.0, in1=fr[:], op0=ALU.mult, op1=ALU.min))
        exp_steps(nc, L, w[1][:], w[0][:], w[2][:], w[3][:], whole[:])
        L(ts(w[0][:], w[1][:], 2.0, None, ALU.add))
        L(nc.vector.reciprocal(w[2][:], w[0][:]))
        L(tt(w[0][:], w[1][:], w[2][:], ALU.mult))
        L(tt(w[1][:], w[0][:], w[0][:], ALU.mult))
        L(ts(w[2][:], w[1][:], 1.0 / 17, None, ALU.mult))
        for k in range(15, 1, -2):
            L(stt(out=w[2][:], in0=w[2][:], scalar=1.0 / k, in1=w[1][:], op0=ALU.add, op1=ALU.mult))
        L(stt(out=w[2][:], in0=w[2][:], scalar=1.0, in1=w[0][:], op0=ALU.add, op1=ALU.mult))
        L(ts(w[0][:], fr[:], 0.0, None, ALU.min))
        L(stt(out=w[0][:], in0=w[2][:], scalar=-2.0, in1=w[0][:], op0=ALU.mult, op1=ALU.add))
        L(nc.vector.tensor_tensor_scan(w[1][:], ones[:], w[0][:], 0.0, ALU.mult, ALU.add))
        L(tt(q[:, 0, :], li[:], w[1][:], ALU.subtract))
        L(nc.vector.tensor_tensor_scan(run[:], q[:, 0, :], zeros[:], -3.0e38, ALU.max, ALU.add))
        L(nc.vector.tensor_copy(ends[:, 0:1], run[:, MC - 1:MC]))
        nc.vector.tensor_copy(ends[:, 1:2], w[1][:, MC - 1:MC]).then_inc(ends_ready, 1)
        v.wait_ge(moved, 80)
        nc.vector.tensor_tensor_scan(mrow[:, 1:NMC + 1], er[:, 0, :], er[:, 1, :], 0.0, ALU.max, ALU.add).then_inc(m_ready, 1)
        v.wait_ge(moved, 112)
        L(ts(run[:], run[:], mcol[:, 0:1], None, ALU.max))
        L(ts(q[:, 1, :], run[:], mcol[:, 0:1], -1.0, ALU.subtract, ALU.mult))
        L(ts(q[:, 2, :], q[:, 0, :], run[:, MC - 1:MC], None, ALU.subtract))
        L(tt(q[:, 3, :], run[:], w[1][:], ALU.add))
        ts(q[:, 3, :], q[:, 3, :], -1.0, None, ALU.mult).then_inc(exp_in, 1)

    @block.scalar
    def _(act):
        act.wait_ge(exp_in, 1)
        nc.scalar.activation(q[:, 1:4, :], q[:, 1:4, :], ACT.Exp).then_inc(exp_out, 1)
        act.wait_ge(exp_out, 1)
        nc.scalar.copy(mcol[:, 1:2], q[:, 1, MC - 1:MC]).then_inc(q_ready, 1)

    @block.tensor
    def _(pe):
        pe.wait_ge(exp_out, 1)
        pe.wait_ge(*bank_read)
        for j in range(4):
            tr = nc.tensor.transpose(ps[:, j, :], q[:, j, :], m.ident[0:R, 0:R])
        tr.then_inc(turned, 1)

    def finish():
        @block.vector
        def _(v):
            v.wait_ge(turned, 1)
            nc.vector.tensor_copy(m.gcol[:], ps[:].rearrange("p q (h c) -> p c q h", h=MH)).then_inc(exp_in, 1)
            v.wait_ge(exp_in, 2)

    return finish


def glu(m, a):
    nc = m.nc
    with ExitStack() as ctx:
        sb = lambda n, s, d=F32: ctx.enter_context(nc.sbuf_tensor(n, s, d))
        raw = [sb(f"g_raw{j}", [P, D]) for j in range(2)]
        wg = sb("g_w", [P, 2, KC, D], F32R)
        gt = [sb(f"g_g{j}", [P, KC, BT]) for j in range(2)]
        ut, zt = sb("g_u", [P, KC, BT]), sb("g_z", [P, KC, BT])
        gh = sb("g_gh", [P, 2, KC, BT], F32R)
        sg = sb("g_s", [P, KC, BT])
        ot = [sb(f"g_o{j}", [P, BT]) for j in range(2)]
        ps = [ctx.enter_context(nc.psum_tensor(f"g_ps{n}", [P, BT], F32)) for n in range(KC)]
        w_in = [m.sem(f"g_w_in{j}") for j in range(2)]
        w_hi, w_lo = m.sem("g_w_hi"), m.sem("g_w_lo")
        y_in, z_in = m.sem("g_y_in"), m.sem("g_z_in")
        y0_in = [m.sem(f"g_y0_in{p}") for p in range(KC // 2)]
        pre, gel, hi, lo = m.sem("g_pre"), m.sem("g_gelu"), m.sem("g_hi"), m.sem("g_lo")
        used, done, sig, gated, stored = m.sem("g_used"), m.sem("g_done"), m.sem("g_sigmoid"), m.sem("g_gated"), m.sem("g_final")
        out = [m.sem(f"g_out{j}") for j in range(2)]
        wv = a["s5_w_glu"][0].rearrange("(k p) n -> k p n", p=P)
        tiled = lambda d_: d_.rearrange("(k p) b j c -> b p k (j c)", p=P)
        yd = m.ys_d.rearrange("(k p) (b t) -> k p b t", p=P, b=NB)
        tt, stt = nc.vector.tensor_tensor, nc.vector.scalar_tensor_tensor

        def gelu(act, b, n):
            act.wait_ge(pre, b * KC + n + 1)
            nc.scalar.activation(gt[b % 2][:, n], gt[b % 2][:, n], ACT.Gelu_apprx_tanh).then_inc(gel, 1)

        def store(act, b, n):
            act.wait_ge(stored, b * KC + n + 1)
            act.dma_start(yd[n, :, b], ot[n % 2][:]).then_inc(out[n % 2], 16)

        def finish_block(act, b):
            if b + 1 < NB:
                for n in range(KC):
                    gelu(act, b + 1, n)
            for n in range(KC):
                act.wait_ge(done, b * KC + n + 1)
                if b:
                    act.wait_ge(gated, (b - 1) * KC + n + 1)
                nc.scalar.activation(sg[:, n], ps[n][:], ACT.Sigmoid).then_inc(sig, 1)
            for n in range(KC):
                store(act, b, n)

        def sum_(b, n):
            stt(out=gt[b % 2][:, n], in0=ut[:, n], scalar=m.cols[:, ROWS["s5_d"] + n:ROWS["s5_d"] + n + 1],
                in1=gt[b % 2][:, n], op0=ALU.mult, op1=ALU.add).then_inc(pre, 1)

        def parts(v, b, k):
            v.wait_ge(gel, b * KC + k + 1)
            if b and k < KC - 1:
                v.wait_ge(used, (b - 1) * (KC - 1) + k + 1)
            elif b:
                v.wait_ge(done, b * KC)
            nc.vector.tensor_copy(gh[:, 0, k], gt[b % 2][:, k]).then_inc(hi, 1)
            v.wait_ge(hi, b * KC + k + 1)
            tt(gh[:, 1, k], gt[b % 2][:, k], gh[:, 0, k].bitcast(F32), ALU.subtract).then_inc(lo, 1)

        def gate_block(v, b):
            if b + 1 < NB:
                v.wait_ge(y_in, 32 * (b + 1))
                for n in range(KC):
                    sum_(b + 1, n)
                for k in range(KC):
                    parts(v, b + 1, k)
            v.wait_ge(z_in, 16 * (b + 1))
            for n in range(KC):
                v.wait_ge(sig, b * KC + n + 1)
                tt(sg[:, n], sg[:, n], gt[b % 2][:, n], ALU.mult).then_inc(gated, 1)
                v.wait_ge(gated, b * KC + n + 1)
                if b or n >= 2:
                    v.wait_ge(out[n % 2], 16 * ((b * KC + n) // 2))
                tt(ot[n % 2][:].rearrange("p (k j) -> p j k", j=CH), sg[:, n].rearrange("p (j k) -> p j k", j=CH),
                   zt[:, n].rearrange("p (j k) -> p j k", j=CH), ALU.mult).then_inc(stored, 1)

        with nc.Block() as block:
            @block.sync
            def _(sp):
                def y_and_u(b):
                    if b >= 2:
                        sp.wait_ge(stored, (b - 1) * KC)
                    if b >= 1:
                        sp.wait_ge(pre, b * KC)
                    sp.dma_start(gt[b % 2][:], tiled(m.y_d)[b]).then_inc(y_in, 16)
                    sp.dma_start(ut[:], tiled(m.u_d)[b]).then_inc(y_in, 16)

                def z(b):
                    if b >= 1:
                        sp.wait_ge(stored, b * KC)
                    sp.dma_start(zt[:], tiled(m.sz_d)[b]).then_inc(z_in, 16)

                def first_pair(p):
                    for tile, d_ in ((gt[0], m.y_d), (ut, m.u_d)):
                        sp.dma_start(tile[:, 2 * p:2 * p + 2], tiled(d_)[0][:, 2 * p:2 * p + 2]).then_inc(y0_in[p], 16)

                def weights(k):
                    sp.wait_ge(w_lo, k + 1)
                    sp.dma_start(raw[k % 2][:], wv[k]).then_inc(w_in[k % 2], 16)

                sp.sem_inc(w_lo, 2)
                for p in range(KC // 2):
                    first_pair(p)
                    weights(2 * p)
                    weights(2 * p + 1)
                y_and_u(1)
                z(0)
                for b in range(1, NB):
                    if b + 1 < NB:
                        y_and_u(b + 1)
                    z(b)

            @block.scalar
            def _(act):
                def weights(k):
                    act.wait_ge(w_in[k % 2], 16 * (k // 2 + 1))
                    nc.scalar.copy(wg[:, 0, k, :], raw[k % 2][:]).then_inc(w_hi, 1)

                for k in range(KC):
                    gelu(act, 0, k)
                    weights(k)
                for b in range(NB - 1):
                    finish_block(act, b)

            @block.vector
            def _(v):
                for k in range(KC):
                    v.wait_ge(y0_in[k // 2], 32)
                    sum_(0, k)
                    v.wait_ge(w_hi, k + 1)
                    tt(wg[:, 1, k, :], raw[k % 2][:], wg[:, 0, k, :].bitcast(F32), ALU.subtract).then_inc(w_lo, 1)
                    parts(v, 0, k)
                for b in range(NB - 1):
                    gate_block(v, b)

            @block.tensor
            def _(pe):
                for b in range(NB):
                    for k in range(KC):
                        if b == 0:
                            pe.wait_ge(w_lo, k + 3)
                        pe.wait_ge(lo, b * KC + k + 1)
                        for n in range(KC):
                            if k == 0 and b:
                                pe.wait_ge(sig, (b - 1) * KC + n + 1)
                            w = lambda part: wg[:, part, k, n * P:(n + 1) * P]
                            nc.tensor.matmul(ps[n][:], w(0), gh[:, 0, k, :], start=(k == 0), stop=False)
                            nc.tensor.matmul(ps[n][:], w(0), gh[:, 1, k, :], start=False, stop=False)
                            last = nc.tensor.matmul(ps[n][:], w(1), gh[:, 0, k, :], start=False, stop=(k == KC - 1))
                            if k == KC - 1:
                                last.then_inc(done, 1)
                            elif n == KC - 1:
                                last.then_inc(used, 1)

            finish_gates = gates(m, a, ctx, block, ps[0], (sig, (NB - 1) * KC + 1))

            @block.scalar
            def _(act):
                finish_block(act, NB - 1)
                for j in range(2):
                    act.wait_ge(out[j], 16 * (KC // 2 * NB))

            @block.vector
            def _(v):
                gate_block(v, NB - 1)

            finish_gates()


def mlstm(m, a):
    nc = m.nc
    HW = HD + 1
    with ExitStack() as ctx:
        sb = lambda n, s, d=F32: ctx.enter_context(nc.sbuf_tensor(n, s, d))
        wq, wk = sb("x_wq", [P, 2 * MH, HD]), sb("x_wk", [P, 2 * MH, HD])
        wvo = sb("x_wvo", [P, 2 * MH, 2, HD])
        wo = sb("x_wout", [P, 2, KC, D])
        gates0 = sb("x_gate", [P, D])
        w_in, wvo_in, ws_in, wo_in = (m.sem(f"x_{n}_in") for n in ("w", "wvo", "ws", "wo"))
        mt, xt, zt, yst = (sb(f"x_{n}", [P, KC, MC]) for n in ("m", "xc", "mz", "ys"))
        xr, ho = m.spare[:, 0:D], m.spare[:, D:2 * D]
        gb = sb("x_gb", [P, MH, MC])
        mask = sb("x_mask", [P, MC])
        cc = sb("x_cols", [P, 4, MH])
        dec = sb("x_dec", [P, MH])
        qt = sb("x_qt", [P, 2, 2, MC])
        kt = sb("x_kt", [P, 2, 2, MC])
        kw = [sb(f"x_kw{j}", [P, HD]) for j in range(2)]
        ve = [sb(f"x_ve{j}", [P, HW]) for j in range(2)]
        og = sb("x_og", [P, MH, HD])
        pm = sb("x_pm", [P, MH, MC])
        st = [sb(f"x_st{j}", [P, MC]) for j in range(2)]
        cst = sb("x_c", [P, MH, 2, HW])
        bs = [sb(f"x_bs{j}", [P, HW]) for j in range(2)]
        ha = sb("x_ha", [P, MH, HW])
        hs = sb("x_hs", [P, MH, HD])
        sm = sb("x_small", [P, 6, MH])
        xs = sb("x_skip", [P, KC, MC])
        ym = sb("x_ym", [P, KC, MC])
        pb = [ctx.enter_context(nc.psum_tensor(f"x_ps{j}", [P, 512], F32)) for j in range(8)]
        QK, KT, VO, SS, AA, BB, C0, C1 = pb
        made = m.sem("x_made")
        in_mx, in_gb, in_zy, in_x = m.sem("x_in_mx"), m.sem("x_in_gb"), m.sem("x_in_zy"), m.sem("x_in_x")
        (qk_done, kt_done, vo_done, s_done, a_done, b_done, c_done, y_turned, o_done) = (
            m.sem(f"x_{n}") for n in ("qk_done", "kt_done", "vo_done", "s_done", "a_done", "b_done", "c_done",
                                      "y_turned", "o_done"))
        (qk_read, kw_ready, ve_ready, pm_ready, st_ready, bs_ready, ha_ready, c_ready, h_ready, y_read, y_ready,
         h1_ready, masked, skipped, cols_ready, o_ready, sq_ready, root_ready, var_ready) = (
            m.sem(f"x_{n}") for n in ("qk_read", "kw_ready", "ve_ready", "pm_ready", "st_ready", "bs_ready", "ha_ready",
                                      "c_ready", "h_ready", "y_read", "y_ready", "h1_ready", "masked", "skipped",
                                      "cols_ready", "o_ready", "sq_ready", "root_ready", "var_ready"))
        h1_out, xs_made = m.sem("x_h1_out"), m.sem("x_xs_made")
        hs_ready = m.sem("x_hs_ready")
        step = Tally(m.sem("x_step"))
        fm = lambda d_: d_.rearrange("(k p) (c t) -> c p k t", p=P, t=MC)

        with nc.Block() as block:
            @block.sync
            def _(sp):
                def inputs(c):
                    sp.wait_ge(skipped, c + 1)
                    sp.wait_ge(vo_done, c * MH + 1)
                    sp.dma_start(mt[:], fm(m.m_d)[c]).then_inc(in_mx, 16)
                    sp.dma_start(xt[:], fm(m.xc_d)[c]).then_inc(in_mx, 16)
                    sp.wait_ge(masked, c + 1)
                    sp.dma_start(gb[:], m.gb_d.rearrange("(h c) t -> c h t", h=MH)[c].partition_broadcast(P)).then_inc(in_gb, 16)

                def rest(c):
                    sp.wait_ge(y_ready, c + 1)
                    sp.wait_ge(o_done, c + 1)
                    sp.dma_start(zt[:], fm(m.smz_d)[c]).then_inc(in_zy, 16)
                    sp.dma_start(yst[:], fm(m.ys_d)[c]).then_inc(in_zy, 16)
                    sp.wait_ge(h1_ready, c * 2 + 2)
                    sp.dma_start(xr, a["x"].rearrange("o (c t) d -> (o c) t d", t=MC)[c]).then_inc(in_x, 16)

                def store(c):
                    sp.wait_ge(h1_ready, c * 2 + 4)
                    sp.dma_start(m.h1_d.rearrange("(c t) d -> c t d", t=MC)[c], ho).then_inc(h1_out, 16)

                sp.sem_inc(h1_out, 16)
                head = lambda n: a[n][0].rearrange("h (k p) e -> p (h k) e", p=P)
                for tile, name in ((wq, "m_wq"), (wk, "m_wk")):
                    sp.dma_start(tile[:], head(name)).then_inc(w_in, 16)
                inputs(0)
                for n, name in enumerate(("m_wv", "m_wo")):
                    sp.dma_start(wvo[:, :, n, :], head(name)).then_inc(wvo_in, 16)
                rest(0)
                wov = a["ev_w_out"][0].rearrange("(h k p) n -> h p k n", h=2, p=P)
                sp.dma_start(wo[:, 0], wov[0]).then_inc(ws_in, 16)
                sp.dma_start(wo[:, 1], wov[1]).then_inc(wo_in, 16)
                sp.dma_start(gates0[:], m.gate_d[0:1].broadcast_to([P, D])).then_inc(wo_in, 16)
                with sp.Fori(0, NMC - 1) as c:
                    inputs(c + 1)
                    store(c)
                    rest(c + 1)
                store(NMC - 1)
                sp.wait_ge(h1_out, 16 * (NMC + 1))

            @block.gpsimd
            def _(pool):
                nc.gpsimd.memset(mask[:], 0.0).then_inc(made, 1)
                nc.gpsimd.memset(cst[:], 0.0).then_inc(made, 1)
                for j in range(2):
                    nc.gpsimd.memset(ve[j][:, HD:HW], 1.0).then_inc(made, 1)
                pool.wait_ge(made, 4)
                nc.gpsimd.affine_select(out=mask[:], in_=mask[:], compare_op=ALU.is_ge, fill=NEG, base=0,
                                        pattern=[[1, MC]], channel_multiplier=-1).then_inc(made, 1)
                pool.wait_ge(made, 5)
                pool.sem_inc(masked, 1)
                pool.sem_inc(skipped, 1)
                skip = m.cols[:, ROWS["m_skip"]:ROWS["m_skip"] + KC].unsqueeze(2).broadcast_to([P, KC, MC])
                with pool.Fori(0, NMC) as c:
                    pool.wait_ge(in_gb, c * 16 + 16)
                    pool.wait_ge(pm_ready, c * MH + MH)
                    pool.wait_ge(st_ready, c * MH + MH)
                    nc.gpsimd.tensor_tensor(pm[:], mask[:].unsqueeze(1).broadcast_to([P, MH, MC]), gb[:], ALU.subtract).then_inc(masked, 1)
                    pool.wait_ge(in_mx, c * 32 + 32)
                    pool.wait_ge(y_ready, c + 1)
                    nc.gpsimd.tensor_tensor(xs[:], xt[:], skip, ALU.mult).then_inc(xs_made, 1)
                    pool.wait_ge(xs_made, c + 1)
                    pool.wait_ge(kt_done, c * MH + (MH + 1))
                    pool.wait_ge(qk_done, c * MH + (MH + 1))
                    pool.sem_inc(skipped, 1)

            @block.scalar
            def _(act):
                act.sem_inc(pm_ready, MH)
                act.sem_inc(ve_ready, 2)
                act.sem_inc(bs_ready, 2)
                act.sem_inc(o_ready, 1)
                act.wait_ge(made, 5)

                def exps(c):
                    act.wait_ge(cols_ready, c + 1)
                    act.wait_ge(masked, c + 2)
                    for h in range(MH):
                        nc.scalar.activation(pm[:, h, :], pm[:, h, :], ACT.Exp, bias=cc[:, 0, h:h + 1]).then_inc(pm_ready, 1)

                def square(c, h):
                    act.wait_ge(hs_ready, c * MH + (h + 1))
                    nc.scalar.activation(ha[:, h, 0:HD], hs[:, h], ACT.Square, accum_out=sm[:, 2, h:h + 1]).then_inc(sq_ready, 1)

                def one(c, last_one):
                    for h in range(MH):
                        r = h % 2
                        act.wait_ge(qk_done, c * MH + (h + 1 + 1))
                        act.wait_ge(c_done, c * MH + (h + 1))
                        nc.scalar.activation(qt[:, r], QK[:, 0:2 * MC].rearrange("p (a b) -> p a b", a=2), ACT.Copy, scale=HD ** -0.5)
                        nc.scalar.copy(kt[:, r], QK[:, 2 * MC:4 * MC].rearrange("p (a b) -> p a b", a=2)).then_inc(qk_read, 1)
                        act.wait_ge(vo_done, c * MH + (h + 1 + 1))
                        act.wait_ge(a_done, c * MH + (h + 1))
                        act.wait_ge(h_ready, c + 1)
                        nc.scalar.activation(og[:, h, :], VO[:, HD:2 * HD], ACT.Sigmoid)
                        nc.scalar.copy(ve[r][:, 0:HD], VO[:, 0:HD]).then_inc(ve_ready, 1)
                        act.wait_ge(b_done, c * MH + (h + 1))
                        act.wait_ge(ha_ready, c * MH + (h + 1))
                        nc.scalar.activation(bs[r][:], BB[:, 0:HW], ACT.Copy, scale=cc[:, 1, h:h + 1]).then_inc(bs_ready, 1)
                        if h:
                            square(c, h - 1)
                    square(c, MH - 1)
                    act.wait_ge(var_ready, c + 1)
                    nc.scalar.activation(sm[:, 3], sm[:, 2], ACT.Sqrt).then_inc(root_ready, 1)
                    for k in range(KC):
                        if k % 4 == 0:
                            act.wait_ge(y_turned, c * 2 + (k // 4 + 1))
                            if k == 0:
                                act.wait_ge(o_done, c + 1)
                        last = nc.scalar.activation(ym[:, k, :], (QK, VO)[k // 4][:, (k % 4) * MC:(k % 4 + 1) * MC], ACT.Copy,
                                                    scale=m.cols[:, ROWS["m_norm_g"] + k:ROWS["m_norm_g"] + k + 1])
                        if k % 4 == 3:
                            last.then_inc(y_read, 1)
                    if not last_one:
                        exps(c + 1)

                exps(0)
                with act.Fori(0, NMC - 1) as c:
                    one(c, False)
                one(NMC - 1, True)

            @block.vector
            def _(v):
                def L(ins):
                    v.wait_ge(step.sem, step.add(ins))

                tt, stt, ts = nc.vector.tensor_tensor, nc.vector.scalar_tensor_tensor, nc.vector.tensor_scalar
                v.sem_inc(kw_ready, 2)
                v.sem_inc(st_ready, MH)
                v.sem_inc(ha_ready, 2)
                v.sem_inc(h_ready, 1)
                v.sem_inc(y_ready, 1)
                v.sem_inc(h1_ready, 2)
                v.sem_inc(c_ready, 1)
                v.wait_ge(made, 5)

                def columns(c):
                    v.wait_ge(ha_ready, c * MH + 2)
                    v.wait_ge(bs_ready, c * MH + 2)
                    v.wait_ge(pm_ready, c * MH + MH)
                    v.wait_ge(c_ready, c * MH + 1)
                    L(nc.vector.tensor_copy(dec[:], m.decay[:, :, c]))
                    nc.vector.tensor_copy(cc[:], m.gcol[:, c]).then_inc(cols_ready, 1)

                def one(c, last_one):
                    v.wait_ge(cols_ready, c + 1)
                    for h in range(MH):
                        r = h % 2
                        v.wait_ge(kt_done, c * MH + (h + 1 + 1))
                        v.wait_ge(c_done, c * MH + (h + 1))
                        ts(kw[r][:], KT[:, 0:HD], cc[:, 2, h:h + 1], None, ALU.mult).then_inc(kw_ready, 1)
                        v.wait_ge(s_done, c * MH + (h + 1))
                        v.wait_ge(pm_ready, c * MH + (h + 1 + MH))
                        v.wait_ge(a_done, c * MH + (h + 1))
                        tt(st[r][:], SS[:, 0:MC], pm[:, h, :], ALU.mult).then_inc(st_ready, 1)
                        v.wait_ge(c_done, c * MH + (h + 1 + 2))
                        v.wait_ge(c_ready, c * MH + (h + 1))
                        stt(out=cst[:, h, 0], in0=cst[:, h, 0], scalar=dec[:, h:h + 1], in1=C0[:, 0:HW], op0=ALU.mult, op1=ALU.add)
                        stt(out=cst[:, h, 1], in0=cst[:, h, 1], scalar=dec[:, h:h + 1], in1=C1[:, 0:HW],
                            op0=ALU.mult, op1=ALU.add).then_inc(c_ready, 1)
                        v.wait_ge(a_done, c * MH + (h + 1 + 2))
                        v.wait_ge(bs_ready, c * MH + (h + 1 + 2))
                        tt(ha[:, h, :], AA[:, 0:HW], bs[r][:], ALU.add).then_inc(ha_ready, 1)
                        v.wait_ge(ha_ready, c * MH + (h + 1 + 2))
                        one_h = lambda row: sm[:, row, h:h + 1]
                        L(stt(out=one_h(0), in0=ha[:, h, HD:HW], scalar=-1.0, in1=ha[:, h, HD:HW], op0=ALU.mult, op1=ALU.max))
                        L(tt(one_h(0), one_h(0), cc[:, 3, h:h + 1], ALU.max))
                        L(nc.vector.reciprocal(one_h(1), one_h(0)))
                        stt(out=hs[:, h], in0=ha[:, h, 0:HD], scalar=one_h(1), in1=og[:, h], op0=ALU.mult, op1=ALU.mult).then_inc(hs_ready, 1)
                    v.wait_ge(sq_ready, c * MH + MH)
                    ts(sm[:, 2], sm[:, 2], 1.0 / HD, EPS, ALU.mult, ALU.add).then_inc(var_ready, 1)
                    v.wait_ge(var_ready, c + 1)
                    if not last_one:
                        columns(c + 1)
                    v.wait_ge(root_ready, c + 1)
                    rsqrt_steps(nc, L, sm[:, 2], sm[:, 3], sm[:, 4], sm[:, 5])
                    tt(hs[:], hs[:], sm[:, 4].unsqueeze(2).broadcast_to([P, MH, HD]), ALU.mult).then_inc(h_ready, 1)
                    v.wait_ge(y_read, c * 2 + 4)
                    v.wait_ge(xs_made, c + 1)
                    L(tt(ym[:], ym[:], xs[:], ALU.add))
                    v.wait_ge(in_zy, c * 32 + 32)
                    tt(ym[:], ym[:], zt[:], ALU.mult).then_inc(y_ready, 1)
                    v.wait_ge(in_x, c * 16 + 16)
                    v.wait_ge(h1_out, c * 16 + 16)
                    v.wait_ge(o_done, c + 2)
                    for n, bank in enumerate((KT, SS)):
                        at = slice(n * 512, (n + 1) * 512)
                        L(tt(ho[:, at], bank[:], gates0[:, at], ALU.mult))
                        tt(ho[:, at], ho[:, at], xr[:, at], ALU.add).then_inc(h1_ready, 1)
                columns(0)
                with v.Fori(0, NMC - 1) as c:
                    step.enter(c, 3 * MH + 8)
                    one(c, False)
                step.leave(NMC - 1)
                one(NMC - 1, True)

            @block.tensor
            def _(pe):
                pe.sem_inc(vo_done, 1)
                pe.sem_inc(kt_done, 1)
                pe.sem_inc(qk_done, 1)
                pe.sem_inc(c_done, 2)
                pe.sem_inc(a_done, 2)
                pe.sem_inc(o_done, 1)
                pe.sem_inc(qk_read, 1)
                pe.sem_inc(y_read, 2)
                pe.wait_ge(w_in, 16 * 2)
                mm = nc.tensor.matmul

                def inputs(c, h):
                    pe.wait_ge(qk_read, c * MH + (h + 1))
                    if h == 0:
                        pe.wait_ge(y_read, c * 2 + 2)
                    for j, w in enumerate((wq, wk)):
                        for e in range(2):
                            at = (2 * j + e) * MC
                            for k in range(2):
                                last = mm(QK[:, at:at + MC], w[:, 2 * h + k, e * P:(e + 1) * P], xt[:, 2 * h + k, :],
                                          start=(k == 0), stop=(k == 1))
                    last.then_inc(qk_done, 1)
                    pe.wait_ge(wvo_in, 16 * 2)
                    pe.wait_ge(ve_ready, c * MH + (h + 2))
                    for k in range(2):
                        last = mm(VO[:], mt[:, 2 * h + k, :], wvo[:, 2 * h + k].rearrange("p a e -> p (a e)"), start=(k == 0), stop=(k == 1))
                    last.then_inc(vo_done, 1)

                def cell(c, h):
                    r = h % 2
                    pe.wait_ge(qk_read, c * MH + (h + 2))
                    if h == 0:
                        pe.wait_ge(h1_ready, c * 2 + 2)
                    pe.wait_ge(kw_ready, c * MH + (h + 2))
                    for e in range(2):
                        tr = nc.tensor.transpose(KT[:, e * P:(e + 1) * P], kt[:, r, e], m.ident[:])
                    tr.then_inc(kt_done, 1)
                    pe.wait_ge(st_ready, c * MH + (h + MH))
                    for e in range(2):
                        last = mm(SS[:, 0:MC], kt[:, r, e], qt[:, r, e], start=(e == 0), stop=(e == 1))
                    last.then_inc(s_done, 1)
                    pe.wait_ge(bs_ready, c * MH + (h + 2))
                    pe.wait_ge(c_ready, c * MH + (h + 1))
                    for e in range(2):
                        last = mm(BB[:, 0:HW], qt[:, r, e], cst[:, h, e], start=(e == 0), stop=(e == 1))
                    last.then_inc(b_done, 1)
                    pe.wait_ge(kw_ready, c * MH + (h + 3))
                    pe.wait_ge(ve_ready, c * MH + (h + 3))
                    mm(C0[:, 0:HW], kw[r][:, 0:P], ve[r][:], start=True, stop=True)
                    mm(C1[:, 0:HW], kw[r][:, P:2 * P], ve[r][:], start=True, stop=True).then_inc(c_done, 1)
                    pe.wait_ge(ha_ready, c * MH + (h + 2))
                    pe.wait_ge(st_ready, c * MH + (h + 1 + MH))
                    mm(AA[:, 0:HW], st[r][:], ve[r][:], start=True, stop=True).then_inc(a_done, 1)

                def s5_half(n, bank):
                    at = slice(n * 512, (n + 1) * 512)
                    for k in range(KC):
                        mm(bank[:], yst[:, k, :], wo[:, 0, k, at], start=(k == 0), stop=False)

                with pe.Fori(0, NMC) as c:
                    pe.wait_ge(in_mx, c * 32 + 32)
                    for h in range(MH):
                        inputs(c, h)
                        cell(c, h)
                    pe.wait_ge(in_zy, c * 32 + 32)
                    pe.wait_ge(ws_in, 16)
                    s5_half(0, KT)
                    pe.wait_ge(h_ready, c + 2)
                    hf = hs[:].rearrange("p h e -> p (h e)")
                    for k in range(KC):
                        tr = nc.tensor.transpose((QK, VO)[k // 4][:, (k % 4) * MC:(k % 4 + 1) * MC], hf[:, k * P:(k + 1) * P], m.ident[:])
                        if k % 4 == 3:
                            tr.then_inc(y_turned, 1)
                    s5_half(1, SS)
                    pe.wait_ge(wo_in, 32)
                    pe.wait_ge(y_ready, c + 2)
                    for n, bank in enumerate((KT, SS)):
                        for k in range(KC):
                            last = mm(bank[:], ym[:, k, :], wo[:, 1, k, n * 512:(n + 1) * 512], start=False, stop=(k == KC - 1))
                    last.then_inc(o_done, 1)


def attention(m, a, out):
    nc = m.nc
    NH = AH + AKV
    NCHUNK = 5
    GW = 4 * AD
    H8 = ROPE // 2
    LAST = TT - 1
    with ExitStack() as ctx:
        sb = lambda n, s, d=F32: ctx.enter_context(nc.sbuf_tensor(n, s, d))
        win = sb("a_win", [P, NCHUNK, KC, 512])
        wout = sb("a_wout", [P, KC, D])
        pos_i, pos_f = sb("a_pos_i", [TT, P], I32), sb("a_pos_f", [TT, P])
        post = sb("a_pos", [P, TT])
        rc, rs_, rt = (sb(n, [P, TT, H8]) for n in ("a_rope_c", "a_rope_s", "a_rope_t"))
        ra = sb("a_rope_a", [P, TT, H8])
        gr = sb("a_g_rows", [P, 2, AD])
        sink = sb("a_sink", [P, AH])
        mk = [sb(f"a_mask{j}", [P, 2, P]) for j in range(2)]
        mk_first = sb("a_mask_first", [P, 2, P])
        ht = [sb(f"a_h{j}", [P, D]) for j in range(2)]
        xn = sb("a_xn", [P, D])
        xT = sb("a_xT", [P, KC, P])
        qk = sb("a_qk", [P, NH, AD])
        qr = sb("a_qr", [P, NH, AD])
        r4 = [sb(f"a_r{j}", [P, NH, H8]) for j in range(4)]
        qT = sb("a_qT", [P, KC, P])
        kT = sb("a_kT", [P, 2, 2, P])
        v_new = sb("a_v_new", [P, AKV * AD])
        vv = sb("a_v", [P, 2, AKV * AD])
        sz = sb("a_sz", [P, D])
        sc = [sb(f"a_sc{j}", [P, 4, 2 * P]) for j in range(2)]
        pT = [sb(f"a_pT{j}", [P, 8, P]) for j in range(2)]
        att = sb("a_att", [P, D])
        aT = sb("a_aT", [P, KC, P])
        ot = [sb(f"a_o{j}", [P, D]) for j in range(2)]
        gate = aT[:].rearrange("p k t -> p (k t)")
        st = sb("a_stat", [P, 6])
        hstat = sb("a_hstat", [P, 5, NH])
        mx, nmx, rsum, den = (sb(n, [P, AH]) for n in ("a_mx", "a_nmx", "a_rsum", "a_den"))
        ps = lambda n, s: ctx.enter_context(nc.psum_tensor(n, s, F32))
        B = (ps("a_chunk0", [P, 512]), ps("a_chunk1", [P, 512]))
        psc = ps("a_psc", [P, 4, 2 * P])
        T = (ps("a_t0", [P, 4, P]), ps("a_t1", [P, 4, P]))
        tx = ps("a_tx", [P, 512])
        pv = ps("a_pv", [P, 2, GW])
        halves = [h.rearrange("p (a b) -> p a b", b=P) for h in (tx[:], pv[:].rearrange("p a b -> p (a b)"))]

        w_in = [None] + [m.sem(f"a_w_in{n}") for n in range(1, NCHUNK)]
        w0_in = [m.sem(f"a_w0_in{n}") for n in range(2)]
        wo_in, c_in = m.sem("a_wo_in"), m.sem("a_c_in")
        h_in, o_out = m.sem("a_h_in"), m.sem("a_o_out")
        step = Tally(m.sem("a_step"))
        S = lambda names: (m.sem(f"a_{n}") for n in names.split())
        pool_made, wo_ready, pos_ready, pos_turned, angles, tables = S("made wo_ready pos_ready pos_turned angles tables")
        sq_ready, var_ready, root_ready, xn_ready, xn_turned, xT_ready, o_copied = S(
            "sq_ready var_ready root_ready xn_ready xn_turned xT_ready o_copied")
        q_done, kv_done, z_done, q_out, v_out, v_ready, z_out = S("q_done kv_done z_done q_out v_out v_ready z_out")
        qk_var, qk_root, qk_ready, qk_turned, qT_ready, qT2_ready = S("qk_var qk_root qk_ready qk_turned qT_ready qT2_ready")
        s_done, s_read, max_ready, exp_ready, p_turned, pT_ready, pT2_ready = S(
            "s_done s_read max_ready exp_ready p_turned pT_ready pT2_ready")
        pv_done, pv_read, att_ready, att_turned, aT_ready, o_done, o_added, mask_ready = S(
            "pv_done pv_read att_ready att_turned aT_ready o_done o_added mask_ready")

        def steps(eng, one, per=0, tally=None):
            one(0, 0, True, False)
            with eng.Fori(0, (TT - 2) // 2) as i:
                if tally:
                    tally.enter(i, 2 * per)
                for u in range(2):
                    one(i * 2 + (u + 1), (u + 1) % 2, False, False)
            if tally:
                tally.leave((TT - 2) // 2)
            one(LAST, LAST % 2, False, True)

        with nc.Block() as block:
            @block.sync
            def _(sp):
                hv = m.h1_d.rearrange("(t p) d -> t p d", p=P)
                ov = out.rearrange("o (t p) d -> (o t) p d", p=P)
                sp.dma_start(ht[0][:], hv[0]).then_inc(h_in, 16)
                sp.dma_start(pos_i[:], a["positions"].rearrange("o (t p) -> (o t) p", p=P)).then_inc(c_in, 16)
                sp.dma_start(gr[:, 0, :], a["od_q_norm_g"].broadcast_to([P, AD])).then_inc(c_in, 16)
                sp.dma_start(gr[:, 1, :], a["od_k_norm_g"].broadcast_to([P, AD])).then_inc(c_in, 16)
                sp.dma_start(sink[:], a["od_sinks"].broadcast_to([P, AH])).then_inc(c_in, 16)
                wv = a["od_w_in"][0].rearrange("(k p) (c n) -> c p k n", p=P, n=512)
                for k in range(0, KC, KC // 2):
                    sp.dma_start(win[:, 0, k:k + KC // 2], wv[0][:, k:k + KC // 2]).then_inc(w0_in[2 * k // KC], 16)
                for n in range(1, NCHUNK):
                    sp.dma_start(win[:, n], wv[n]).then_inc(w_in[n], 16)
                sp.dma_start(gate, m.gate_d[1:2].broadcast_to([P, D])).then_inc(wo_in, 16)
                sp.dma_start(wout[:], a["od_w_out"][0].rearrange("(k p) n -> p k n", p=P)).then_inc(wo_in, 16)
                sp.wait_ge(h_in, 16)
                sp.dma_start(ht[1][:], hv[1]).then_inc(h_in, 16)
                sp.sem_inc(o_out, 16)

                def load(t, j):
                    sp.wait_ge(o_copied, t - 1)
                    sp.wait_ge(h_in, t * 16)
                    sp.dma_start(ht[j][:], hv[t]).then_inc(h_in, 16)

                def store(t, j):
                    sp.wait_ge(o_added, t * 2 + 2)
                    sp.wait_ge(o_out, t * 16 + 16)
                    sp.dma_start(ov[t], ot[j][:]).then_inc(o_out, 16)

                with sp.Fori(0, (TT - 2) // 2) as i:
                    for j in range(2):
                        load(i * 2 + (j + 2), j)
                        store(i * 2 + j, j)
                for j in range(2):
                    store(TT - 2 + j, j)
                sp.wait_ge(o_out, 16 * (TT + 1))

            @block.gpsimd
            def _(pool):
                made = 0
                for tile in (mk[0], mk[1], kT, vv):
                    nc.gpsimd.memset(tile[:], 0.0).then_inc(pool_made, 1)
                    made += 1
                nc.gpsimd.memset(mk_first[:, 1, :], NEG).then_inc(pool_made, 1)
                nc.gpsimd.memset(mk_first[:, 0, :], 0.0).then_inc(pool_made, 1)
                made += 2
                pool.wait_ge(pool_made, made)
                now = dict(pattern=[[-1, P]], channel_multiplier=1, base=0)
                then = dict(pattern=[[1, P]], channel_multiplier=-1, base=-1)
                for tile, pat in ((mk_first[:, 0, :], now), (mk[0][:, 0, :], now), (mk[0][:, 1, :], then),
                                  (mk[1][:, 1, :], now), (mk[1][:, 0, :], then)):
                    nc.gpsimd.affine_select(out=tile, in_=tile, compare_op=ALU.is_ge, fill=NEG, **pat).then_inc(pool_made, 1)
                pool.wait_ge(pool_made, made + 5)
                pool.sem_inc(mask_ready, 1)
                pool.wait_ge(wo_in, 32)
                for k in range(KC):
                    nc.gpsimd.tensor_tensor(wout[:, k], wout[:, k], gate, ALU.mult).then_inc(wo_ready, 1)

            @block.scalar
            def _(act):
                AC = nc.scalar.activation
                act.sem_inc(qk_ready, 1)
                act.sem_inc(att_ready, 1)
                act.wait_ge(mask_ready, 1)

                def norm(t, j):
                    act.wait_ge(h_in, t * 16 + 16)
                    act.wait_ge(xn_turned, t * 2 + 2)
                    AC(xn[:], ht[j][:], ACT.Square, accum_out=st[:, 0:1]).then_inc(sq_ready, 1)
                    act.wait_ge(var_ready, t + 1)
                    AC(st[:, 2:3], st[:, 1:2], ACT.Sqrt).then_inc(root_ready, 1)

                def x_turned(t):
                    act.wait_ge(xn_turned, t * 2 + 3)
                    for k in range(KC // 2):
                        last = AC(xT[:, k, :], halves[0][:, k, :], ACT.Identity, scale=m.moda[:, 1, k:k + 1], bias=m.ada[:, 1, k:k + 1])
                    last.then_inc(xT_ready, 1)

                def copy_h(t, j):
                    act.wait_ge(o_out, t * 16)
                    nc.scalar.copy(ot[j][:], ht[j][:]).then_inc(o_copied, 1)

                def q_half(t, n, bank):
                    act.wait_ge(q_done, t * 2 + (n + 1))
                    if n == 0:
                        act.wait_ge(qk_ready, t + 1)
                        act.wait_ge(qk_turned, t * 3 + 3)
                    src = bank[:].rearrange("p (h d) -> p h d", d=AD)
                    nc.scalar.copy(qk[:, 8 * n:8 * n + 8], src)
                    AC(qr[:, 8 * n:8 * n + 8], src, ACT.Square).then_inc(q_out, 1)

                def kv(t, bank):
                    act.wait_ge(kv_done, t + 1)
                    src = bank[:, 0:AKV * AD].rearrange("p (h d) -> p h d", d=AD)
                    nc.scalar.copy(qk[:, AH:NH], src)
                    AC(qr[:, AH:NH], src, ACT.Square)
                    nc.scalar.copy(v_new[:], bank[:, AKV * AD:512]).then_inc(v_out, 1)

                def silu_z(t, n, bank):
                    act.wait_ge(z_done, t * 2 + (n + 1))
                    if n == 0:
                        act.wait_ge(att_ready, t + 1)
                    AC(sz[:, n * 512:(n + 1) * 512], bank[:], ACT.Silu).then_inc(z_out, 1)

                def keep_v(t, j):
                    act.wait_ge(v_out, t + 1)
                    act.wait_ge(pv_done, t * 4 + 4)
                    nc.scalar.copy(vv[:, j, :], v_new[:]).then_inc(v_ready, 1)

                def head_roots(t):
                    act.wait_ge(qk_var, t + 1)
                    AC(hstat[:, 2], hstat[:, 1], ACT.Sqrt).then_inc(qk_root, 1)

                def qk_turned_out(t, j):
                    act.wait_ge(qk_turned, t * 3 + 4)
                    nc.scalar.copy(kT[:, :, j, :], psc[:, 0, :].rearrange("p (a b) -> p a b", b=P))
                    act.wait_ge(qk_turned, t * 3 + 5)
                    nc.scalar.copy(qT[:, 0:4, :], T[0][:]).then_inc(qT_ready, 1)

                def exps(t, g):
                    act.wait_ge(max_ready, t * 4 + (g + 1))
                    for h in range(4 * g, 4 * g + 4):
                        AC(sc[g % 2][:, h % 4, :], sc[g % 2][:, h % 4, :], ACT.Exp, bias=nmx[:, h:h + 1], accum_out=rsum[:, h:h + 1])
                    AC(den[:, 4 * g:4 * g + 4], den[:, 4 * g:4 * g + 4], ACT.Exp).then_inc(exp_ready, 1)

                def p_half(t, g):
                    act.wait_ge(p_turned, t * 8 + (2 * g + 5))
                    act.wait_ge(pv_done, t * 4 + (g + 3))
                    nc.scalar.copy(pT[g % 2][:, 0:4, :], T[0][:]).then_inc(pT_ready, 1)

                norm(0, 0)
                x_turned(0)
                act.wait_ge(angles, 1)
                AC(rs_[:], rs_[:], ACT.Sin)
                AC(rc[:], rc[:], ACT.Sin).then_inc(tables, 1)
                q_half(0, 0, B[0])
                q_half(0, 1, B[1])
                kv(0, B[0])
                head_roots(0)
                silu_z(0, 0, B[1])
                silu_z(0, 1, B[0])
                keep_v(0, 0)
                qk_turned_out(0, 0)
                nc.scalar.copy(ot[0][:], ht[0][:]).then_inc(o_copied, 1)

                def one(t, j, first, last):
                    b = lambda n: B[(j + n + 1) % 2]
                    n1 = t + 1
                    if not last:
                        norm(n1, 1 - j)
                        x_turned(n1)
                    exps(t, 0)
                    p_half(t, 0)
                    exps(t, 1)
                    if not last:
                        q_half(n1, 0, b(2))
                    p_half(t, 1)
                    exps(t, 2)
                    if not last:
                        copy_h(n1, 1 - j)
                        q_half(n1, 1, b(3))
                    p_half(t, 2)
                    exps(t, 3)
                    if not last:
                        kv(n1, b(4))
                    p_half(t, 3)
                    if not last:
                        head_roots(n1)
                        silu_z(n1, 0, b(5))
                        keep_v(n1, 1 - j)
                    if first:
                        act.wait_ge(wo_ready, KC)
                    act.wait_ge(att_turned, t * 2 + 3)
                    nc.scalar.copy(aT[:, 0:4, :], halves[0]).then_inc(aT_ready, 1)
                    if not last:
                        silu_z(n1, 1, b(6))
                        qk_turned_out(n1, 1 - j)

                steps(act, one)

            @block.vector
            def _(v):
                def L(ins):
                    v.wait_ge(step.sem, step.add(ins))

                tt, stt, ts = nc.vector.tensor_tensor, nc.vector.scalar_tensor_tensor, nc.vector.tensor_scalar

                def norm(t, j):
                    v.wait_ge(sq_ready, t + 1)
                    ts(st[:, 1:2], st[:, 0:1], 1.0 / D, EPS, ALU.mult, ALU.add).then_inc(var_ready, 1)
                    v.wait_ge(root_ready, t + 1)
                    v.wait_ge(var_ready, t + 1)
                    rsqrt_steps(nc, L, st[:, 1:2], st[:, 2:3], st[:, 3:4], st[:, 4:5])
                    ts(xn[:], ht[j][:], st[:, 3:4], None, ALU.mult).then_inc(xn_ready, 1)

                def x_turned(t):
                    v.wait_ge(xn_turned, t * 2 + 4)
                    for k in range(KC // 2, KC):
                        last = ts(xT[:, k, :], halves[1][:, k - KC // 2, :], m.moda[:, 1, k:k + 1], m.ada[:, 1, k:k + 1], ALU.mult, ALU.add)
                    last.then_inc(xT_ready, 1)

                def q_and_k(t):
                    v.wait_ge(q_out, t * 2 + 2)
                    v.wait_ge(v_out, t + 1)
                    L(nc.vector.tensor_reduce(hstat[:, 0], qr[:], AX.X, ALU.add))
                    ts(hstat[:, 1], hstat[:, 0], 1.0 / AD, EPS, ALU.mult, ALU.add).then_inc(qk_var, 1)
                    v.wait_ge(qk_root, t + 1)
                    rsqrt_steps(nc, L, hstat[:, 1], hstat[:, 2], hstat[:, 3], hstat[:, 4])
                    L(tt(qk[:], qk[:], hstat[:, 3].unsqueeze(2).broadcast_to([P, NH, AD]), ALU.mult))
                    for b in range(2):
                        q8 = slice(8 * b, 8 * b + 8)
                        step.add(tt(qr[:, q8].rearrange("p (r b) d -> p b r d", b=2), qk[:, q8].rearrange("p (b r) d -> p b r d", b=2),
                                    gr[:, 0:1, :].unsqueeze(1).broadcast_to([P, 2, 4, AD]), ALU.mult))
                    L(tt(qr[:, AH:NH], qk[:, AH:NH], gr[:, 1:2, :].broadcast_to([P, AKV, AD]), ALU.mult))
                    c8, s8 = (x[:, t, :].unsqueeze(1).broadcast_to([P, NH, H8]) for x in (rc, rs_))
                    x1, x2 = qr[:, :, 0:H8], qr[:, :, H8:ROPE]
                    step.add(tt(r4[0][:], x1, c8, ALU.mult))
                    step.add(tt(r4[1][:], x2, s8, ALU.mult))
                    step.add(tt(r4[2][:], x2, c8, ALU.mult))
                    L(tt(r4[3][:], x1, s8, ALU.mult))
                    step.add(tt(x1, r4[0][:], r4[1][:], ALU.subtract))
                    tt(x2, r4[2][:], r4[3][:], ALU.add).then_inc(qk_ready, 1)

                def q_turned(t):
                    v.wait_ge(qk_turned, t * 3 + 6)
                    nc.vector.tensor_copy(qT[:, 4:8, :], T[1][:]).then_inc(qT2_ready, 1)

                def maxima(t, g, mask):
                    hs = slice(4 * g, 4 * g + 4)
                    v.wait_ge(s_done, t * 4 + (g + 1))
                    v.wait_ge(p_turned, t * 8 + (2 * g + 2))
                    tt(sc[g % 2][:], psc[:], mask[:].rearrange("p a b -> p (a b)").unsqueeze(1).broadcast_to([P, 4, 2 * P]),
                       ALU.add).then_inc(s_read, 1)
                    v.wait_ge(s_read, t * 4 + (g + 2))
                    L(nc.vector.tensor_reduce(mx[:, hs], sc[g % 2][:], AX.X, ALU.max))
                    L(tt(mx[:, hs], mx[:, hs], sink[:, hs], ALU.max))
                    step.add(tt(den[:, hs], sink[:, hs], mx[:, hs], ALU.subtract))
                    ts(nmx[:, hs], mx[:, hs], -1.0, None, ALU.mult).then_inc(max_ready, 1)

                def p_half(t, g):
                    v.wait_ge(p_turned, t * 8 + (2 * g + 6))
                    nc.vector.tensor_copy(pT[g % 2][:, 4:8, :], T[1][:]).then_inc(pT2_ready, 1)

                def products(t, g):
                    hs, ds = slice(4 * g, 4 * g + 4), slice(GW * g, GW * (g + 1))
                    v.wait_ge(exp_ready, t * 4 + (g + 1))
                    L(tt(den[:, hs], den[:, hs], rsum[:, hs], ALU.add))
                    L(nc.vector.reciprocal(den[:, hs], den[:, hs]))
                    v.wait_ge(pv_done, t * 4 + (g + 5))
                    if g == 0:
                        v.wait_ge(att_turned, t * 2 + 2)
                        v.wait_ge(z_out, t * 2 + 2)
                    tt(att[:, ds].rearrange("p (h d) -> p h d", d=AD), pv[:, g % 2, :].rearrange("p (h d) -> p h d", d=AD),
                       den[:, hs].unsqueeze(2).broadcast_to([P, 4, AD]), ALU.mult).then_inc(pv_read, 1)
                    v.wait_ge(pv_read, t * 4 + (g + 3))
                    last = tt(att[:, ds], att[:, ds], sz[:, ds], ALU.mult)
                    if g == AKV - 1:
                        last.then_inc(att_ready, 1)
                    else:
                        step.add(last)

                def output(t, j, n, bank):
                    v.wait_ge(o_copied, t + 1)
                    v.wait_ge(o_done, t * 2 + (n + 1))
                    ns = slice(n * 512, (n + 1) * 512)
                    tt(ot[j][:, ns], ot[j][:, ns], bank[:], ALU.add).then_inc(o_added, 1)

                v.sem_inc(s_read, 1)
                v.sem_inc(pv_read, 2)
                norm(0, 0)
                x_turned(0)
                v.wait_ge(c_in, 64)
                nc.vector.tensor_copy(pos_f[:], pos_i[:]).then_inc(pos_ready, 1)
                L(ts(gr[:, 0, :], gr[:, 0, :], AD ** -0.5, None, ALU.mult))
                v.wait_ge(pos_turned, 1)
                L(nc.vector.tensor_copy(post[:], T[0][:, 0, 0:TT]))
                freq = rope_frequencies()
                for f in range(H8):
                    L(ts(ra[:, :, f], post[:], freq[f], None, ALU.mult))
                L(ts(rt[:], ra[:], 1.0 / TWO_PI, ROUND, ALU.mult, ALU.add))
                L(ts(rt[:], rt[:], ROUND, None, ALU.subtract))
                for c in TWO_PI_PARTS:
                    L(stt(out=ra[:], in0=rt[:], scalar=-c, in1=ra[:], op0=ALU.mult, op1=ALU.add))
                L(ts(rs_[:], ra[:], PI_SAFE, -PI_SAFE, ALU.min, ALU.max))
                L(ts(rt[:], ra[:], math.pi / 2, -TWO_PI, ALU.is_gt, ALU.mult))
                L(stt(out=rc[:], in0=ra[:], scalar=math.pi / 2, in1=rt[:], op0=ALU.add, op1=ALU.add))
                L(ts(rc[:], rc[:], PI_SAFE, -PI_SAFE, ALU.min, ALU.max))
                v.sem_inc(angles, 1)
                v.wait_ge(tables, 1)
                v.wait_ge(mask_ready, 1)
                q_and_k(0)
                q_turned(0)

                def one(t, j, first, last):
                    b = lambda n: B[(j + n + 1) % 2]
                    n1 = t + 1
                    mask = mk_first if first else mk[j]
                    if not last:
                        norm(n1, 1 - j)
                    if not first:
                        output(t - 1, 1 - j, 0, b(0))
                    maxima(t, 0, mask)
                    if not last:
                        x_turned(n1)
                    if not first:
                        output(t - 1, 1 - j, 1, b(1))
                    maxima(t, 1, mask)
                    p_half(t, 0)
                    maxima(t, 2, mask)
                    products(t, 0)
                    p_half(t, 1)
                    maxima(t, 3, mask)
                    products(t, 1)
                    p_half(t, 2)
                    products(t, 2)
                    p_half(t, 3)
                    if not last:
                        q_and_k(n1)
                    products(t, 3)
                    if first:
                        v.wait_ge(wo_ready, KC)
                    v.wait_ge(att_turned, t * 2 + 4)
                    nc.vector.tensor_copy(aT[:, 4:8, :], halves[1]).then_inc(aT_ready, 1)
                    if not last:
                        q_turned(n1)

                steps(v, one, 4 + 14 + 12 + 11, step)
                for n in range(2):
                    output(LAST, LAST % 2, n, B[(TT % 2 + n + 1) % 2])

            @block.tensor
            def _(pe):
                mm = nc.tensor.matmul
                pe.sem_inc(xn_turned, 2)
                pe.sem_inc(qk_turned, 3)
                pe.sem_inc(pv_done, 4)
                pe.sem_inc(p_turned, 4)
                pe.sem_inc(att_turned, 2)

                def turn(dst, src, done):
                    for k in range(KC):
                        tr = nc.tensor.transpose(dst[k // 4][:, k % 4, :], src[:, k * P:(k + 1) * P], m.ident[:])
                        if k % 4 == 3:
                            tr.then_inc(done, 1)

                def chunk(bank, n, loaded=None):
                    for k in range(KC):
                        if loaded and k % (KC // 2) == 0:
                            pe.wait_ge(loaded[2 * k // KC], 16)
                        last = mm(bank[:], xT[:, k, :], win[:, n, k, :], start=(k == 0), stop=(k == KC - 1))
                    return last

                def turn_x(t):
                    pe.wait_ge(xn_ready, t + 1)
                    turn(halves, xn, xn_turned)

                def turn_qk(t):
                    pe.wait_ge(qk_ready, t + 2)
                    pe.wait_ge(s_read, t * 4 + 1)
                    for n in (8, 9, 0, 1, 2, 3, 4, 5, 6, 7):
                        dst = psc[:, 0, (n - 8) * P:(n - 7) * P] if n >= 8 else T[n // 4][:, n % 4, :]
                        tr = nc.tensor.transpose(dst, qr[:, 2 * n:2 * n + 2, :].rearrange("p h d -> p (h d)"), m.ident[:])
                        if n in (9, 3, 7):
                            tr.then_inc(qk_turned, 1)

                def outputs(t, n, bank):
                    pe.wait_ge(aT_ready, t * 2 + 2)
                    for k in range(KC):
                        last = mm(bank[:], aT[:, k, :], wout[:, k, n * 512:(n + 1) * 512], start=(k == 0), stop=(k == KC - 1))
                    last.then_inc(o_done, 1)

                def scores(t, g):
                    lo = AD * (g % 2)
                    pe.wait_ge(s_read, t * 4 + (g + 1))
                    if g == 0:
                        pe.wait_ge(qT_ready, t + 1)
                        pe.wait_ge(qT2_ready, t + 1)
                    for r in range(4):
                        last = mm(psc[:, r, :], qT[lo:lo + AD, 4 * (g // 2) + r, :],
                                  kT[lo:lo + AD, g // 2].rearrange("p a b -> p (a b)"), start=True, stop=True)
                    last.then_inc(s_done, 1)

                def turn_p(t, g):
                    pe.wait_ge(exp_ready, t * 4 + (g + 1))
                    for x in range(8):
                        tr = nc.tensor.transpose(T[x // 4][:, x % 4, :], sc[g % 2][:, x // 2, (x % 2) * P:(x % 2 + 1) * P], m.ident[:])
                        if x % 4 == 3:
                            tr.then_inc(p_turned, 1)

                def products(t, g):
                    pe.wait_ge(pT_ready, t * 4 + (g + 1))
                    pe.wait_ge(pT2_ready, t * 4 + (g + 1))
                    pe.wait_ge(pv_read, t * 4 + (g + 1))
                    if g == 0:
                        pe.wait_ge(v_ready, t + 1)
                    for r in range(4):
                        for s in range(2):
                            last = mm(pv[:, g % 2, r * AD:(r + 1) * AD], pT[g % 2][:, 2 * r + s, :], vv[:, s, g * AD:(g + 1) * AD],
                                      start=(s == 0), stop=(s == 1))
                    last.then_inc(pv_done, 1)

                turn_x(0)
                pe.wait_ge(pos_ready, 1)
                nc.tensor.transpose(T[0][:, 0, 0:TT], pos_f[:], m.ident[0:TT, 0:TT]).then_inc(pos_turned, 1)
                pe.wait_ge(xT_ready, 2)
                for n, done in enumerate((q_done, q_done, kv_done, z_done, z_done)):
                    if n:
                        pe.wait_ge(w_in[n], 16)
                    if n == 2:
                        pe.wait_ge(q_out, 1)
                    if n == 3:
                        pe.wait_ge(q_out, 2)
                    if n == 4:
                        pe.wait_ge(v_out, 1)
                    chunk(B[n % 2], n, None if n else w0_in).then_inc(done, 1)
                turn_qk(0)

                def one(t, j, first, last):
                    b = lambda n: B[(j + n + 1) % 2]
                    n1 = t + 1
                    if not first:
                        pe.wait_ge(z_out, t * 2 + 1)
                        outputs(t - 1, 0, b(0))
                    scores(t, 0)
                    if not last:
                        turn_x(n1)
                    if not first:
                        pe.wait_ge(z_out, t * 2 + 2)
                        outputs(t - 1, 1, b(1))
                    scores(t, 1)
                    turn_p(t, 0)
                    if not last:
                        pe.wait_ge(xT_ready, t * 2 + 4)
                        if first:
                            pe.wait_ge(z_out, 1)
                        else:
                            pe.wait_ge(o_added, t * 2 - 1)
                        chunk(b(2), 0).then_inc(q_done, 1)
                    products(t, 0)
                    scores(t, 2)
                    turn_p(t, 1)
                    if not last:
                        if first:
                            pe.wait_ge(z_out, 2)
                        else:
                            pe.wait_ge(o_added, t * 2)
                        chunk(b(3), 1).then_inc(q_done, 1)
                    products(t, 1)
                    scores(t, 3)
                    turn_p(t, 2)
                    if not last:
                        pe.wait_ge(q_out, t * 2 + 3)
                        chunk(b(4), 2).then_inc(kv_done, 1)
                    products(t, 2)
                    turn_p(t, 3)
                    if not last:
                        pe.wait_ge(q_out, t * 2 + 4)
                        chunk(b(5), 3).then_inc(z_done, 1)
                    products(t, 3)
                    if not last:
                        pe.wait_ge(v_out, t + 2)
                        chunk(b(6), 4).then_inc(z_done, 1)
                    pe.wait_ge(att_ready, t + 2)
                    turn(halves, att, att_turned)
                    if not last:
                        turn_qk(n1)

                steps(pe, one)
                pe.wait_ge(o_added, LAST * 2)
                for n in range(2):
                    outputs(LAST, n, B[(TT % 2 + n + 1) % 2])


_INS = ['x', 'c', 'positions', 'ada_w', 'ada_b', 'norm_g', 'ev_w_in', 's5_a_re', 's5_a_im', 's5_log_dt',
        's5_b_re', 's5_b_im', 's5_c_re', 's5_c_im', 's5_d', 's5_w_glu', 'm_conv_w', 'm_conv_b',
        'm_wq', 'm_wk', 'm_wv', 'm_wo', 'm_w_if', 'm_b_if', 'm_norm_g', 'm_skip', 'ev_w_out', 'od_w_in',
        'od_q_norm_g', 'od_k_norm_g', 'od_sinks', 'od_w_out']


def trunk(nc, a, out):
    with ExitStack() as ctx:
        m = names(nc, ctx)
        s5_tables(m, a)
        with ExitStack() as own:
            m.hT = own.enter_context(nc.sbuf_tensor("hT", [P, 2, KC, SEQ], F32R))
            norm_transposed(m, a)
            project(m, a)
        m.clear()
        glu(m, a)
        mlstm(m, a)
        attention(m, a, out)


def kernel(**inputs):
    import concourse.bacc as bacc
    from concourse.bass_utils import run_bass_kernel_spmd

    nc = bacc.Bacc("TRN2", target_bir_lowering=False, num_devices=1)
    arrays, a = {}, {}
    for name in _INS:
        arrays[f"in_{name}"] = np.ascontiguousarray(inputs[name])
        a[name] = nc.dram_tensor(f"in_{name}", arrays[f"in_{name}"].shape, mybir.dt.from_np(arrays[f"in_{name}"].dtype),
                                 kind="ExternalInput").ap()
    out = nc.dram_tensor("out", [1, SEQ, D], F32, kind="ExternalOutput").ap()
    trunk(nc, a, out)
    r = run_bass_kernel_spmd(nc, [arrays], core_ids=[0])
    return r.results[0]["out"]
```
